# Optimizing a Trainium2 kernel written in Bass

```python
import jax, jax.numpy as jnp
from jax import lax
import numpy as np

D_MODEL = 1024
BATCH = 1
SEQ = 1024
DEPTH = 1

CHUNK = 64
POOL_WINDOWS = (2, 4, 8, 16)
POOL_GROUP = 64
D_POOL = POOL_GROUP * len(POOL_WINDOWS)
N_HEADS = 8
HEAD_DIM = 64
D_ATTN = N_HEADS * HEAD_DIM
N_PREV_CHUNKS = 8
BAND = (N_PREV_CHUNKS + 1) * CHUNK
REL_CLIP = 128
N_REL = 2 * REL_CLIP + 1
D_CONV = 256
CONV_WIDTH = 31
D_FF = 4 * D_MODEL
N_BRANCH = 3
IN_SIZES = (D_POOL, D_ATTN, D_ATTN, D_ATTN, 2 * D_CONV, N_BRANCH * D_MODEL)
IN_SPLITS = tuple(int(v) for v in np.cumsum(IN_SIZES)[:-1])
D_IN = int(sum(IN_SIZES))
ALPHA = (2.0 * DEPTH) ** 0.25
BETA = (8.0 * DEPTH) ** -0.25
LN_EPS = 1e-5
NEG_INF = -1e30

kernel_name = "hybrid_chunk_causal_pool_attn_conv_block"

def layer_norm(x, g=None, b=None):
    xf = x.astype(jnp.float32)
    mu = jnp.mean(xf, axis=-1, keepdims=True)
    var = jnp.mean(jnp.square(xf - mu), axis=-1, keepdims=True)
    y = (xf - mu) * lax.rsqrt(var + LN_EPS)
    if g is not None:
        y = y * g.astype(jnp.float32) + b.astype(jnp.float32)
    return y.astype(x.dtype)

def pool_mixer(a, w_pool, pool_scale):
    B, S, _ = a.shape
    t = jnp.arange(S)
    outs = []
    for gi, w in enumerate(POOL_WINDOWS):
        xg = a[..., gi * POOL_GROUP:(gi + 1) * POOL_GROUP].astype(jnp.float32)
        cs = jnp.cumsum(xg, axis=1)
        cs_lag = jnp.pad(cs, ((0, 0), (w, 0), (0, 0)))[:, :S]
        count = jnp.minimum(t + 1, w).astype(jnp.float32)[None, :, None]
        outs.append((cs - cs_lag) / count - xg)
    p = jnp.stack(outs, axis=2).astype(a.dtype)
    p = jnp.einsum('bsgc,gcd->bsgd', p, w_pool).reshape(B, S, D_POOL)
    return p * pool_scale

def chunk_attention(q, k, v, rel_bias):
    B, S, _ = q.shape
    nc = S // CHUNK
    q = q.reshape(B, nc, CHUNK, N_HEADS, HEAD_DIM) * (HEAD_DIM ** -0.5)
    pad = ((0, 0), (N_PREV_CHUNKS * CHUNK, 0), (0, 0))
    kc = jnp.pad(k, pad).reshape(B, nc + N_PREV_CHUNKS, CHUNK, N_HEADS, HEAD_DIM)
    vc = jnp.pad(v, pad).reshape(B, nc + N_PREV_CHUNKS, CHUNK, N_HEADS, HEAD_DIM)
    band_idx = jnp.arange(nc)[:, None] + jnp.arange(N_PREV_CHUNKS + 1)[None, :]
    kb = kc[:, band_idx].reshape(B, nc, BAND, N_HEADS, HEAD_DIM)
    vb = vc[:, band_idx].reshape(B, nc, BAND, N_HEADS, HEAD_DIM)
    s = jnp.einsum('bnqhd,bnkhd->bnhqk', q, kb).astype(jnp.float32)
    qi = jnp.arange(CHUNK)[:, None]
    kj = jnp.arange(BAND)[None, :]
    rel = jnp.clip(N_PREV_CHUNKS * CHUNK + qi - kj, -REL_CLIP, REL_CLIP) + REL_CLIP
    bias = rel_bias[:, rel].astype(jnp.float32)
    key_pos = jnp.arange(nc)[:, None] * CHUNK + kj - N_PREV_CHUNKS * CHUNK
    valid = (key_pos >= 0)[None, :, None, None, :]
    s = jnp.where(valid, s + bias[None, None], NEG_INF)
    p = jax.nn.softmax(s, axis=-1).astype(vb.dtype)
    o = jnp.einsum('bnhqk,bnkhd->bnqhd', p, vb)
    return o.reshape(B, S, D_ATTN)

def conv_module(cin, conv_w, conv_b, ln_g, ln_b):
    h = cin[..., :D_CONV] * jax.nn.sigmoid(cin[..., D_CONV:])
    h = jnp.pad(h, ((0, 0), (CONV_WIDTH - 1, 0), (0, 0)))
    h = lax.conv_general_dilated(h, conv_w[:, None, :].astype(h.dtype), window_strides=(1,),
                                 padding='VALID', dimension_numbers=('NWC', 'WIO', 'NWC'),
                                 feature_group_count=D_CONV) + conv_b
    return jax.nn.silu(layer_norm(h, ln_g, ln_b))

def setup_inputs(seed: int = 0) -> dict:
    key = jax.random.key(seed)
    ks = jax.random.split(key, 26)
    L, D = DEPTH, D_MODEL

    def nrm(k, shape, scale):
        return jax.random.normal(k, shape, jnp.float32) * scale

    return {
        'x': nrm(ks[0], (BATCH, SEQ, D), 1.0),
        'c': nrm(ks[1], (BATCH, D), 1.0),
        'w_ada': nrm(ks[2], (L, D, 6 * D), 0.5 * D ** -0.5),
        'b_ada': nrm(ks[3], (L, 6 * D), 0.02),
        'w_in': nrm(ks[4], (L, D, D_IN), D ** -0.5),
        'b_gate': nrm(ks[5], (L, N_BRANCH * D), 0.1),
        'w_pool': nrm(ks[6], (L, len(POOL_WINDOWS), POOL_GROUP, POOL_GROUP), POOL_GROUP ** -0.5),
        'pool_scale': 1.0 + nrm(ks[7], (L, D_POOL), 0.1),
        'rel_bias': nrm(ks[8], (L, N_HEADS, N_REL), 0.1),
        'conv_w': nrm(ks[9], (L, CONV_WIDTH, D_CONV), CONV_WIDTH ** -0.5),
        'conv_b': nrm(ks[10], (L, D_CONV), 0.02),
        'conv_ln_g': 1.0 + nrm(ks[11], (L, D_CONV), 0.05),
        'conv_ln_b': nrm(ks[12], (L, D_CONV), 0.02),
        'w_br_pool': nrm(ks[13], (L, D_POOL, D), BETA * D_POOL ** -0.5),
        'w_br_attn': nrm(ks[14], (L, D_ATTN, D), BETA * D_ATTN ** -0.5),
        'w_br_conv': nrm(ks[15], (L, D_CONV, D), BETA * D_CONV ** -0.5),
        'w_o': nrm(ks[16], (L, D, D), BETA * D ** -0.5),
        'ln_mix_g': 1.0 + nrm(ks[17], (L, D), 0.05),
        'ln_mix_b': nrm(ks[18], (L, D), 0.02),
        'w_ff1': nrm(ks[19], (L, D, D_FF), D ** -0.5),
        'b_ff1': nrm(ks[20], (L, D_FF), 0.02),
        'w_ff2': nrm(ks[21], (L, D_FF, D), BETA * D_FF ** -0.5),
        'b_ff2': nrm(ks[22], (L, D), 0.02),
        'ln_ff_g': 1.0 + nrm(ks[23], (L, D), 0.05),
        'ln_ff_b': nrm(ks[24], (L, D), 0.02),
    }

def reference(x, c, w_ada, b_ada, w_in, b_gate, w_pool, pool_scale, rel_bias, conv_w, conv_b,
              conv_ln_g, conv_ln_b, w_br_pool, w_br_attn, w_br_conv, w_o, ln_mix_g, ln_mix_b,
              w_ff1, b_ff1, w_ff2, b_ff2, ln_ff_g, ln_ff_b):
    B, S, _ = x.shape
    c_act = jax.nn.silu(c)
    for l in range(DEPTH):
        mod = (c_act @ w_ada[l] + b_ada[l])[:, None, :]
        sh_m, sc_m, g_m, sh_f, sc_f, g_f = jnp.split(mod, 6, axis=-1)

        u = layer_norm(x) * (1 + sc_m) + sh_m
        z = u @ w_in[l]
        z_pool, z_q, z_k, z_v, z_conv, z_gate = jnp.split(z, IN_SPLITS, axis=-1)
        y_pool = pool_mixer(z_pool, w_pool[l], pool_scale[l]) @ w_br_pool[l]
        y_attn = chunk_attention(z_q, z_k, z_v, rel_bias[l]) @ w_br_attn[l]
        y_conv = conv_module(z_conv, conv_w[l], conv_b[l], conv_ln_g[l], conv_ln_b[l]) @ w_br_conv[l]
        gates = jax.nn.sigmoid(z_gate + b_gate[l]).reshape(B, S, N_BRANCH, D_MODEL)
        merged = gates[:, :, 0] * y_pool + gates[:, :, 1] * y_attn + gates[:, :, 2] * y_conv
        mix_out = merged @ w_o[l]
        x = layer_norm(ALPHA * x + g_m * mix_out, ln_mix_g[l], ln_mix_b[l])

        u = layer_norm(x) * (1 + sc_f) + sh_f
        h = jnp.square(jax.nn.relu(u @ w_ff1[l] + b_ff1[l]))
        ff_out = h @ w_ff2[l] + b_ff2[l]
        x = layer_norm(ALPHA * x + g_f * ff_out, ln_ff_g[l], ln_ff_b[l])
    return x


_drawn_inputs = setup_inputs


def setup_inputs(seed=0):
    import zlib

    import numpy as np

    out = dict(_drawn_inputs(seed))
    spreads = {}
    factors = {'b_ada': 3.627,
     'b_gate': 8.0,
     'pool_scale': 8.0,
     'rel_bias': 31.624,
     'conv_b': 8.0,
     'conv_ln_g': 34.385,
     'conv_ln_b': 64.0,
     'w_br_attn': 3.407,
     'ln_mix_b': 2.924,
     'b_ff1': 8.0,
     'b_ff2': 8.0,
     'ln_ff_b': 2.849}
    for name, (base, spread) in spreads.items():
        noise = np.random.default_rng([zlib.crc32(name.encode()), seed]).standard_normal(out[name].shape)
        drawn = base * np.exp(spread * noise) if base else spread * noise
        out[name] = __import__('jax').numpy.asarray(drawn.astype(out[name].dtype))
    for name, factor in factors.items():
        out[name] = (out[name] * factor).astype(out[name].dtype)
    return out
```

```python
import concourse.bass as bass
from concourse import mybir
from contextlib import ExitStack

SEQ = 1024
D = 1024
P = 128
KT = D // P
ST = SEQ // P
HALF = 512
D_POOL, D_ATTN, D_CONV = 256, 512, 256
CHUNK, N_PREV = 64, 8
HEADS, HEAD_DIM = 8, 64
PAIRS = HEADS // 2
TAPS = 31
REL_CLIP = 128
N_REL = 2 * REL_CLIP + 1
D_FF = 4 * D
BAND_BLOCKS = N_PREV * CHUNK // P + 1
BAND = BAND_BLOCKS * P
ALPHA = 2.0 ** 0.25
EPS = 1e-5
MASKED = -1e30
C_POOL, C_Q = 0, D_POOL
C_K, C_V = C_Q + D_ATTN, C_Q + 2 * D_ATTN
C_CONV = C_Q + 3 * D_ATTN
C_GATE = C_CONV + 2 * D_CONV
R_ADA, R_GATE, R_FF1 = 0, 48, 72
R_CONVB, R_CLNG, R_CLNB, R_PSC = 104, 106, 108, 110
ROWS_A, ROWS_C = 112, 2 * TAPS
N_P1 = 6
N_GATE0 = N_P1 + 3 * PAIRS
N_FF0 = N_GATE0 + 4 * KT
GROUP = 4
GROUPS = D_FF // (P * GROUP)
STEPS = 2 * ST
PROJ = 3 * 2 * KT * 3
PER_STEP = PROJ // STEPS


def trunk_layer(nc, x, c, w_ada, b_ada, w_in, b_gate, w_pool, pool_scale, rel_bias, conv_w, conv_b,
                conv_ln_g, conv_ln_b, w_br_pool, w_br_attn, w_br_conv, w_o, ln_mix_g, ln_mix_b,
                w_ff1, b_ff1, w_ff2, b_ff2, ln_ff_g, ln_ff_b, out):
    f32, f32r = mybir.dt.float32, mybir.dt.float32r
    ALU, ACT = mybir.AluOpType, mybir.ActivationFunctionType

    KB = 1024
    base = (nc.sbuf_base + 63) // 64 * 64
    top = nc.sbuf_usable_end

    def at(name, shape, dt, offset):
        size = 4
        for n in shape[1:]:
            size *= n
        assert base + offset + size <= top, (name, base + offset + size - top)
        return nc.alloc_sbuf_tensor_at(name, shape, dt, offset=base + offset)

    act_hi = at("act_hi", [P, KT, SEQ], f32r, 0)
    act_lo = at("act_lo", [P, KT, SEQ], f32r, 32 * KB)
    mid = at("mid", [P, KT, SEQ], f32, 64 * KB)
    w_raw = [at(f"w_raw{i}", [P, KT, P], f32, (96 + 4 * i) * KB) for i in range(2)]
    w_hi = [at(f"w_hi{i}", [P, KT, P], f32r, (104 + 4 * i) * KB) for i in range(2)]
    w_lo = [at(f"w_lo{i}", [P, KT, P], f32r, (112 + 4 * i) * KB) for i in range(2)]
    X = 120 * KB
    ada = [at(f"ada{i}", [P, 8, HALF], f32, X + 16 * i * KB) for i in range(3)]
    partial = [at(f"partial{i}", [P, HALF], f32, X + (48 + 2 * i) * KB) for i in range(2)]
    glu_gate = at("glu_gate", [P, SEQ], f32, X + 52 * KB)
    u_tmp = [at(f"u_tmp{i}", [P, SEQ], f32, X + (56 - 4 * i) * KB) for i in range(2)]
    rel_ext = at("rel_ext", [HEADS, 768], f32, X + 60 * KB)
    rows_a = at("rows_a", [ROWS_A, P], f32, X + 63 * KB)
    rows_c = at("rows_c", [ROWS_C, P], f32, X + 63 * KB + 512)
    q_hi = [at(f"q_hi{i}", [P, SEQ], f32r, X + 16 * i * KB) for i in range(2)]
    q_lo = [at(f"q_lo{i}", [P, SEQ], f32r, X + (16 * i + 4) * KB) for i in range(2)]
    k_hi = [at(f"k_hi{i}", [P, SEQ], f32r, X + (16 * i + 8) * KB) for i in range(2)]
    k_lo = [at(f"k_lo{i}", [P, SEQ], f32r, X + (16 * i + 12) * KB) for i in range(2)]
    v_hi = [at(f"v_hi{i}", [P, ST, P], f32r, X + (32 + 8 * i) * KB) for i in range(2)]
    v_lo = [at(f"v_lo{i}", [P, ST, P], f32r, X + (36 + 8 * i) * KB) for i in range(2)]
    bias_rev = [at(f"bias_rev{i}", [P, 2, BAND], f32, X + (48 + 5 * i) * KB) for i in range(2)]
    probs = [at(f"probs{i}", [P, BAND], f32, X + 58 * KB + 2560 * i) for i in range(2)]
    pt_hi = at("pt_hi", [P, BAND_BLOCKS, 2, P], f32r, X + 63 * KB)
    pt_lo = at("pt_lo", [P, BAND_BLOCKS, 2, P], f32r, X + 68 * KB)
    PAD = TAPS - 1
    h_pad = at("h_pad", [P, 2, PAD + SEQ], f32, X + 74 * KB)
    z_pool = at("z_pool", [P, 2, SEQ], f32, X + 82 * KB + 512)
    w_pool_bd = at("w_pool_bd", [P, 2, P], f32, X + 90 * KB + 512)
    sq = at("sq", [P, 2, SEQ], f32, X + 64 * KB)
    conv_sig = at("conv_sig", [P, SEQ], f32, X + 72 * KB)
    conv_rstd = at("conv_rstd", [P, SEQ], f32, X + 76 * KB)
    br_hi = at("br_hi", [P, KT, SEQ], f32r, X)
    br_lo = at("br_lo", [P, KT, SEQ], f32r, X + 32 * KB)
    gate = [at(f"gate{i}", [P, SEQ], f32, X + (72 + 4 * i) * KB) for i in range(3)]
    row_raw = [at(f"row_raw{i}", [P, D], f32, X + (64 + 4 * i) * KB) for i in range(2)]
    ln_g = at("ln_g", [P, D], f32, X + 72 * KB)
    ln_b = at("ln_b", [P, D], f32, X + 76 * KB)
    ff2_bias = at("ff2_bias", [P, D], f32, X + 80 * KB)
    tmp = [at(f"tmp{i}", [P, D], f32, X + (84 + 4 * i) * KB) for i in range(2)]
    mix_tmp = at("mix_tmp", [P, D], f32, 100 * KB)
    gate_mix = at("gate_mix", [P, D], f32, X + 92 * KB)
    gate_ff = at("gate_ff", [P, D], f32, X + 96 * KB)
    h_hi = at("h_hi", [P, GROUP, SEQ], f32r, X)
    h_lo = at("h_lo", [P, GROUP, SEQ], f32r, X + 16 * KB)
    w2_hi = at("w2_hi", [P, GROUP, D], f32r, X + 32 * KB)
    w2_lo = at("w2_lo", [P, GROUP, D], f32r, X + 48 * KB)
    small = X + 100 * KB

    def little(name, shape):
        nonlocal small
        t = at(name, shape, f32, small)
        n = 4
        for m in shape[1:]:
            n *= m
        small += (n + 31) // 32 * 32
        return t

    ident = little("ident", [P, P])
    cols = little("cols", [P, ROWS_A + ROWS_C])
    mod = little("mod", [P, 48])
    ones_row = at("ones_row", [P, P], f32, X + 91 * KB + 512)
    inv_count = little("inv_count", [P, 2, 16])
    c_raw = little("c_raw", [P, 8])
    c_sig = little("c_sig", [P, 8])
    c_act = little("c_act", [P, 8])
    neg_max = little("neg_max", [P, 2 * STEPS])
    row_sum = little("row_sum", [P, 2 * STEPS])
    inv_sum = little("inv_sum", [P, 2 * STEPS])
    bn = little("bn", [P, 12])
    mean_var = little("mean_var", [P, ST, 2])
    rstd = little("rstd", [P, ST])
    neg_mean = little("neg_mean", [P, ST])

    rel_dram = nc.dram_tensor("rel_scratch", (HEADS, 768), f32, kind="Internal").ap()

    x_rows = x[0].rearrange("(t p) d -> t p d", p=P)
    out_rows = out[0].rearrange("(t p) d -> t p d", p=P)
    ada_view = w_ada[0].rearrange("(p k) n -> p k n", k=8)
    win_view = w_in[0].rearrange("(k p) n -> p k n", p=P)
    wff1_view = w_ff1[0].rearrange("(k p) n -> p k n", p=P)
    brp_view = w_br_pool[0].rearrange("(k p) n -> p k n", p=P)
    bra_view = w_br_attn[0].rearrange("(k p) n -> p k n", p=P)
    brc_view = w_br_conv[0].rearrange("(k p) n -> p k n", p=P)

    def win_col(n):
        if n < 4:
            return C_CONV + ((n + 1) % 2) * D_CONV + (n // 2) * P
        if n < N_P1:
            return C_POOL + (n - 4) * P
        pair, part = divmod(n - N_P1, 3)
        return (C_Q, C_K, C_V)[part] + pair * P

    with ExitStack() as ctx:
        ps = ctx.enter_context(nc.psum_tensor("ps", [P, 8, HALF], f32))

        def sem(name):
            return ctx.enter_context(nc.semaphore(name))

        def banks(b, n=2):
            return ps[:, b:b + n, :].rearrange("p b n -> p (b n)")

        def f(ap):
            return ap.bitcast(f32)

        c_in, small_in = sem("c_in"), sem("small_in")
        x_in = [sem(f"x_in{i}") for i in range(ST)]
        ada_in = [sem(f"ada_in{i}") for i in range(3)]
        w_arrived = [sem(f"w_arrived{i}") for i in range(2)]
        pool_w_in, rel_in, rel_stored = sem("pool_w_in"), sem("rel_in"), sem("rel_stored")
        bias_in = [sem(f"bias_in{i}") for i in range(2)]
        row_in = [sem(f"row_in{i}") for i in range(2)]
        res_in = [sem(f"res_in{i}") for i in range(ST)]
        ada_bias_in, ln_in, ln2_in, ff2b_in = sem("ada_bias_in"), sem("ln_in"), sem("ln2_in"), sem("ff2b_in")
        stored = [sem(f"stored{i}") for i in range(2)]
        consts_done, bd_zeroed = sem("consts_done"), sem("bd_zeroed")
        pool_step, dve_step = sem("pool_step"), sem("dve_step")
        c_sig_done, c_act_done, cols_t, cols_done, rel_done = (
            sem("c_sig_done"), sem("c_act_done"), sem("cols_t"), sem("cols_done"), sem("rel_done"))
        partial_done, reduced, mod_done, gates_done = (
            sem("partial_done"), sem("reduced"), sem("mod_done"), sem("gates_done"))
        var_done, std_done, norm_ready, normed = sem("var_done"), sem("std_done"), sem("norm_ready"), sem("normed")
        w_hi_done, w_lo_done = sem("w_hi_done"), sem("w_lo_done")
        row_hi_done, row_lo_done, row_scaled = sem("row_hi_done"), sem("row_lo_done"), sem("row_scaled")
        z_done, u_tmp_done, u_lo_done = sem("z_done"), sem("u_tmp_done"), sem("u_lo_done")
        glu_sig_done, glu_done, zp_done, pooled_done = (
            sem("glu_sig_done"), sem("glu_done"), sem("zp_done"), sem("pooled_done"))
        h_done, half_hi, h_free = sem("h_done"), sem("half_hi"), [sem(f"h_free{i}") for i in range(2)]
        scores_done, biased, exp_done, probs_done = (
            sem("scores_done"), sem("biased"), sem("exp_done"), sem("probs_done"))
        pt_done, pt_hi_done, pt_lo_done = sem("pt_done"), sem("pt_hi_done"), sem("pt_lo_done")
        pv_done, o_copied, bias_ready = sem("pv_done"), sem("o_copied"), sem("bias_ready")
        pm_done, pm_scaled, tap_done = sem("pm_done"), sem("pm_scaled"), sem("tap_done")
        cmean_done, centred, squared, cvar_done, cvar_read = (
            sem("cmean_done"), sem("centred"), sem("squared"), sem("cvar_done"), sem("cvar_read"))
        cstd_done, cnormed, conv_sig_done, conv_done = (
            sem("cstd_done"), sem("cnormed"), sem("conv_sig_done"), sem("conv_done"))
        br_hi_done, br_lo_done = sem("br_hi_done"), sem("br_lo_done")
        g_done, sig_done, y_done, y_used, merged_step = (
            sem("g_done"), sem("sig_done"), sem("y_done"), sem("y_used"), sem("merged_step"))
        mg_hi_done, mg_lo_done = sem("mg_hi_done"), sem("mg_lo_done")
        mix_done, mix_free, res_done, x1_done = sem("mix_done"), sem("mix_free"), sem("res_done"), sem("x1_done")
        x2t_done, x2_tmp_done, x2_hi_done, x2_lo_done = (
            sem("x2t_done"), sem("x2_tmp_done"), sem("x2_hi_done"), sem("x2_lo_done"))
        ff2b_scaled, x1_scaled = sem("ff2b_scaled"), sem("x1_scaled")
        f1_done, relu_done, sq_done, h_hi_done, h_lo_done = (
            sem("f1_done"), sem("relu_done"), sem("sq_done"), sem("h_hi_done"), sem("h_lo_done"))
        f2_done, acc_done, y_ready = sem("f2_done"), sem("acc_done"), sem("y_ready")

        block = ctx.enter_context(nc.Block())

        def block_used(n):
            if n < N_P1:
                return z_done, 8 + n + 1
            pair, part = divmod(n - N_P1, 3)
            return h_done, 8 * pair + 2 * part + 2

        W0_GATES = 16 * N_GATE0 // 2
        W0_FF = [W0_GATES + 32 * KT, W0_GATES + 64 * KT]

        def blocks_of(t):
            return min(t + 1, BAND_BLOCKS)

        def score_cols(nb):
            if nb < BAND_BLOCKS:
                return banks(4)[:, 0:nb * P]
            return ps[:, 4:6, 0:BAND // 2]

        def like_scores(ap, nb):
            return ap if nb < BAND_BLOCKS else ap.rearrange("p (b n) -> p b n", b=2)

        @block.sync
        def _(sp):
            def load_block(n):
                if n >= 2:
                    sp.wait_ge(w_lo_done, n - 1)
                c0 = win_col(n)
                sp.dma_start(w_raw[n % 2][:, :, :], win_view[:, :, c0:c0 + P]).then_inc(w_arrived[n % 2], 16)

            def load_ada(i):
                if i >= 3:
                    sp.wait_ge(partial_done, i - 2)
                sp.dma_start(ada[i % 3][:, :, :], ada_view[:, :, i * HALF:(i + 1) * HALF]).then_inc(ada_in[i % 3], 16)

            sp.dma_start(c_raw[:, :], c[0].rearrange("(p k) -> p k", k=8)).then_inc(c_in, 16)
            for i in range(ST):
                sp.dma_start(mid[:, i, :], x_rows[i]).then_inc(x_in[i], 16)
            for i in range(3):
                load_ada(i)
            for row, n, src in ((R_ADA, 48, b_ada), (R_GATE, 24, b_gate), (R_FF1, 32, b_ff1), (R_CONVB, 2, conv_b),
                                (R_CLNG, 2, conv_ln_g), (R_CLNB, 2, conv_ln_b), (R_PSC, 2, pool_scale)):
                sp.dma_start(rows_a[row:row + n, :], src[0].rearrange("(r p) -> r p", p=P)).then_inc(small_in, 16)
            sp.dma_start(rows_c[:, :], conv_w[0].rearrange("t (c p) -> (t c) p", p=P)).then_inc(small_in, 16)
            load_ada(3)
            load_block(0)
            load_block(1)
            sp.dma_start(rel_ext[:, 0:2 * REL_CLIP], rel_bias[0][:, 1:N_REL]).then_inc(rel_in, 16)
            sp.wait_ge(bd_zeroed, 1)
            for g in range(4):
                lo = 64 * (g % 2)
                sp.dma_start(w_pool_bd[lo:lo + 64, g // 2, lo:lo + 64], w_pool[0, g]).then_inc(pool_w_in, 16)
            for t, col in ((gate_mix, 2 * D), (gate_ff, 5 * D)):
                sp.dma_start(t[:, :], b_ada[0:1, col:col + D].partition_broadcast(P)).then_inc(ada_bias_in, 16)
            sp.wait_ge(rel_done, 1)
            sp.dma_start(rel_dram, rel_ext[:, :]).then_inc(rel_stored, 16)
            load_ada(4)
            load_ada(5)
            load_block(2)
            load_ada(6)
            load_ada(7)
            load_block(3)
            load_ada(8)
            load_ada(9)
            load_block(4)
            load_ada(10)
            load_block(5)
            load_ada(11)

            def load_bias(pair):
                if pair >= 2:
                    sp.wait_ge(biased, STEPS * (pair - 1))
                for h in range(2):
                    head = 2 * pair + h
                    src = bass.AP(rel_dram.tensor, head * 768, [[1, P], [1, BAND]])
                    sp.dma_start(bias_rev[pair % 2][:, h, :], src).then_inc(bias_in[pair % 2], 16)

            load_block(6)
            sp.wait_ge(reduced, 12)
            sp.wait_ge(glu_done, 2)
            sp.wait_ge(u_lo_done, KT)
            sp.wait_ge(rel_stored, 16)
            load_bias(0)
            load_bias(1)
            for n in range(7, N_GATE0):
                if n == N_P1 + 10:
                    load_bias(2)
                load_block(n)
            load_bias(3)

            with sp.Fori(1, KT + 1) as j_next:
                j = j_next - 1
                first = [sp.snap(j * P + (C_GATE + b * D)) for b in range(3)]
                cut = [sp.snap(j * 4 + (N_GATE0 + b - 1)) for b in range(4)]
                for b in range(4):
                    sp.wait_ge(w_lo_done, cut[b])
                    slot = (N_GATE0 + b) % 2
                    if b < 3:
                        sp.dma_start(w_raw[slot][:, :, :], win_view[:, :, bass.ds(first[b], P)])\
                            .then_inc(w_arrived[slot], 16)
                    else:
                        for k0, k1, view in ((0, 2, brp_view), (2, 6, bra_view), (6, 8, brc_view)):
                            sp.dma_start(w_raw[slot][:, k0:k1, :], view[:, :, bass.ds(j_next * P - P, P)])\
                                .then_inc(w_arrived[slot], 16)

            def load_row(q, src):
                sp.dma_start(row_raw[q % 2][:, :], src).then_inc(row_in[q % 2], 16)

            sp.wait_ge(conv_done, 2)
            for q in range(2):
                load_row(q, w_o[0, q * P:(q + 1) * P, :])
            for n in range(2):
                sp.wait_ge(w_lo_done, N_FF0 + n - 1)
                sp.dma_start(w_raw[n][:, :, :], wff1_view[:, :, n * P:(n + 1) * P]).then_inc(w_arrived[n], 16)
            sp.wait_ge(y_used, 3 * KT)
            for q in range(2, KT):
                sp.wait_ge(row_lo_done, q - 1)
                load_row(q, w_o[0, q * P:(q + 1) * P, :])
                if q == 2:
                    sp.dma_start(ln_g[:, :], ln_mix_g[0:1, :].partition_broadcast(P)).then_inc(ln_in, 16)
                    sp.dma_start(ln_b[:, :], ln_mix_b[0:1, :].partition_broadcast(P)).then_inc(ln_in, 16)
                    sp.dma_start(ff2_bias[:, :], b_ff2[0:1, :].partition_broadcast(P)).then_inc(ff2b_in, 16)
                if q >= 4:
                    sp.wait_ge(mg_lo_done, q - 3)
                    sp.dma_start(mid[:, q - 4, :], x_rows[q - 4]).then_inc(res_in[q - 4], 16)
            for i in range(4, ST):
                sp.wait_ge(mg_lo_done, i + 1)
                sp.dma_start(mid[:, i, :], x_rows[i]).then_inc(res_in[i], 16)

            def ff_loads(g, last):
                first = [g * (GROUP * P) + t * P for t in range(GROUP + 2)]
                rows_cut = [g * GROUP + (KT + t - 1) for t in range(GROUP)]
                block_cut = [g * GROUP + (N_FF0 + t + 1) for t in range(GROUP)]
                if not last:
                    first, rows_cut, block_cut = ([sp.snap(v) for v in vs] for vs in (first, rows_cut, block_cut))
                for t in range(GROUP):
                    sp.wait_ge(row_lo_done, rows_cut[t])
                    sp.dma_start(row_raw[t % 2][:, :], w_ff2[0, bass.ds(first[t], P), :]).then_inc(row_in[t % 2], 16)
                    if not (last and t >= 2):
                        sp.wait_ge(w_lo_done, block_cut[t])
                        sp.dma_start(w_raw[t % 2][:, :, :], wff1_view[:, :, bass.ds(first[t + 2], P)])\
                            .then_inc(w_arrived[t % 2], 16)

            sp.wait_ge(x1_done, ST)
            with sp.Fori(0, GROUPS - 1) as g:
                ff_loads(g, False)
            ff_loads(GROUPS - 1, True)
            sp.dma_start(ln_g[:, :], ln_ff_g[0:1, :].partition_broadcast(P)).then_inc(ln2_in, 16)
            sp.dma_start(ln_b[:, :], ln_ff_b[0:1, :].partition_broadcast(P)).then_inc(ln2_in, 16)
            for t in range(ST):
                sp.wait_ge(y_ready, t + 1)
                sp.dma_start(out_rows[t], tmp[t % 2][:, :]).then_inc(stored[t % 2], 16)
            for b in range(2):
                sp.wait_ge(stored[b], 16 * ST // 2)

        def arrived(n):
            if n < N_GATE0:
                return 16 * (n // 2 + 1)
            j, b = divmod(n - N_GATE0, 4)
            return gate_arrived(j, b)

        def gate_arrived(j, b):
            return (j * 32 + (W0_GATES + (16, 16, 32, 64)[b])) if b % 2 == 0 else (j * 64 + (W0_GATES + (16, 16, 32, 64)[b]))

        def ff_arrived(g, t):
            return g * (16 * GROUP // 2) + (W0_FF[t % 2] + 16 * (t // 2 + 1))

        @block.gpsimd
        def _(pool):
            steps = [0]

            def link(ins):
                steps[0] += 1
                ins.then_inc(pool_step, 1)
                pool.wait_ge(pool_step, steps[0])

            link(nc.gpsimd.memset(ident[:, :], 0.0))
            nc.gpsimd.affine_select(out=ident[:, :], in_=ident[:, :], compare_op=ALU.not_equal, fill=1.0, base=0,
                                    pattern=[[-1, P]], channel_multiplier=1).then_inc(consts_done, 1)
            pool.wait_ge(consts_done, 1)
            nc.gpsimd.memset(ones_row[:, :], 1.0).then_inc(consts_done, 1)
            pool.wait_ge(consts_done, 2)
            nc.gpsimd.memset(w_pool_bd[:, :, :], 0.0).then_inc(bd_zeroed, 1)
            pool.wait_ge(bd_zeroed, 1)
            nc.gpsimd.memset(h_pad[:, :, 0:PAD], 0.0).then_inc(consts_done, 1)
            pool.wait_ge(consts_done, 3)
            for g, window in enumerate((2, 4, 8, 16)):
                rows = slice(64 * (g % 2), 64 * (g % 2) + 64)
                for t in range(window - 1):
                    link(nc.gpsimd.memset(inv_count[rows, g // 2, t:t + 1], 1.0 / (t + 1)))
                link(nc.gpsimd.memset(inv_count[rows, g // 2, window - 1:16], 1.0 / window))

            def shifted_sum(dst, src, shift, rows=slice(0, P)):
                link(nc.gpsimd.tensor_copy(dst[rows, 0:shift], src[rows, 0:shift]))
                link(nc.gpsimd.tensor_tensor(dst[rows, shift:SEQ], src[rows, shift:SEQ], src[rows, 0:SEQ - shift],
                                             ALU.add))

            def window_mean(c, half, total):
                rows = slice(64 * half, 64 * half + 64)
                first = total[rows, 0:16]
                link(nc.gpsimd.tensor_tensor(first, first, inv_count[rows, c, :], ALU.mult))
                link(nc.gpsimd.tensor_scalar(total[rows, 16:SEQ], total[rows, 16:SEQ], inv_count[rows, c, 15:16], None,
                                             ALU.mult))
                z = z_pool[rows, c, :]
                ins = nc.gpsimd.tensor_tensor(z, total[rows, :], z, ALU.subtract)
                if half == 1:
                    ins.then_inc(pooled_done, 1)
                    pool.wait_ge(pooled_done, c + 1)
                else:
                    link(ins)

            def mask_bias(pair):
                pool.wait_ge(bias_in[pair % 2], 32 * (pair // 2 + 1))
                link(nc.gpsimd.memset(bias_rev[pair % 2][0:64, :, 0:CHUNK], MASKED))
                nc.gpsimd.memset(bias_rev[pair % 2][64:P, :, BAND - CHUNK:BAND], MASKED).then_inc(bias_ready, 1)
                pool.wait_ge(bias_ready, pair + 1)

            pool.wait_ge(z_done, KT)
            a, b = mid[:, 3, :], mid[:, 4, :]
            pool.wait_ge(zp_done, 1)
            z = z_pool[:, 0, :]
            shifted_sum(a, z, 1)
            shifted_sum(b, a, 2, slice(64, P))
            window_mean(0, 0, a)
            window_mean(0, 1, b)
            mask_bias(0)
            pool.wait_ge(zp_done, 2)
            z = z_pool[:, 1, :]
            shifted_sum(a, z, 1)
            shifted_sum(b, a, 2)
            shifted_sum(a, b, 4)
            shifted_sum(b, a, 8, slice(64, P))
            window_mean(1, 0, a)
            window_mean(1, 1, b)
            for pair in range(1, PAIRS):
                mask_bias(pair)
            pool.wait_ge(gates_done, 4)
            pool.wait_ge(ff2b_in, 16)
            nc.gpsimd.tensor_tensor(ff2_bias[:, :], ff2_bias[:, :], gate_ff[:, :], ALU.mult).then_inc(ff2b_scaled, 1)
            pool.wait_ge(ff2b_scaled, 1)
            for t in range(ST):
                pool.wait_ge(x1_scaled, t + 1)
                nc.gpsimd.tensor_tensor(mid[:, t, :], mid[:, t, :], ff2_bias[:, :], ALU.add).then_inc(res_done, 1)

        half_after = {}
        for r in range(6):
            half_after[-(-24 * (r + 1) // PER_STEP) - 1] = r

        @block.scalar
        def _(act):
            def copy(out, in_, **kw):
                return nc.scalar.activation(out, in_, ACT.Copy, **kw)

            def cut_hi(n):
                act.wait_ge(w_arrived[n % 2], arrived(n))
                if n >= 2:
                    act.wait_ge(*block_used(n - 2))
                copy(w_hi[n % 2][:, :, :], w_raw[n % 2][:, :, :]).then_inc(w_hi_done, 1)

            act.wait_ge(c_in, 16)
            nc.scalar.activation(c_sig[:, :], c_raw[:, :], ACT.Sigmoid).then_inc(c_sig_done, 1)
            for i in range(ST):
                act.wait_ge(var_done, i + 1)
                nc.scalar.activation(rstd[:, i:i + 1], rstd[:, i:i + 1], ACT.Sqrt).then_inc(std_done, 1)
            for i in range(ST):
                act.wait_ge(norm_ready, i + 1)
                nc.scalar.activation(mid[:, i, :], mid[:, i, :], ACT.Identity, bias=neg_mean[:, i:i + 1],
                                     scale=rstd[:, i:i + 1]).then_inc(normed, 1)
            cut_hi(0)
            cut_hi(1)
            for k in range(KT):
                if k == 0:
                    act.wait_ge(mod_done, 1)
                if k >= 2:
                    act.wait_ge(u_lo_done, k - 1)
                act.wait_ge(z_done, k + 1)
                nc.scalar.activation(u_tmp[k % 2][:, :], banks(2 * (k % 2)), ACT.Identity, bias=mod[:, k:k + 1],
                                     scale=mod[:, KT + k:KT + k + 1]).then_inc(u_tmp_done, 1)
            for n in range(N_P1):
                act.wait_ge(z_done, KT + n + 1)
                src = banks(2 * (n % 2))
                if n in (0, 2):
                    if n == 0:
                        act.wait_ge(u_lo_done, KT)
                    else:
                        act.wait_ge(glu_done, 1)
                    nc.scalar.activation(glu_gate[:, :], src, ACT.Sigmoid).then_inc(glu_sig_done, 1)
                if n >= 4:
                    copy(z_pool[:, n - 4, :], src).then_inc(zp_done, 1)
                cut_hi(n + 2)

            def take_half(pair, r):
                hz = 8 * pair + r
                part, half = divmod(r, 2)
                cs = slice(half * HALF, (half + 1) * HALF)
                src = ps[:, r % 2, :]
                act.wait_ge(h_done, hz + 1)
                if part == 0:
                    if pair >= 2:
                        act.wait_ge(scores_done, STEPS * (pair - 1))
                    elif pair == 0:
                        act.wait_ge(partial_done, 12)
                    copy(q_hi[pair % 2][:, cs], src, scale=HEAD_DIM ** -0.5).then_inc(half_hi, 1)
                elif part == 1:
                    copy(k_hi[pair % 2][:, cs], src).then_inc(half_hi, 1)
                elif part == 2:
                    copy(mid[:, 5, cs], src).then_inc(h_free[r % 2], 1)
                else:
                    if pair >= 2:
                        act.wait_ge(pv_done, ST * (pair - 1))
                    copy(v_hi[pair % 2][:, 4 * half:4 * half + 4, :], src.rearrange("p (t d) -> p t d", d=P))\
                        .then_inc(half_hi, 1)
                if r in (1, 3, 5) and N_P1 + 3 * pair + part + 2 < N_GATE0:
                    cut_hi(N_P1 + 3 * pair + part + 2)

            for r in range(6):
                take_half(0, r)
            N_STEPS = PAIRS * STEPS
            for a in range(N_STEPS + 2):
                pair, i = divmod(a, STEPS)
                if a < N_STEPS:
                    col, width = a % (2 * STEPS), P * blocks_of(i // 2)
                    act.wait_ge(biased, a + 1)
                    nc.scalar.activation(probs[a % 2][:, 0:width], probs[a % 2][:, 0:width], ACT.Exp,
                                         bias=neg_max[:, col:col + 1], scale=-1.0,
                                         accum_out=row_sum[:, col:col + 1]).then_inc(exp_done, 1)
                if a < N_STEPS and i == 0:
                    take_half(pair, 6)
                    take_half(pair, 7)
                if a >= 3 and a % 2 == 1:
                    tile = (a - 3) // 2
                    act.wait_ge(pv_done, tile + 1)
                    if tile == ST:
                        act.wait_ge(pooled_done, 2)
                    ts = slice(tile % ST * P, (tile % ST + 1) * P)
                    for h in range(2):
                        rows = slice(h * HEAD_DIM, (h + 1) * HEAD_DIM)
                        copy(mid[rows, 2 + tile // ST, ts], ps[rows, 2, h * P:(h + 1) * P]).then_inc(o_copied, 1)
                if 1 <= a <= N_STEPS:
                    b = a - 1
                    nb = blocks_of(b % STEPS // 2)
                    act.wait_ge(pt_done, b + 1)
                    if b >= 2:
                        act.wait_ge(pv_done, b // 2)
                    copy(pt_hi[:, 0:nb, b % 2, :], banks(6)[:, 0:nb * P].rearrange("p (b q) -> p b q", q=P))\
                        .then_inc(pt_hi_done, 1)
                if pair < PAIRS - 1 and i in half_after:
                    take_half(pair + 1, half_after[i])

            for b in range(2):
                act.wait_ge(w_arrived[b], gate_arrived(0, b))
                act.wait_ge(*block_used(N_GATE0 + b - 2))
                copy(w_hi[b][:, :, :], w_raw[b][:, :, :]).then_inc(w_hi_done, 1)

            for t in range(2):
                act.wait_ge(pm_done, t + 1)
                copy(mid[:, t, :], banks(4 + 2 * t), scale=cols[:, R_PSC + t:R_PSC + t + 1]).then_inc(pm_scaled, 1)
            for t in range(2):
                act.wait_ge(centred, t + 1)
                nc.scalar.activation(sq[:, t, :], mid[:, 6 + t, :], ACT.Square).then_inc(squared, 1)
            act.wait_ge(cvar_read, 1)
            nc.scalar.activation(conv_rstd[:, :], conv_rstd[:, :], ACT.Sqrt).then_inc(cstd_done, 1)
            for t in range(2):
                act.wait_ge(cnormed, t + 1)
                if t == 1:
                    act.wait_ge(conv_done, 1)
                nc.scalar.activation(conv_sig[:, :], mid[:, 6 + t, :], ACT.Sigmoid,
                                     bias=cols[:, R_CLNB + t:R_CLNB + t + 1],
                                     scale=cols[:, R_CLNG + t:R_CLNG + t + 1]).then_inc(conv_sig_done, 1)
            act.wait_ge(pm_scaled, 2)
            act.wait_ge(o_copied, N_STEPS)
            act.wait_ge(pt_lo_done, N_STEPS)
            for k in range(KT):
                if k == 6:
                    act.wait_ge(conv_done, 2)
                copy(br_hi[:, k, :], mid[:, k, :]).then_inc(br_hi_done, 1)
            act.wait_ge(conv_done, 2)

            with act.Fori(0, KT) as j:
                for b in range(4):
                    if b < 3:
                        act.wait_ge(g_done, j * 3 + (b + 1))
                        if b == 0:
                            act.wait_ge(w_lo_done, j * 4 + (N_GATE0 + 2))
                        nc.scalar.activation(gate[b][:, :], banks(2 * (b % 2)), ACT.Sigmoid,
                                             bias=cols[:, bass.ds(j + (R_GATE + 8 * b), 1)]).then_inc(sig_done, 1)
                    else:
                        act.wait_ge(y_done, j * 3 + 3)
                    act.wait_ge(w_arrived[b % 2], gate_arrived(j, b + 2) if b < 2 else gate_arrived(j + 1, b - 2))
                    copy(w_hi[b % 2][:, :, :], w_raw[b % 2][:, :, :]).then_inc(w_hi_done, 1)

            act.wait_ge(g_done, 3 * KT)
            act.wait_ge(y_done, 3 * KT)
            for k in range(KT):
                act.wait_ge(merged_step, 3 * (k + 1))
                copy(act_hi[:, k, :], mid[:, k, :]).then_inc(mg_hi_done, 1)
                act.wait_ge(row_in[k % 2], 16 * (k // 2 + 1))
                copy(br_hi[:, k, :], row_raw[k % 2][:, :]).then_inc(row_hi_done, 1)

            def take_root(count, t):
                act.wait_ge(var_done, count + 1)
                nc.scalar.activation(rstd[:, t:t + 1], rstd[:, t:t + 1], ACT.Sqrt).then_inc(std_done, 1)

            def norm(count, t, tile):
                act.wait_ge(norm_ready, count + 1)
                nc.scalar.activation(tile[:, :], mid[:, t, :], ACT.Identity, bias=neg_mean[:, t:t + 1],
                                     scale=rstd[:, t:t + 1]).then_inc(normed, 1)

            for t in range(ST + 2):
                if t < ST:
                    take_root(ST + 2 * t, t)
                if 1 <= t <= ST:
                    q = t - 1
                    if q >= 2:
                        act.wait_ge(x2_lo_done, q - 1)
                    norm(ST + 2 * q + 1, q, tmp[q % 2])
                if t < ST:
                    norm(ST + 2 * t, t, mix_tmp)
                if 1 <= t <= ST:
                    copy(mid[:, t - 1, :], mid[:, t - 1, :], scale=ALPHA).then_inc(x1_scaled, 1)
                if t >= 2:
                    q = t - 2
                    act.wait_ge(x2t_done, q + 1)
                    for k in range(KT):
                        ins = nc.scalar.activation(tmp[q % 2][:, k * P:(k + 1) * P],
                                                   banks(4 + 2 * (q % 2))[:, k * P:(k + 1) * P], ACT.Identity,
                                                   bias=mod[:, 24 + k:25 + k], scale=mod[:, 32 + k:33 + k])
                    ins.then_inc(x2_tmp_done, 1)
                    act.wait_ge(x2_tmp_done, q + 1)
                    copy(act_hi[:, :, q * P:(q + 1) * P], tmp[q % 2][:, :].rearrange("p (k s) -> p k s", s=P))\
                        .then_inc(x2_hi_done, 1)
                if t < ST:
                    take_root(ST + 2 * t + 1, t)

            def mlp_group(g, last):
                for t in range(GROUP):
                    act.wait_ge(f1_done, g * GROUP + (t + 1))
                    if t >= 2:
                        act.wait_ge(h_lo_done, g * GROUP + (t - 1))
                    nc.scalar.activation(tmp[t % 2][:, :], banks(2 * (t % 2)), ACT.Relu,
                                         bias=cols[:, bass.ds(g * GROUP + (R_FF1 + t), 1)]).then_inc(relu_done, 1)
                    act.wait_ge(relu_done, g * GROUP + (t + 1))
                    nc.scalar.activation(tmp[t % 2][:, :], tmp[t % 2][:, :], ACT.Square).then_inc(sq_done, 1)
                    act.wait_ge(sq_done, g * GROUP + (t + 1))
                    copy(h_hi[:, t, :], tmp[t % 2][:, :]).then_inc(h_hi_done, 1)
                    if not (last and t >= 2):
                        act.wait_ge(w_arrived[t % 2], ff_arrived(g, t + 2))
                        copy(w_hi[t % 2][:, :, :], w_raw[t % 2][:, :, :]).then_inc(w_hi_done, 1)
                    act.wait_ge(row_scaled, g * GROUP + (t + 1))
                    copy(w2_hi[:, t, :], row_raw[t % 2][:, :]).then_inc(row_hi_done, 1)

            with act.Fori(0, GROUPS - 1) as g:
                mlp_group(g, False)
            mlp_group(GROUPS - 1, True)
            for t in range(ST):
                if t >= 2:
                    act.wait_ge(stored[t % 2], 16 * (t // 2))
                take_root(3 * ST + t, t)
                norm(3 * ST + t, t, tmp[t % 2])

        @block.vector
        def _(dve):
            steps = [0]

            def link(ins, offset=0):
                steps[0] += 1
                ins.then_inc(dve_step, 1)
                dve.wait_ge(dve_step, offset + steps[0])

            def cut_lo(n):
                dve.wait_ge(w_hi_done, n + 1)
                nc.vector.tensor_tensor(w_lo[n % 2][:, :, :], w_raw[n % 2][:, :, :], f(w_hi[n % 2][:, :, :]),
                                        ALU.subtract).then_inc(w_lo_done, 1)

            def stats(src, t):
                for half in range(2):
                    ins = nc.vector.bn_stats(bn[:, 6 * half:6 * half + 6], src[:, half * HALF:(half + 1) * HALF])
                link(ins)
                link(nc.vector.bn_aggr(mean_var[:, t, :], bn[:, :]))
                nc.vector.tensor_scalar_add(rstd[:, t:t + 1], mean_var[:, t, 1:2], EPS).then_inc(var_done, 1)

            def scale_bias(count, t):
                dve.wait_ge(std_done, count + 1)
                link(nc.vector.reciprocal(rstd[:, t:t + 1], rstd[:, t:t + 1]))
                nc.vector.scalar_tensor_tensor(out=neg_mean[:, t:t + 1], in0=mean_var[:, t, 0:1], scalar=-1.0,
                                               in1=rstd[:, t:t + 1], op0=ALU.mult, op1=ALU.mult)\
                    .then_inc(norm_ready, 1)

            dve.wait_ge(c_sig_done, 1)
            link(nc.vector.tensor_tensor(c_act[:, :], c_raw[:, :], c_sig[:, :], ALU.mult))
            for i in range(ST):
                dve.wait_ge(x_in[i], 16)
                stats(mid[:, i, :], i)
            for i in range(ST):
                scale_bias(i, i)

            def ada_chunk(i):
                dve.wait_ge(ada_in[i % 3], 16 * (i // 3 + 1))
                if i >= 2:
                    dve.wait_ge(reduced, i - 1)
                dst, src = partial[i % 2][:, :], ada[i % 3]
                link(nc.vector.tensor_scalar(dst, src[:, 0, :], c_act[:, 0:1], None, ALU.mult))
                for k in range(1, 8):
                    ins = nc.vector.scalar_tensor_tensor(out=dst, in0=src[:, k, :], scalar=c_act[:, k:k + 1], in1=dst,
                                                         op0=ALU.mult, op1=ALU.add)
                    if k < 7:
                        link(ins)
                ins.then_inc(partial_done, 1)

            def gate_chunk(i):
                dve.wait_ge(reduced, i + 1)
                dve.wait_ge(ada_bias_in, 32)
                half = slice(i % 2 * HALF, i % 2 * HALF + HALF)
                dst = (gate_mix if i < 6 else gate_ff)[:, half]
                nc.vector.tensor_tensor(dst, ps[:, 4 + i % 2, :], dst, ALU.add).then_inc(gates_done, 1)

            def mod_columns(c0, bank):
                link(nc.vector.tensor_tensor(mod[:, c0:c0 + 16], ps[:, bank, 0:16], cols[:, c0:c0 + 16], ALU.add))
                nc.vector.tensor_scalar_add(mod[:, c0 + 8:c0 + 16], mod[:, c0 + 8:c0 + 16], 1.0).then_inc(mod_done, 1)

            dve.wait_ge(cols_t, 2)
            nc.vector.tensor_copy(cols[:, 0:ROWS_A], ps[:, 4, 0:ROWS_A])
            nc.vector.tensor_copy(cols[:, ROWS_A:ROWS_A + ROWS_C], ps[:, 5, 0:ROWS_C]).then_inc(cols_done, 1)
            for i in range(4):
                ada_chunk(i)
            dve.wait_ge(rel_in, 16)
            nc.vector.tensor_copy(rel_ext[:, 2 * REL_CLIP:768],
                                  rel_ext[:, 2 * REL_CLIP - 1:2 * REL_CLIP].to_broadcast([HEADS, 768 - 2 * REL_CLIP]))\
                .then_inc(rel_done, 1)
            dve.wait_ge(cols_done, 1)
            dve.wait_ge(reduced, 4)
            mod_columns(0, 6)
            cut_lo(0)
            cut_lo(1)
            for k in range(KT):
                dve.wait_ge(u_tmp_done, k + 1)
                link(nc.vector.tensor_copy(act_hi[:, k, :], u_tmp[k % 2][:, :]))
                nc.vector.tensor_tensor(act_lo[:, k, :], u_tmp[k % 2][:, :], f(act_hi[:, k, :]), ALU.subtract)\
                    .then_inc(u_lo_done, 1)
            chunks_at = {0: (4,), 1: (5, 6), 2: (7,), 3: (8, 9), 4: (10,), 5: (11,)}
            for n in range(N_P1):
                for i in chunks_at[n]:
                    ada_chunk(i)
                if n in (1, 3):
                    t = n // 2
                    dve.wait_ge(z_done, KT + n + 1)
                    dve.wait_ge(glu_sig_done, t + 1)
                    dve.wait_ge(consts_done, 3)
                    nc.vector.tensor_tensor(h_pad[:, t, PAD:PAD + SEQ], banks(2), glu_gate[:, :], ALU.mult)\
                        .then_inc(glu_done, 1)
                cut_lo(n + 2)
                for i in chunks_at[n]:
                    if i in (4, 5, 10, 11):
                        gate_chunk(i)
            dve.wait_ge(reduced, 10)
            mod_columns(24, 7)

            def take_half_lo(pair, r):
                part, half = divmod(r, 2)
                cs = slice(half * HALF, (half + 1) * HALF)
                src, s = ps[:, r % 2, :], pair % 2
                if part != 2:
                    dve.wait_ge(half_hi, 6 * pair + (r if r < 4 else r - 2) + 1)
                if part == 0:
                    nc.vector.scalar_tensor_tensor(out=q_lo[s][:, cs], in0=src, scalar=HEAD_DIM ** -0.5,
                                                   in1=f(q_hi[s][:, cs]), op0=ALU.mult, op1=ALU.subtract)\
                        .then_inc(h_free[r % 2], 1)
                elif part == 1:
                    nc.vector.tensor_tensor(k_lo[s][:, cs], src, f(k_hi[s][:, cs]), ALU.subtract)\
                        .then_inc(h_free[r % 2], 1)
                elif part == 3:
                    ts = slice(4 * half, 4 * half + 4)
                    nc.vector.tensor_tensor(v_lo[s][:, ts, :], src.rearrange("p (t d) -> p t d", d=P),
                                            f(v_hi[s][:, ts, :]), ALU.subtract).then_inc(h_free[r % 2], 1)
                if r in (1, 3, 5) and N_P1 + 3 * pair + part + 2 < N_GATE0:
                    cut_lo(N_P1 + 3 * pair + part + 2)

            def conv_tap(n):
                t, tap = divmod(n, TAPS)
                w = cols[:, ROWS_A + 2 * tap + t:ROWS_A + 2 * tap + t + 1]
                src, acc = h_pad[:, t, tap:tap + SEQ], mid[:, 6 + t, :]
                if tap == 0:
                    nc.vector.tensor_scalar(acc, src, w, cols[:, R_CONVB + t:R_CONVB + t + 1], ALU.mult, ALU.add)\
                        .then_inc(tap_done, 1)
                else:
                    dve.wait_ge(tap_done, n)
                    nc.vector.scalar_tensor_tensor(out=acc, in0=src, scalar=w, in1=acc, op0=ALU.mult, op1=ALU.add)\
                        .then_inc(tap_done, 1)

            dve.wait_ge(glu_done, 2)
            for r in range(6):
                take_half_lo(0, r)
            N_STEPS = PAIRS * STEPS
            for a in range(N_STEPS + 1):
                pair, i = divmod(a, STEPS)
                if a < N_STEPS:
                    col, width = a % (2 * STEPS), P * blocks_of(i // 2)
                    dve.wait_ge(scores_done, a + 1)
                    if i == 0:
                        dve.wait_ge(bias_ready, pair + 1)
                    if a >= 2:
                        dve.wait_ge(pt_done, a - 1)
                    nb = blocks_of(i // 2)
                    bias = bias_rev[pair % 2][:, i % 2, 0:width][:, ::-1]
                    nc.vector.tensor_tensor_reduce(out=like_scores(probs[a % 2][:, 0:width], nb), in0=score_cols(nb),
                                                   in1=like_scores(bias, nb),
                                                   scale=-1.0, scalar=3e38, op0=ALU.add, op1=ALU.min,
                                                   accum_out=neg_max[:, col:col + 1]).then_inc(biased, 1)
                if a < N_STEPS and i == 0:
                    take_half_lo(pair, 6)
                    take_half_lo(pair, 7)
                if a < 2 * TAPS:
                    conv_tap(a)
                if a < N_STEPS:
                    dve.wait_ge(exp_done, a + 1)
                    link(nc.vector.reciprocal(inv_sum[:, col:col + 1], row_sum[:, col:col + 1]))
                    nc.vector.tensor_scalar(probs[a % 2][:, 0:width], probs[a % 2][:, 0:width],
                                            inv_sum[:, col:col + 1], None, ALU.mult).then_inc(probs_done, 1)
                if a >= 1:
                    b = a - 1
                    nb = blocks_of(b % STEPS // 2)
                    dve.wait_ge(pt_hi_done, b + 1)
                    nc.vector.tensor_tensor(pt_lo[:, 0:nb, b % 2, :],
                                            banks(6)[:, 0:nb * P].rearrange("p (b q) -> p b q", q=P),
                                            f(pt_hi[:, 0:nb, b % 2, :]), ALU.subtract).then_inc(pt_lo_done, 1)
                if pair < PAIRS - 1 and i in half_after:
                    take_half_lo(pair + 1, half_after[i])

            for b in range(2):
                cut_lo(N_GATE0 + b)
            dve.wait_ge(cmean_done, 1)
            for t in range(2):
                acc = mid[:, 6 + t, :]
                nc.vector.scalar_tensor_tensor(out=acc, in0=banks(0), scalar=-1.0 / D_CONV, in1=acc,
                                               op0=ALU.mult, op1=ALU.add).then_inc(centred, 1)
            dve.wait_ge(cvar_done, 1)
            nc.vector.tensor_scalar(conv_rstd[:, :], banks(2), 1.0 / D_CONV, EPS, ALU.mult, ALU.add)\
                .then_inc(cvar_read, 1)
            dve.wait_ge(cstd_done, 1)
            link(nc.vector.reciprocal(conv_rstd[:, :], conv_rstd[:, :]))
            dve.wait_ge(centred, 2)
            dve.wait_ge(squared, 2)
            for t in range(2):
                acc = mid[:, 6 + t, :]
                nc.vector.tensor_tensor(acc, acc, conv_rstd[:, :], ALU.mult).then_inc(cnormed, 1)
            for t in range(2):
                acc = mid[:, 6 + t, :]
                dve.wait_ge(conv_sig_done, t + 1)
                link(nc.vector.tensor_scalar(acc, acc, cols[:, R_CLNG + t:R_CLNG + t + 1],
                                             cols[:, R_CLNB + t:R_CLNB + t + 1], ALU.mult, ALU.add))
                nc.vector.tensor_tensor(acc, acc, conv_sig[:, :], ALU.mult).then_inc(conv_done, 1)
            for k in range(KT):
                dve.wait_ge(br_hi_done, k + 1)
                nc.vector.tensor_tensor(br_lo[:, k, :], mid[:, k, :], f(br_hi[:, k, :]), ALU.subtract)\
                    .then_inc(br_lo_done, 1)

            dve.wait_ge(pm_done, 2)
            with dve.Fori(0, KT) as j:
                out_tile = mid[:, bass.ds(j, 1), :].rearrange("p o s -> p (o s)")
                for b in range(4):
                    if b == 3:
                        for y in range(3):
                            dve.wait_ge(y_done, j * 3 + (y + 1))
                            dve.wait_ge(sig_done, j * 3 + (y + 1))
                            dst = out_tile if y == 0 else tmp[y - 1][:, :]
                            nc.vector.tensor_tensor(dst, banks((4, 6, 2)[y]), gate[y][:, :], ALU.mult)\
                                .then_inc(y_used, 1)
                            dve.wait_ge(y_used, j * 3 + (y + 1))
                            if y > 0:
                                if y == 2:
                                    dve.wait_ge(merged_step, j * 3 + 1)
                                nc.vector.tensor_tensor(out_tile, out_tile, tmp[y - 1][:, :], ALU.add)\
                                    .then_inc(merged_step, y)
                    dve.wait_ge(w_hi_done, j * 4 + (N_GATE0 + b + 3))
                    nc.vector.tensor_tensor(w_lo[b % 2][:, :, :], w_raw[b % 2][:, :, :], f(w_hi[b % 2][:, :, :]),
                                            ALU.subtract).then_inc(w_lo_done, 1)

            for k in range(KT):
                dve.wait_ge(mg_hi_done, k + 1)
                nc.vector.tensor_tensor(act_lo[:, k, :], mid[:, k, :], f(act_hi[:, k, :]), ALU.subtract)\
                    .then_inc(mg_lo_done, 1)
                dve.wait_ge(row_hi_done, k + 1)
                nc.vector.tensor_tensor(br_lo[:, k, :], row_raw[k % 2][:, :], f(br_hi[:, k, :]), ALU.subtract)\
                    .then_inc(row_lo_done, 1)

            def cut_x2(t):
                dve.wait_ge(x2_hi_done, t + 1)
                nc.vector.tensor_tensor(act_lo[:, :, t * P:(t + 1) * P],
                                        tmp[t % 2][:, :].rearrange("p (k s) -> p k s", s=P),
                                        f(act_hi[:, :, t * P:(t + 1) * P]), ALU.subtract).then_inc(x2_lo_done, 1)

            dve.wait_ge(ln_in, 32)
            dve.wait_ge(ff2b_scaled, 1)
            for t in range(ST + 2):
                if t < ST:
                    row = mid[:, t, :]
                    dve.wait_ge(mix_done, t + 1)
                    nc.vector.tensor_tensor(mix_tmp[:, :], banks(2 * (t % 2)), gate_mix[:, :], ALU.mult)\
                        .then_inc(mix_free, 1)
                    dve.wait_ge(mix_free, t + 1)
                    dve.wait_ge(res_in[t], 16)
                    link(nc.vector.scalar_tensor_tensor(out=row, in0=row, scalar=ALPHA, in1=mix_tmp[:, :],
                                                        op0=ALU.mult, op1=ALU.add))
                    stats(row, t)
                if t >= 3:
                    cut_x2(t - 3)
                if 1 <= t <= ST:
                    scale_bias(ST + 2 * (t - 1) + 1, t - 1)
                if t < ST:
                    scale_bias(ST + 2 * t, t)
                if t < ST:
                    dve.wait_ge(normed, ST + 2 * t + 1)
                    link(nc.vector.tensor_tensor(mix_tmp[:, :], mix_tmp[:, :], ln_g[:, :], ALU.mult))
                    nc.vector.tensor_tensor(row, mix_tmp[:, :], ln_b[:, :], ALU.add).then_inc(x1_done, 1)
                    dve.wait_ge(x1_done, t + 1)
                    stats(row, t)
            cut_x2(ST - 1)
            dve.wait_ge(res_done, ST)

            def mlp_group(g, last):
                for t in range(GROUP):
                    row = row_raw[t % 2]
                    dve.wait_ge(row_in[t % 2], g * (16 * GROUP // 2) + (16 * KT // 2 + 16 * (t // 2 + 1)))
                    nc.vector.tensor_tensor(row[:, :], row[:, :], gate_ff[:, :], ALU.mult).then_inc(row_scaled, 1)
                    dve.wait_ge(row_scaled, g * GROUP + (t + 1))
                    dve.wait_ge(h_hi_done, g * GROUP + (t + 1))
                    nc.vector.tensor_tensor(h_lo[:, t, :], tmp[t % 2][:, :], f(h_hi[:, t, :]), ALU.subtract)\
                        .then_inc(h_lo_done, 1)
                    if not (last and t >= 2):
                        dve.wait_ge(w_hi_done, g * GROUP + (N_FF0 + t + 3))
                        nc.vector.tensor_tensor(w_lo[t % 2][:, :, :], w_raw[t % 2][:, :, :],
                                                f(w_hi[t % 2][:, :, :]), ALU.subtract).then_inc(w_lo_done, 1)
                    dve.wait_ge(row_hi_done, g * GROUP + (KT + t + 1))
                    nc.vector.tensor_tensor(w2_lo[:, t, :], row[:, :], f(w2_hi[:, t, :]), ALU.subtract)\
                        .then_inc(row_lo_done, 1)
                for t in range(ST):
                    dve.wait_ge(f2_done, g * ST + (t + 1))
                    nc.vector.tensor_tensor(mid[:, t, :], mid[:, t, :], banks(4 + 2 * (t % 2)), ALU.add)\
                        .then_inc(acc_done, 1)
                    if last:
                        dve.wait_ge(acc_done, g * ST + (t + 1))
                        stats(mid[:, t, :], t)
                        if t >= 1:
                            finish_tile(t - 1)
                        scale_bias(3 * ST + t, t)
                if last:
                    finish_tile(ST - 1)

            def finish_tile(t):
                dve.wait_ge(normed, 3 * ST + t + 1)
                if t == 0:
                    dve.wait_ge(ln2_in, 32)
                tile = tmp[t % 2][:, :]
                link(nc.vector.tensor_tensor(tile, tile, ln_g[:, :], ALU.mult))
                nc.vector.tensor_tensor(tile, tile, ln_b[:, :], ALU.add).then_inc(y_ready, 1)

            with dve.Fori(0, GROUPS - 1) as g:
                mlp_group(g, False)
            mlp_group(GROUPS - 1, True)

        @block.tensor
        def _(pe):
            def product(out, parts, first, last):
                (sh, sl), (mh, ml) = parts
                nc.tensor.matmul(out, sh, mh, start=first, stop=False)
                nc.tensor.matmul(out, sh, ml, start=False, stop=False)
                return nc.tensor.matmul(out, sl, mh, start=False, stop=last)

            def act_part(k, cs):
                return act_hi[:, k, cs], act_lo[:, k, cs]

            def w_part(n, k):
                return w_hi[n % 2][:, k, :], w_lo[n % 2][:, k, :]

            def half_cols(h):
                return slice(h * HALF, (h + 1) * HALF)

            pe.wait_ge(consts_done, 2)
            pe.wait_ge(small_in, 16 * 8)
            nc.tensor.transpose(ps[:, 4, 0:ROWS_A], rows_a[:, :], ident[0:ROWS_A, 0:ROWS_A]).then_inc(cols_t, 1)
            nc.tensor.transpose(ps[:, 5, 0:ROWS_C], rows_c[:, :], ident[0:ROWS_C, 0:ROWS_C]).then_inc(cols_t, 1)

            def reduce_chunk(i):
                pe.wait_ge(partial_done, i + 1)
                if i in (4, 5, 10, 11):
                    if i < 6:
                        pe.wait_ge(cols_done, 1)
                    else:
                        pe.wait_ge(gates_done, i - 9)
                    ins = nc.tensor.matmul(ps[:, 4 + i % 2, :], ones_row[:, :], partial[i % 2][:, :],
                                           start=True, stop=True)
                else:
                    bank, first = (6, 0) if i < 4 else (7, 6)
                    for m in range(4):
                        col = (i - first) * 4 + m
                        ins = nc.tensor.matmul(ps[:, bank, col:col + 1], partial[i % 2][:, m * P:(m + 1) * P],
                                               ones_row[:, 0:1], start=True, stop=True)
                ins.then_inc(reduced, 1)

            for i in range(4):
                reduce_chunk(i)
            pe.wait_ge(normed, ST)
            for k in range(KT):
                if k >= 2:
                    pe.wait_ge(u_tmp_done, k - 1)
                for i in range(ST):
                    ins = nc.tensor.transpose(ps[:, 2 * (k % 2) + i // 4, (i % 4) * P:(i % 4 + 1) * P],
                                              mid[:, i, k * P:(k + 1) * P], ident[:, :])
                ins.then_inc(z_done, 1)
            chunks_at = {0: (4,), 1: (5, 6), 2: (7,), 3: (8, 9), 4: (10,), 5: (11,)}
            for n in range(N_P1):
                pe.wait_ge(w_lo_done, n + 1)
                if n < 2:
                    pe.wait_ge(u_tmp_done, KT + n - 1)
                elif n in (2, 4):
                    pe.wait_ge(glu_sig_done, n // 2)
                else:
                    pe.wait_ge(glu_done, n // 2)
                for h in range(2):
                    for k in range(KT):
                        if n == 0 and h == 0:
                            pe.wait_ge(u_lo_done, k + 1)
                        ins = product(ps[:, 2 * (n % 2) + h, :], (w_part(n, k), act_part(k, half_cols(h))),
                                      k == 0, k == KT - 1)
                ins.then_inc(z_done, 1)
                for i in chunks_at[n]:
                    reduce_chunk(i)

            def project(pair, m):
                part, r = divmod(m, 48)
                half, kk = divmod(r, 24)
                k, term = divmod(kk, 3)
                n, hz = N_P1 + 3 * pair + part, 2 * part + half
                if r == 0:
                    pe.wait_ge(w_lo_done, n + 1)
                if kk == 0:
                    wait_bank(pair, hz)
                (sh, sl), (mh, ml) = w_part(n, k), act_part(k, half_cols(half))
                s, v = ((sh, mh), (sh, ml), (sl, mh))[term]
                ins = nc.tensor.matmul(ps[:, hz % 2, :], s, v, start=kk == 0, stop=kk == 23)
                if kk == 23:
                    ins.then_inc(h_done, 1)

            def wait_bank(pair, r):
                if pair == 0 and r < 2:
                    pe.wait_ge(zp_done, 1)
                else:
                    pe.wait_ge(h_free[r % 2], 4 * pair + r // 2)

            def transpose_v(pair, half):
                if half == 0:
                    for b in range(2):
                        pe.wait_ge(h_free[b], 4 * pair + 3)
                wait_bank(pair, 6 + half)
                for t in range(4 * half, 4 * half + 4):
                    ins = nc.tensor.transpose(ps[:, half, (t % 4) * P:(t % 4 + 1) * P], mid[:, 5, t * P:(t + 1) * P],
                                              ident[:, :])
                ins.then_inc(h_done, 1)

            def scores(a):
                pair, i = divmod(a, STEPS)
                t, h = divmod(i, 2)
                nb = blocks_of(t)
                s, rows, qs = pair % 2, slice(h * HEAD_DIM, (h + 1) * HEAD_DIM), slice(t * P, (t + 1) * P)
                if i == 0:
                    for b in range(2):
                        pe.wait_ge(h_free[b], 4 * pair + 2)
                if a == 0:
                    pe.wait_ge(gates_done, 4)
                    pe.wait_ge(mod_done, 2)
                else:
                    pe.wait_ge(biased, a)
                first_key = (t + 1 - nb) * P
                parts = 2 if nb == BAND_BLOCKS else 1
                n = nb * P // parts
                for part in range(parts):
                    ks = slice(first_key + part * n, first_key + (part + 1) * n)
                    ins = product(ps[:, 4 + part, 0:n],
                                  ((q_hi[s][rows, qs], q_lo[s][rows, qs]), (k_hi[s][rows, ks], k_lo[s][rows, ks])),
                                  True, True)
                ins.then_inc(scores_done, 1)

            def transpose_probs(a):
                pe.wait_ge(probs_done, a + 1)
                if a >= 1:
                    pe.wait_ge(pt_lo_done, a)
                for b in range(blocks_of(a % STEPS // 2)):
                    ins = nc.tensor.transpose(banks(6)[:, b * P:(b + 1) * P], probs[a % 2][:, b * P:(b + 1) * P],
                                              ident[:, :])
                ins.then_inc(pt_done, 1)

            def weigh(tile):
                pair, t = divmod(tile, ST)
                nb = blocks_of(t)
                s = pair % 2
                pe.wait_ge(pt_lo_done, 2 * tile + 2)
                if t == 0:
                    for b in range(2):
                        pe.wait_ge(h_free[b], 4 * pair + 4)
                if tile >= 1:
                    pe.wait_ge(o_copied, 2 * tile)
                else:
                    pe.wait_ge(zp_done, 2)
                for b in range(nb):
                    kt = t + 1 - nb + b
                    ins = product(ps[:, 2, 0:2 * P],
                                  ((v_hi[s][:, kt, :], v_lo[s][:, kt, :]), (pt_hi[:, b, :, :], pt_lo[:, b, :, :])),
                                  b == 0, b == nb - 1)
                ins.then_inc(pv_done, 1)

            for m in range(PROJ):
                project(0, m)
            N_STEPS = PAIRS * STEPS
            for a in range(N_STEPS + 2):
                pair, i = divmod(a, STEPS)
                if a < N_STEPS:
                    scores(a)
                    if i == 0:
                        transpose_v(pair, 0)
                        transpose_v(pair, 1)
                if pair < PAIRS - 1:
                    for m in range(PER_STEP * i, PER_STEP * i + PER_STEP // 2):
                        project(pair + 1, m)
                if a >= 3 and a % 2 == 1:
                    weigh((a - 3) // 2)
                if 1 <= a <= N_STEPS:
                    transpose_probs(a - 1)
                if pair < PAIRS - 1:
                    for m in range(PER_STEP * i + PER_STEP // 2, PER_STEP * (i + 1)):
                        project(pair + 1, m)

            pe.wait_ge(pooled_done, 2)
            pe.wait_ge(pool_w_in, 64)
            pe.wait_ge(biased, N_STEPS)
            pe.wait_ge(pt_lo_done, N_STEPS)
            for t in range(2):
                for h in range(2):
                    ins = nc.tensor.matmul(ps[:, 4 + 2 * t + h, :], w_pool_bd[:, t, :], z_pool[:, t, half_cols(h)],
                                           start=True, stop=True)
                ins.then_inc(pm_done, 1)
            pe.wait_ge(tap_done, 2 * TAPS)
            for b in range(2):
                pe.wait_ge(h_free[b], 4 * PAIRS)
            for h in range(2):
                for t in range(2):
                    ins = nc.tensor.matmul(ps[:, h, :], ones_row[:, :], mid[:, 6 + t, half_cols(h)],
                                           start=t == 0, stop=t == 1)
            ins.then_inc(cmean_done, 1)
            pe.wait_ge(squared, 2)
            pe.wait_ge(o_copied, N_STEPS)
            for h in range(2):
                for t in range(2):
                    ins = nc.tensor.matmul(ps[:, 2 + h, :], ones_row[:, :], sq[:, t, half_cols(h)],
                                           start=t == 0, stop=t == 1)
            ins.then_inc(cvar_done, 1)

            pe.wait_ge(centred, 2)
            pe.wait_ge(pm_scaled, 2)
            pe.wait_ge(cvar_read, 1)
            with pe.Fori(0, KT) as j:
                for b in range(3):
                    pe.wait_ge(w_lo_done, j * 4 + (N_GATE0 + b + 1))
                    if b == 2:
                        pe.wait_ge(sig_done, j * 3 + 1)
                    for h in range(2):
                        for k in range(KT):
                            ins = product(ps[:, 2 * (b % 2) + h, :], (w_part(b, k), act_part(k, half_cols(h))),
                                          k == 0, k == KT - 1)
                    ins.then_inc(g_done, 1)
                pe.wait_ge(w_lo_done, j * 4 + (N_GATE0 + 4))
                pe.wait_ge(br_lo_done, KT)
                for y, (k0, k1, bank) in enumerate(((0, 2, 4), (2, 6, 6), (6, 8, 2))):
                    if y == 2:
                        pe.wait_ge(sig_done, j * 3 + 2)
                    for h in range(2):
                        cs = half_cols(h)
                        for k in range(k0, k1):
                            ins = product(ps[:, bank + h, :], (w_part(3, k), (br_hi[:, k, cs], br_lo[:, k, cs])),
                                          k == k0, k == k1 - 1)
                    ins.then_inc(y_done, 1)

            def transpose_x2(t):
                pe.wait_ge(normed, ST + 2 * t + 2)
                if t >= 2:
                    pe.wait_ge(x2_tmp_done, t - 1)
                for k in range(KT):
                    ins = nc.tensor.transpose(banks(4 + 2 * (t % 2))[:, k * P:(k + 1) * P],
                                              tmp[t % 2][:, k * P:(k + 1) * P], ident[:, :])
                ins.then_inc(x2t_done, 1)

            pe.wait_ge(sig_done, 3 * KT)
            pe.wait_ge(y_used, 3 * KT)
            for t in range(ST):
                if t >= 2:
                    pe.wait_ge(mix_free, t - 1)
                ts = slice(t * P, (t + 1) * P)
                for k in range(KT):
                    if t >= 2 and k == KT // 2:
                        transpose_x2(t - 2)
                    if t == 0:
                        pe.wait_ge(mg_lo_done, k + 1)
                        pe.wait_ge(row_lo_done, k + 1)
                    for h in range(2):
                        cs = half_cols(h)
                        ins = product(ps[:, 2 * (t % 2) + h, :], (act_part(k, ts), (br_hi[:, k, cs], br_lo[:, k, cs])),
                                      k == 0, k == KT - 1)
                ins.then_inc(mix_done, 1)
            transpose_x2(ST - 2)

            def ff1_half(g, t, h):
                for k in range(KT):
                    ins = product(ps[:, 2 * (t % 2) + h, :], (w_part(t, k), act_part(k, half_cols(h))),
                                  k == 0, k == KT - 1)
                if h == 1:
                    ins.then_inc(f1_done, 1)

            def mlp_group(g, first):
                if first:
                    for h in range(2):
                        pe.wait_ge(x2_lo_done, ST // 2 * (h + 1))
                        for t in range(2):
                            if h == 0:
                                pe.wait_ge(w_lo_done, N_FF0 + t + 1)
                                pe.wait_ge(mix_free, ST - 1 + t)
                            ff1_half(g, t, h)
                        if h == 0:
                            transpose_x2(ST - 1)
                for t in range(2 if first else 0, GROUP):
                    pe.wait_ge(w_lo_done, g * GROUP + (N_FF0 + t + 1))
                    pe.wait_ge(relu_done, g * GROUP + (t - 1))
                    for h in range(2):
                        ff1_half(g, t, h)
                for pair in range(ST // 2):
                    for k in range(GROUP):
                        if pair == 0:
                            pe.wait_ge(h_lo_done, g * GROUP + (k + 1))
                            pe.wait_ge(row_lo_done, g * GROUP + (KT + k + 1))
                        for t in (2 * pair, 2 * pair + 1):
                            ts = slice(t * P, (t + 1) * P)
                            if k == 0 and not (first and pair == 0):
                                pe.wait_ge(acc_done, g * ST + (t - 1))
                            for h in range(2):
                                cs = half_cols(h)
                                ins = product(ps[:, 4 + 2 * (t % 2) + h, :],
                                              ((h_hi[:, k, ts], h_lo[:, k, ts]), (w2_hi[:, k, cs], w2_lo[:, k, cs])),
                                              k == 0, k == GROUP - 1)
                            if k == GROUP - 1:
                                ins.then_inc(f2_done, 1)

            mlp_group(0, True)
            with pe.Fori(1, GROUPS) as g:
                mlp_group(g, False)


_INS = ['x', 'c', 'w_ada', 'b_ada', 'w_in', 'b_gate', 'w_pool', 'pool_scale', 'rel_bias', 'conv_w', 'conv_b',
        'conv_ln_g', 'conv_ln_b', 'w_br_pool', 'w_br_attn', 'w_br_conv', 'w_o', 'ln_mix_g', 'ln_mix_b',
        'w_ff1', 'b_ff1', 'w_ff2', 'b_ff2', 'ln_ff_g', 'ln_ff_b']
_OUTS = [((1, SEQ, D), 'float32')]


def kernel(**inputs):
    import numpy as _np
    import concourse.bacc as _bacc
    from concourse import mybir as _mybir
    from concourse.bass_utils import run_bass_kernel_spmd as _run

    nc = _bacc.Bacc("TRN2", target_bir_lowering=False, num_devices=1, dynamic_dma_scratch_size=1024)
    arrays, args = {}, []
    for name in _INS:
        a = _np.ascontiguousarray(inputs[name])
        arrays[f"in_{name}_dram"] = a
        args.append(nc.dram_tensor(f"in_{name}_dram", a.shape, _mybir.dt.from_np(a.dtype), kind="ExternalInput").ap())
    for i, (shape, dtype) in enumerate(_OUTS):
        dt = _mybir.dt.from_np(_np.dtype(dtype))
        args.append(nc.dram_tensor(f"out_{i}_dram", shape, dt, kind="ExternalOutput").ap())
    trunk_layer(nc, *args)
    r = _run(nc, [arrays], core_ids=[0])
    got = tuple(r.results[0][f"out_{i}_dram"] for i in range(len(_OUTS)))
    return got[0]
```

```python
import concourse.bass as bass
from concourse import mybir
from contextlib import ExitStack

SEQ = 1024
D = 1024
P = 128
KT = D // P
ST = SEQ // P
HALF = 512
D_POOL, D_ATTN, D_CONV = 256, 512, 256
CHUNK, N_PREV = 64, 8
HEADS, HEAD_DIM = 8, 64
PAIRS = HEADS // 2
TAPS = 31
REL_CLIP = 128
N_REL = 2 * REL_CLIP + 1
D_FF = 4 * D
BAND_BLOCKS = N_PREV * CHUNK // P + 1
BAND = BAND_BLOCKS * P
ALPHA = 2.0 ** 0.25
EPS = 1e-5
MASKED = -1e30
C_POOL, C_Q = 0, D_POOL
C_K, C_V = C_Q + D_ATTN, C_Q + 2 * D_ATTN
C_CONV = C_Q + 3 * D_ATTN
C_GATE = C_CONV + 2 * D_CONV
R_ADA, R_GATE, R_FF1 = 0, 48, 72
R_CONVB, R_CLNG, R_CLNB, R_PSC = 104, 106, 108, 110
ROWS_A, ROWS_C = 112, 2 * TAPS
N_P1 = 6
N_GATE0 = N_P1 + 3 * PAIRS
N_FF0 = N_GATE0 + 4 * KT
GROUP = 4
GROUPS = D_FF // (P * GROUP)
STEPS = 2 * ST
PROJ = 3 * 2 * KT * 3
PER_STEP = PROJ // STEPS
EARLY = 2
N_DIRECT = 2
MIX_STEP = 24


def trunk_layer(nc, x, c, w_ada, b_ada, w_in, b_gate, w_pool, pool_scale, rel_bias, conv_w, conv_b,
                conv_ln_g, conv_ln_b, w_br_pool, w_br_attn, w_br_conv, w_o, ln_mix_g, ln_mix_b,
                w_ff1, b_ff1, w_ff2, b_ff2, ln_ff_g, ln_ff_b, out):
    f32, f32r = mybir.dt.float32, mybir.dt.float32r
    ALU, ACT = mybir.AluOpType, mybir.ActivationFunctionType

    KB = 1024
    base = (nc.sbuf_base + 63) // 64 * 64
    top = nc.sbuf_usable_end

    def at(name, shape, dt, offset):
        size = 4
        for n in shape[1:]:
            size *= n
        assert base + offset + size <= top, (name, base + offset + size - top)
        return nc.alloc_sbuf_tensor_at(name, shape, dt, offset=base + offset)

    act_hi = at("act_hi", [P, KT, SEQ], f32r, 0)
    act_lo = at("act_lo", [P, KT, SEQ], f32r, 32 * KB)
    mid = at("mid", [P, KT, SEQ], f32, 64 * KB)
    w_raw = [at(f"w_raw{i}", [P, KT, P], f32, (96 + 4 * i) * KB) for i in range(2)]
    w_hi = [at(f"w_hi{i}", [P, KT, P], f32r, (104 + 4 * i) * KB) for i in range(2)]
    w_lo = [at(f"w_lo{i}", [P, KT, P], f32r, (112 + 4 * i) * KB) for i in range(2)]
    X = 120 * KB
    ada = [at(f"ada{i}", [P, 8, HALF], f32, X + 16 * i * KB) for i in range(3)]
    partial = [at(f"partial{i}", [P, HALF], f32, X + (48 + 2 * i) * KB) for i in range(2)]
    glu_gate = at("glu_gate", [P, SEQ], f32, X + 52 * KB)
    u_tmp = [at(f"u_tmp{i}", [P, SEQ], f32, X + (56 - 4 * i) * KB) for i in range(2)]
    rel_ext = at("rel_ext", [HEADS, 768], f32, X + 60 * KB)
    rows_a = at("rows_a", [ROWS_A, P], f32, X + 63 * KB)
    rows_c = at("rows_c", [ROWS_C, P], f32, X + 63 * KB + 512)
    q_hi = [at(f"q_hi{i}", [P, SEQ], f32r, X + 16 * i * KB) for i in range(2)]
    q_lo = [at(f"q_lo{i}", [P, SEQ], f32r, X + (16 * i + 4) * KB) for i in range(2)]
    k_hi = [at(f"k_hi{i}", [P, SEQ], f32r, X + (16 * i + 8) * KB) for i in range(2)]
    k_lo = [at(f"k_lo{i}", [P, SEQ], f32r, X + (16 * i + 12) * KB) for i in range(2)]
    v_hi = [at(f"v_hi{i}", [P, ST, P], f32r, X + (32 + 8 * i) * KB) for i in range(2)]
    v_lo = [at(f"v_lo{i}", [P, ST, P], f32r, X + (36 + 8 * i) * KB) for i in range(2)]
    bias_rev = [at(f"bias_rev{i}", [P, 2, BAND], f32, X + (48 + 5 * i) * KB) for i in range(2)]
    probs = [at(f"probs{i}", [P, BAND], f32, X + 58 * KB + 2560 * i) for i in range(2)]
    pt_hi = at("pt_hi", [P, BAND_BLOCKS, 2, P], f32r, X + 63 * KB)
    pt_lo = at("pt_lo", [P, BAND_BLOCKS, 2, P], f32r, X + 68 * KB)
    PAD = TAPS - 1
    h_pad = at("h_pad", [P, 2, PAD + SEQ], f32, X + 74 * KB)
    z_pool = at("z_pool", [P, 2, SEQ], f32, X + 82 * KB + 512)
    w_pool_bd = at("w_pool_bd", [P, 2, P], f32, X + 90 * KB + 512)
    sq = at("sq", [P, 2, SEQ], f32, X + 64 * KB)
    conv_sig = at("conv_sig", [P, SEQ], f32, X + 72 * KB)
    conv_rstd = at("conv_rstd", [P, SEQ], f32, X + 76 * KB)
    br_hi = at("br_hi", [P, KT, SEQ], f32r, X)
    br_lo = at("br_lo", [P, KT, SEQ], f32r, X + 32 * KB)
    gate_z = [at(f"gate_z{i}", [P, SEQ], f32, X + (82 + 4 * i) * KB + 512) for i in range(2)]
    gate = [at(f"gate{i}", [P, SEQ], f32, X + (72 + 4 * i) * KB) for i in range(3)]
    row_raw = [at(f"row_raw{i}", [P, D], f32, X + (64 + 4 * i) * KB) for i in range(2)]
    ln_g = at("ln_g", [P, D], f32, X + 72 * KB)
    ln_b = at("ln_b", [P, D], f32, X + 76 * KB)
    ff2_bias = at("ff2_bias", [P, D], f32, X + 80 * KB)
    tmp = [at(f"tmp{i}", [P, D], f32, X + (84 + 4 * i) * KB) for i in range(2)]
    mix_tmp = at("mix_tmp", [P, D], f32, 100 * KB)
    gate_mix = at("gate_mix", [P, D], f32, X + 92 * KB)
    gate_ff = at("gate_ff", [P, D], f32, X + 96 * KB)
    h_hi = at("h_hi", [P, GROUP, SEQ], f32r, X)
    h_lo = at("h_lo", [P, GROUP, SEQ], f32r, X + 16 * KB)
    w2_hi = at("w2_hi", [P, GROUP, D], f32r, X + 32 * KB)
    w2_lo = at("w2_lo", [P, GROUP, D], f32r, X + 48 * KB)
    small = X + 100 * KB

    def little(name, shape):
        nonlocal small
        t = at(name, shape, f32, small)
        n = 4
        for m in shape[1:]:
            n *= m
        small += (n + 31) // 32 * 32
        return t

    ident = little("ident", [P, P])
    cols = little("cols", [P, ROWS_A + ROWS_C])
    mod = little("mod", [P, 48])
    ones_row = at("ones_row", [P, P], f32, X + 91 * KB + 512)
    inv_count = little("inv_count", [P, 2, 16])
    c_raw = little("c_raw", [P, 8])
    c_sig = little("c_sig", [P, 8])
    c_act = little("c_act", [P, 8])
    neg_max = little("neg_max", [P, 2 * STEPS])
    row_sum = little("row_sum", [P, 2 * STEPS])
    inv_sum = little("inv_sum", [P, 2 * STEPS])
    bn = little("bn", [P, 12])
    mean_var = little("mean_var", [P, ST, 2])
    rstd = little("rstd", [P, ST])
    neg_mean = little("neg_mean", [P, ST])

    rel_dram = nc.dram_tensor("rel_scratch", (HEADS, 768), f32, kind="Internal").ap()

    x_rows = x[0].rearrange("(t p) d -> t p d", p=P)
    out_rows = out[0].rearrange("(t p) d -> t p d", p=P)
    ada_view = w_ada[0].rearrange("(p k) n -> p k n", k=8)
    win_view = w_in[0].rearrange("(k p) n -> p k n", p=P)
    wff1_view = w_ff1[0].rearrange("(k p) n -> p k n", p=P)
    brp_view = w_br_pool[0].rearrange("(k p) n -> p k n", p=P)
    bra_view = w_br_attn[0].rearrange("(k p) n -> p k n", p=P)
    brc_view = w_br_conv[0].rearrange("(k p) n -> p k n", p=P)

    def win_col(n):
        if n < 4:
            return C_CONV + ((n + 1) % 2) * D_CONV + (n // 2) * P
        if n < N_P1:
            return C_POOL + (n - 4) * P
        pair, part = divmod(n - N_P1, 3)
        if pair == PAIRS:
            return C_GATE + part * D
        return (C_Q, C_K, C_V)[part] + pair * P

    with ExitStack() as ctx:
        ps = ctx.enter_context(nc.psum_tensor("ps", [P, 8, HALF], f32))

        def sem(name):
            return ctx.enter_context(nc.semaphore(name))

        def banks(b, n=2):
            return ps[:, b:b + n, :].rearrange("p b n -> p (b n)")

        def f(ap):
            return ap.bitcast(f32)

        c_in, small_in = sem("c_in"), sem("small_in")
        x_in = [sem(f"x_in{i}") for i in range(ST)]
        ada_in, ada3_end_in = [sem(f"ada_in{i}") for i in range(3)], sem("ada3_end_in")
        w_arrived = [sem(f"w_arrived{i}") for i in range(2)]
        pool_w_in, rel_in, rel_stored = sem("pool_w_in"), sem("rel_in"), sem("rel_stored")
        bias_in = [sem(f"bias_in{i}") for i in range(2)]
        row_in = [sem(f"row_in{i}") for i in range(2)]
        res_in = [sem(f"res_in{i}") for i in range(ST)]
        ada_bias_in, ln_in, ln2_in, ff2b_in = sem("ada_bias_in"), sem("ln_in"), sem("ln2_in"), sem("ff2b_in")
        stored = [sem(f"stored{i}") for i in range(2)]
        consts_done, bd_zeroed = sem("consts_done"), sem("bd_zeroed")
        pool_step, dve_step = sem("pool_step"), sem("dve_step")
        c_sig_done, c_act_done, cols_t, cols_done, rel_done = (
            sem("c_sig_done"), sem("c_act_done"), sem("cols_t"), sem("cols_done"), sem("rel_done"))
        partial_done, reduced, mod_done, gates_done = (
            sem("partial_done"), sem("reduced"), sem("mod_done"), sem("gates_done"))
        var_done, std_done, norm_ready, normed = sem("var_done"), sem("std_done"), sem("norm_ready"), sem("normed")
        w_hi_done, w_lo_done = sem("w_hi_done"), sem("w_lo_done")
        row_hi_done, row_lo_done, row_scaled = sem("row_hi_done"), sem("row_lo_done"), sem("row_scaled")
        z_done, u_tmp_done, u_lo_done = sem("z_done"), sem("u_tmp_done"), sem("u_lo_done")
        glu_sig_done, glu_done, zp_done, pooled_done = (
            sem("glu_sig_done"), sem("glu_done"), sem("zp_done"), sem("pooled_done"))
        h_done, half_hi, h_free = sem("h_done"), sem("half_hi"), [sem(f"h_free{i}") for i in range(2)]
        scores_done, biased, exp_done, probs_done = (
            sem("scores_done"), sem("biased"), sem("exp_done"), sem("probs_done"))
        pt_done, pt_hi_done, pt_lo_done = sem("pt_done"), sem("pt_hi_done"), sem("pt_lo_done")
        pv_done, o_copied, bias_ready = sem("pv_done"), sem("o_copied"), sem("bias_ready")
        pm_done, pm_scaled, tap_done = sem("pm_done"), sem("pm_scaled"), sem("tap_done")
        cmean_done, centred, squared, cvar_done, cvar_read = (
            sem("cmean_done"), sem("centred"), sem("squared"), sem("cvar_done"), sem("cvar_read"))
        cstd_done, cnormed, conv_sig_done, conv_done = (
            sem("cstd_done"), sem("cnormed"), sem("conv_sig_done"), sem("conv_done"))
        br_hi_done, br_lo_done = sem("br_hi_done"), sem("br_lo_done")
        g_done, sig_done, y_done, y_used, merged_step = (
            sem("g_done"), sem("sig_done"), sem("y_done"), sem("y_used"), sem("merged_step"))
        mg_hi_done, mg_lo_done = sem("mg_hi_done"), sem("mg_lo_done")
        mix_done, mix_free, res_done, x1_done = sem("mix_done"), sem("mix_free"), sem("res_done"), sem("x1_done")
        x2t_done, x2_tmp_done, x2_hi_done, x2_lo_done = (
            sem("x2t_done"), sem("x2_tmp_done"), sem("x2_hi_done"), sem("x2_lo_done"))
        ff2b_scaled, x1_scaled = sem("ff2b_scaled"), sem("x1_scaled")
        f1_done, relu_done, sq_done, h_hi_done, h_lo_done = (
            sem("f1_done"), sem("relu_done"), sem("sq_done"), sem("h_hi_done"), sem("h_lo_done"))
        f2_done, acc_done, y_ready = sem("f2_done"), sem("acc_done"), sem("y_ready")

        block = ctx.enter_context(nc.Block())

        def block_used(n):
            if n < N_P1:
                return z_done, 8 + n + 1
            pair, part = divmod(n - N_P1, 3)
            return h_done, 8 * pair + 2 * part + 2

        W0_GATES = 16 * N_GATE0 // 2
        W0_FF = [W0_GATES + 32 * KT, W0_GATES + 64 * KT]

        def blocks_of(t):
            return min(t + 1, BAND_BLOCKS)

        def score_cols(nb):
            if nb < BAND_BLOCKS:
                return banks(4)[:, 0:nb * P]
            return ps[:, 4:6, 0:BAND // 2]

        def like_scores(ap, nb):
            return ap if nb < BAND_BLOCKS else ap.rearrange("p (b n) -> p b n", b=2)

        @block.sync
        def _(sp):
            def load_block(n):
                if n >= 2:
                    sp.wait_ge(w_lo_done, n - 1)
                c0 = win_col(n)
                sp.dma_start(w_raw[n % 2][:, :, :], win_view[:, :, c0:c0 + P]).then_inc(w_arrived[n % 2], 16)

            def load_ada(i):
                if 3 <= i < 3 + N_DIRECT:
                    sp.wait_ge(reduced, i - 2)
                elif i >= 3:
                    sp.wait_ge(partial_done, i - 2 - N_DIRECT)
                cs = slice(i * HALF, (i + 1) * HALF)
                if i == 3:
                    sp.dma_start(ada[0][:, 0:4, :], ada_view[:, 0:4, cs]).then_inc(ada_in[0], 16)
                    sp.dma_start(ada[0][:, 4:8, :], ada_view[:, 4:8, cs]).then_inc(ada3_end_in, 16)
                else:
                    sp.dma_start(ada[i % 3][:, :, :], ada_view[:, :, cs]).then_inc(ada_in[i % 3], 16)

            sp.dma_start(c_raw[:, :], c[0].rearrange("(p k) -> p k", k=8)).then_inc(c_in, 16)
            load_ada(0)
            for i in range(ST // 2):
                sp.dma_start(mid[:, i, :], x_rows[i]).then_inc(x_in[i], 16)
            for row, n, src in ((R_ADA, 48, b_ada), (R_GATE, 24, b_gate), (R_FF1, 32, b_ff1), (R_CONVB, 2, conv_b),
                                (R_CLNG, 2, conv_ln_g), (R_CLNB, 2, conv_ln_b), (R_PSC, 2, pool_scale)):
                sp.dma_start(rows_a[row:row + n, :], src[0].rearrange("(r p) -> r p", p=P)).then_inc(small_in, 16)
            sp.dma_start(rows_c[:, :], conv_w[0].rearrange("t (c p) -> (t c) p", p=P)).then_inc(small_in, 16)
            load_ada(1)
            for i in range(ST // 2, ST):
                sp.dma_start(mid[:, i, :], x_rows[i]).then_inc(x_in[i], 16)
            load_ada(2)
            load_ada(3)
            load_block(0)
            load_block(1)
            sp.dma_start(rel_ext[:, 0:2 * REL_CLIP], rel_bias[0][:, 1:N_REL]).then_inc(rel_in, 16)
            sp.wait_ge(bd_zeroed, 1)
            for g in range(4):
                lo = 64 * (g % 2)
                sp.dma_start(w_pool_bd[lo:lo + 64, g // 2, lo:lo + 64], w_pool[0, g]).then_inc(pool_w_in, 16)
            for t, col in ((gate_mix, 2 * D), (gate_ff, 5 * D)):
                sp.dma_start(t[:, :], b_ada[0:1, col:col + D].partition_broadcast(P)).then_inc(ada_bias_in, 16)
            sp.wait_ge(rel_done, 1)
            sp.dma_start(rel_dram, rel_ext[:, :]).then_inc(rel_stored, 16)
            load_ada(4)
            load_ada(5)
            load_block(2)
            load_ada(6)
            load_ada(7)
            load_block(3)
            load_ada(8)
            load_ada(9)
            load_block(4)
            load_ada(10)
            load_block(5)
            load_ada(11)

            def load_bias(pair):
                if pair >= 2:
                    sp.wait_ge(biased, STEPS * (pair - 1))
                for h in range(2):
                    head = 2 * pair + h
                    src = bass.AP(rel_dram.tensor, head * 768, [[1, P], [1, BAND]])
                    sp.dma_start(bias_rev[pair % 2][:, h, :], src).then_inc(bias_in[pair % 2], 16)

            load_block(6)
            sp.wait_ge(reduced, 12)
            sp.wait_ge(glu_done, 2)
            sp.wait_ge(u_lo_done, KT)
            sp.wait_ge(rel_stored, 16)
            load_bias(0)
            load_bias(1)
            for n in range(7, N_GATE0 + 3):
                if n == N_P1 + 10:
                    load_bias(2)
                if n == N_GATE0 + 1:
                    load_bias(3)
                load_block(n)

            def load_branches(slot, col):
                for k0, k1, view in ((0, 2, brp_view), (2, 6, bra_view), (6, 8, brc_view)):
                    sp.dma_start(w_raw[slot][:, k0:k1, :], view[:, :, bass.ds(col, P)]).then_inc(w_arrived[slot], 16)

            sp.wait_ge(w_lo_done, N_GATE0 + 2)
            load_branches((N_GATE0 + 3) % 2, 0)

            with sp.Fori(2, KT + 1) as j_next:
                j = j_next - 1
                first = [sp.snap(j * P + (C_GATE + b * D)) for b in range(3)]
                cut = [sp.snap(j * 4 + (N_GATE0 + b - 1)) for b in range(4)]
                for b in range(4):
                    sp.wait_ge(w_lo_done, cut[b])
                    slot = (N_GATE0 + b) % 2
                    if b < 3:
                        sp.dma_start(w_raw[slot][:, :, :], win_view[:, :, bass.ds(first[b], P)])\
                            .then_inc(w_arrived[slot], 16)
                    else:
                        load_branches(slot, j_next * P - P)

            def load_row(q, src):
                sp.dma_start(row_raw[q % 2][:, :], src).then_inc(row_in[q % 2], 16)

            sp.wait_ge(conv_done, 2)
            for q in range(2):
                load_row(q, w_o[0, q * P:(q + 1) * P, :])
            for n in range(2):
                sp.wait_ge(w_lo_done, N_FF0 + n - 1)
                sp.dma_start(w_raw[n][:, :, :], wff1_view[:, :, n * P:(n + 1) * P]).then_inc(w_arrived[n], 16)
            sp.wait_ge(y_used, 3 * KT)
            for q in range(2, KT):
                sp.wait_ge(row_lo_done, q - 1)
                load_row(q, w_o[0, q * P:(q + 1) * P, :])
                if q == 2:
                    sp.dma_start(ln_g[:, :], ln_mix_g[0:1, :].partition_broadcast(P)).then_inc(ln_in, 16)
                    sp.dma_start(ln_b[:, :], ln_mix_b[0:1, :].partition_broadcast(P)).then_inc(ln_in, 16)
                    sp.dma_start(ff2_bias[:, :], b_ff2[0:1, :].partition_broadcast(P)).then_inc(ff2b_in, 16)
                if q >= 4:
                    sp.wait_ge(mg_lo_done, q - 3)
                    sp.dma_start(mid[:, q - 4, :], x_rows[q - 4]).then_inc(res_in[q - 4], 16)
            for i in range(4, ST):
                sp.wait_ge(mg_lo_done, i + 1)
                sp.dma_start(mid[:, i, :], x_rows[i]).then_inc(res_in[i], 16)

            def ff_loads(g, last):
                first = [g * (GROUP * P) + t * P for t in range(GROUP + 2)]
                rows_cut = [g * GROUP + (KT + t - 1) for t in range(GROUP)]
                block_cut = [g * GROUP + (N_FF0 + t + 1) for t in range(GROUP)]
                if not last:
                    first, rows_cut, block_cut = ([sp.snap(v) for v in vs] for vs in (first, rows_cut, block_cut))
                for t in range(GROUP):
                    sp.wait_ge(row_lo_done, rows_cut[t])
                    sp.dma_start(row_raw[t % 2][:, :], w_ff2[0, bass.ds(first[t], P), :]).then_inc(row_in[t % 2], 16)
                    if not (last and t >= 2):
                        sp.wait_ge(w_lo_done, block_cut[t])
                        sp.dma_start(w_raw[t % 2][:, :, :], wff1_view[:, :, bass.ds(first[t + 2], P)])\
                            .then_inc(w_arrived[t % 2], 16)

            sp.wait_ge(x1_done, ST)
            with sp.Fori(0, GROUPS - 1) as g:
                ff_loads(g, False)
            ff_loads(GROUPS - 1, True)
            sp.dma_start(ln_g[:, :], ln_ff_g[0:1, :].partition_broadcast(P)).then_inc(ln2_in, 16)
            sp.dma_start(ln_b[:, :], ln_ff_b[0:1, :].partition_broadcast(P)).then_inc(ln2_in, 16)
            for t in range(ST):
                sp.wait_ge(y_ready, t + 1)
                sp.dma_start(out_rows[t], tmp[t % 2][:, :]).then_inc(stored[t % 2], 16)
            for b in range(2):
                sp.wait_ge(stored[b], 16 * ST // 2)

        def arrived(n):
            if n < N_GATE0:
                return 16 * (n // 2 + 1)
            j, b = divmod(n - N_GATE0, 4)
            return gate_arrived(j, b)

        def gate_arrived(j, b):
            return (j * 32 + (W0_GATES + (16, 16, 32, 64)[b])) if b % 2 == 0 else (j * 64 + (W0_GATES + (16, 16, 32, 64)[b]))

        def ff_arrived(g, t):
            return g * (16 * GROUP // 2) + (W0_FF[t % 2] + 16 * (t // 2 + 1))

        @block.gpsimd
        def _(pool):
            steps = [0]

            def link(ins):
                steps[0] += 1
                ins.then_inc(pool_step, 1)
                pool.wait_ge(pool_step, steps[0])

            link(nc.gpsimd.memset(ident[:, :], 0.0))
            nc.gpsimd.affine_select(out=ident[:, :], in_=ident[:, :], compare_op=ALU.not_equal, fill=1.0, base=0,
                                    pattern=[[-1, P]], channel_multiplier=1).then_inc(consts_done, 1)
            pool.wait_ge(consts_done, 1)
            nc.gpsimd.memset(ones_row[:, :], 1.0).then_inc(consts_done, 1)
            pool.wait_ge(consts_done, 2)
            nc.gpsimd.memset(w_pool_bd[:, :, :], 0.0).then_inc(bd_zeroed, 1)
            pool.wait_ge(bd_zeroed, 1)
            nc.gpsimd.memset(h_pad[:, :, 0:PAD], 0.0).then_inc(consts_done, 1)
            pool.wait_ge(consts_done, 3)
            for g, window in enumerate((2, 4, 8, 16)):
                rows = slice(64 * (g % 2), 64 * (g % 2) + 64)
                for t in range(window - 1):
                    link(nc.gpsimd.memset(inv_count[rows, g // 2, t:t + 1], 1.0 / (t + 1)))
                link(nc.gpsimd.memset(inv_count[rows, g // 2, window - 1:16], 1.0 / window))

            def shifted_sum(dst, src, shift, rows=slice(0, P)):
                link(nc.gpsimd.tensor_copy(dst[rows, 0:shift], src[rows, 0:shift]))
                link(nc.gpsimd.tensor_tensor(dst[rows, shift:SEQ], src[rows, shift:SEQ], src[rows, 0:SEQ - shift],
                                             ALU.add))

            def window_mean(c, half, total):
                rows = slice(64 * half, 64 * half + 64)
                first = total[rows, 0:16]
                link(nc.gpsimd.tensor_tensor(first, first, inv_count[rows, c, :], ALU.mult))
                link(nc.gpsimd.tensor_scalar(total[rows, 16:SEQ], total[rows, 16:SEQ], inv_count[rows, c, 15:16], None,
                                             ALU.mult))
                z = z_pool[rows, c, :]
                ins = nc.gpsimd.tensor_tensor(z, total[rows, :], z, ALU.subtract)
                if half == 1:
                    ins.then_inc(pooled_done, 1)
                    pool.wait_ge(pooled_done, c + 1)
                else:
                    link(ins)

            def mask_bias(pair):
                pool.wait_ge(bias_in[pair % 2], 32 * (pair // 2 + 1))
                link(nc.gpsimd.memset(bias_rev[pair % 2][0:64, :, 0:CHUNK], MASKED))
                nc.gpsimd.memset(bias_rev[pair % 2][64:P, :, BAND - CHUNK:BAND], MASKED).then_inc(bias_ready, 1)
                pool.wait_ge(bias_ready, pair + 1)

            pool.wait_ge(z_done, KT)
            a, b = mid[:, 3, :], mid[:, 4, :]
            pool.wait_ge(zp_done, 1)
            z = z_pool[:, 0, :]
            shifted_sum(a, z, 1)
            shifted_sum(b, a, 2, slice(64, P))
            window_mean(0, 0, a)
            window_mean(0, 1, b)
            mask_bias(0)
            pool.wait_ge(zp_done, 2)
            z = z_pool[:, 1, :]
            shifted_sum(a, z, 1)
            shifted_sum(b, a, 2)
            shifted_sum(a, b, 4)
            shifted_sum(b, a, 8, slice(64, P))
            window_mean(1, 0, a)
            window_mean(1, 1, b)
            for pair in range(1, PAIRS):
                mask_bias(pair)
            pool.wait_ge(gates_done, 4)
            pool.wait_ge(ff2b_in, 16)
            nc.gpsimd.tensor_tensor(ff2_bias[:, :], ff2_bias[:, :], gate_ff[:, :], ALU.mult).then_inc(ff2b_scaled, 1)
            pool.wait_ge(ff2b_scaled, 1)
            for t in range(ST):
                pool.wait_ge(x1_scaled, t + 1)
                nc.gpsimd.tensor_tensor(mid[:, t, :], mid[:, t, :], ff2_bias[:, :], ALU.add).then_inc(res_done, 1)

        half_after = {}
        for r in range(6):
            half_after[-(-24 * (r + 1) // PER_STEP) - 1] = r
        early_per_step = EARLY * 48 // STEPS
        early_after = {24 * (r + 1) // early_per_step - 1: r for r in range(2 * EARLY)}

        def half_of(pair, i):
            if pair < PAIRS - 1 and i in half_after:
                return pair + 1, half_after[i]
            if pair == PAIRS - 1 and i in early_after:
                return PAIRS, early_after[i]
            return None

        def pool_mix_unit(a):
            u = (a - MIX_STEP) // 2
            return u if a >= MIX_STEP and a % 2 == 0 and u < 4 else None

        @block.scalar
        def _(act):
            def copy(out, in_, **kw):
                return nc.scalar.activation(out, in_, ACT.Copy, **kw)

            def cut_hi(n):
                act.wait_ge(w_arrived[n % 2], arrived(n))
                if n >= 2:
                    act.wait_ge(*block_used(n - 2))
                copy(w_hi[n % 2][:, :, :], w_raw[n % 2][:, :, :]).then_inc(w_hi_done, 1)

            def take_root(count, t):
                act.wait_ge(var_done, count + 1)
                nc.scalar.activation(rstd[:, t:t + 1], rstd[:, t:t + 1], ACT.Sqrt).then_inc(std_done, 1)

            def norm(count, t, tile):
                act.wait_ge(norm_ready, count + 1)
                nc.scalar.activation(tile, mid[:, t, :], ACT.Identity, bias=neg_mean[:, t:t + 1],
                                     scale=rstd[:, t:t + 1]).then_inc(normed, 1)

            act.wait_ge(c_in, 16)
            nc.scalar.activation(c_sig[:, :], c_raw[:, :], ACT.Sigmoid).then_inc(c_sig_done, 1)
            for i in range(ST + 1):
                if i < ST:
                    take_root(i, i)
                if i >= 1:
                    norm(i - 1, i - 1, mid[:, i - 1, :])
            cut_hi(0)
            cut_hi(1)
            for k in range(KT):
                if k == 0:
                    act.wait_ge(mod_done, 1)
                if k >= 2:
                    act.wait_ge(u_lo_done, k - 1)
                act.wait_ge(z_done, k + 1)
                nc.scalar.activation(u_tmp[k % 2][:, :], banks(2 * (k % 2)), ACT.Identity, bias=mod[:, k:k + 1],
                                     scale=mod[:, KT + k:KT + k + 1]).then_inc(u_tmp_done, 1)
            for n in range(N_P1):
                act.wait_ge(z_done, KT + n + 1)
                src = banks(2 * (n % 2))
                if n in (0, 2):
                    if n == 0:
                        act.wait_ge(u_lo_done, KT)
                    else:
                        act.wait_ge(glu_done, 1)
                    nc.scalar.activation(glu_gate[:, :], src, ACT.Sigmoid).then_inc(glu_sig_done, 1)
                if n >= 4:
                    copy(z_pool[:, n - 4, :], src).then_inc(zp_done, 1)
                cut_hi(n + 2)

            def take_half(pair, r):
                hz = 8 * pair + r
                part, half = divmod(r, 2)
                cs = slice(half * HALF, (half + 1) * HALF)
                src = ps[:, r % 2, :]
                act.wait_ge(h_done, hz + 1)
                if pair == PAIRS:
                    act.wait_ge(pm_scaled, 4)
                    copy(gate_z[part][:, cs], src).then_inc(h_free[r % 2], 1)
                elif part == 0:
                    if pair >= 2:
                        act.wait_ge(scores_done, STEPS * (pair - 1))
                    elif pair == 0:
                        act.wait_ge(partial_done, 12 - N_DIRECT)
                    copy(q_hi[pair % 2][:, cs], src, scale=HEAD_DIM ** -0.5).then_inc(half_hi, 1)
                elif part == 1:
                    copy(k_hi[pair % 2][:, cs], src).then_inc(half_hi, 1)
                elif part == 2:
                    copy(mid[:, 5, cs], src).then_inc(h_free[r % 2], 1)
                else:
                    if pair >= 2:
                        act.wait_ge(pv_done, ST * (pair - 1))
                    copy(v_hi[pair % 2][:, 4 * half:4 * half + 4, :], src.rearrange("p (t d) -> p t d", d=P))\
                        .then_inc(half_hi, 1)
                if r in (1, 3, 5):
                    cut_hi(N_P1 + 3 * pair + part + 2)

            for r in range(6):
                take_half(0, r)
            N_STEPS = PAIRS * STEPS
            for a in range(N_STEPS + 2):
                pair, i = divmod(a, STEPS)
                if a < N_STEPS:
                    col, width = a % (2 * STEPS), P * blocks_of(i // 2)
                    act.wait_ge(biased, a + 1)
                    nc.scalar.activation(probs[a % 2][:, 0:width], probs[a % 2][:, 0:width], ACT.Exp,
                                         bias=neg_max[:, col:col + 1], scale=-1.0,
                                         accum_out=row_sum[:, col:col + 1]).then_inc(exp_done, 1)
                if a < N_STEPS and i == 0:
                    take_half(pair, 6)
                    take_half(pair, 7)
                if a >= 3 and a % 2 == 1:
                    tile = (a - 3) // 2
                    act.wait_ge(pv_done, tile + 1)
                    if tile == ST:
                        act.wait_ge(pooled_done, 2)
                    ts = slice(tile % ST * P, (tile % ST + 1) * P)
                    for h in range(2):
                        rows = slice(h * HEAD_DIM, (h + 1) * HEAD_DIM)
                        copy(mid[rows, 2 + tile // ST, ts], ps[rows, 2, h * P:(h + 1) * P]).then_inc(o_copied, 1)
                if 1 <= a <= N_STEPS:
                    b = a - 1
                    nb = blocks_of(b % STEPS // 2)
                    act.wait_ge(pt_done, b + 1)
                    if b >= 2:
                        act.wait_ge(pv_done, b // 2)
                    copy(pt_hi[:, 0:nb, b % 2, :], banks(6)[:, 0:nb * P].rearrange("p (b q) -> p b q", q=P))\
                        .then_inc(pt_hi_done, 1)
                if pool_mix_unit(a) is not None:
                    t, half = divmod(pool_mix_unit(a), 2)
                    act.wait_ge(pm_done, 2 * t + half + 1)
                    copy(mid[:, t, half * HALF:(half + 1) * HALF], ps[:, 3, :],
                         scale=cols[:, R_PSC + t:R_PSC + t + 1]).then_inc(pm_scaled, 1)
                if half_of(pair, i):
                    take_half(*half_of(pair, i))

            def cut_branch_hi(k):
                copy(br_hi[:, k, :], mid[:, k, :]).then_inc(br_hi_done, 1)

            act.wait_ge(o_copied, N_STEPS)
            act.wait_ge(pt_lo_done, N_STEPS)
            for t in range(2):
                act.wait_ge(centred, t + 1)
                nc.scalar.activation(sq[:, t, :], mid[:, 6 + t, :], ACT.Square).then_inc(squared, 1)
            cut_branch_hi(0)
            cut_branch_hi(1)
            act.wait_ge(cvar_read, 1)
            nc.scalar.activation(conv_rstd[:, :], conv_rstd[:, :], ACT.Sqrt).then_inc(cstd_done, 1)
            for k in range(2, 6):
                cut_branch_hi(k)
            for t in range(2):
                act.wait_ge(cnormed, t + 1)
                if t == 1:
                    act.wait_ge(conv_done, 1)
                nc.scalar.activation(conv_sig[:, :], mid[:, 6 + t, :], ACT.Sigmoid,
                                     bias=cols[:, R_CLNB + t:R_CLNB + t + 1],
                                     scale=cols[:, R_CLNG + t:R_CLNG + t + 1]).then_inc(conv_sig_done, 1)
            act.wait_ge(conv_done, 2)
            cut_branch_hi(6)
            cut_branch_hi(7)

            def gate_sigmoid(j, b, src):
                nc.scalar.activation(gate[b][:, :], src, ACT.Sigmoid,
                                     bias=cols[:, bass.ds(j + (R_GATE + 8 * b), 1)]).then_inc(sig_done, 1)

            def cut_gate_hi(j, b):
                act.wait_ge(w_arrived[b % 2], gate_arrived(j, b + 2) if b < 2 else gate_arrived(j + 1, b - 2))
                copy(w_hi[b % 2][:, :, :], w_raw[b % 2][:, :, :]).then_inc(w_hi_done, 1)

            for b in range(EARLY):
                gate_sigmoid(0, b, gate_z[b][:, :])
            act.wait_ge(g_done, 1)
            act.wait_ge(sig_done, EARLY)
            gate_sigmoid(0, 2, banks(0))
            cut_gate_hi(0, 2)
            act.wait_ge(y_done, 3)
            cut_gate_hi(0, 3)
            with act.Fori(1, KT) as j:
                for b in range(4):
                    if b < 3:
                        act.wait_ge(g_done, j * 3 + (b + 1 - EARLY))
                        if b == 0:
                            act.wait_ge(w_lo_done, j * 4 + (N_GATE0 + 2))
                        gate_sigmoid(j, b, banks(2 * (b % 2)))
                    else:
                        act.wait_ge(y_done, j * 3 + 3)
                    cut_gate_hi(j, b)

            act.wait_ge(g_done, 3 * KT - EARLY)
            act.wait_ge(y_done, 3 * KT)
            for k in range(KT):
                act.wait_ge(merged_step, 3 * (k + 1))
                copy(act_hi[:, k, :], mid[:, k, :]).then_inc(mg_hi_done, 1)
                act.wait_ge(row_in[k % 2], 16 * (k // 2 + 1))
                copy(br_hi[:, k, :], row_raw[k % 2][:, :]).then_inc(row_hi_done, 1)

            for t in range(ST + 2):
                if t < ST:
                    take_root(ST + 2 * t, t)
                if 1 <= t <= ST:
                    q = t - 1
                    if q >= 2:
                        act.wait_ge(x2_lo_done, q - 1)
                    norm(ST + 2 * q + 1, q, tmp[q % 2][:, :])
                if t < ST:
                    norm(ST + 2 * t, t, mix_tmp[:, :])
                if 1 <= t <= ST:
                    copy(mid[:, t - 1, :], mid[:, t - 1, :], scale=ALPHA).then_inc(x1_scaled, 1)
                if t >= 2:
                    q = t - 2
                    act.wait_ge(x2t_done, q + 1)
                    for k in range(KT):
                        ins = nc.scalar.activation(tmp[q % 2][:, k * P:(k + 1) * P],
                                                   banks(4 + 2 * (q % 2))[:, k * P:(k + 1) * P], ACT.Identity,
                                                   bias=mod[:, 24 + k:25 + k], scale=mod[:, 32 + k:33 + k])
                    ins.then_inc(x2_tmp_done, 1)
                    act.wait_ge(x2_tmp_done, q + 1)
                    copy(act_hi[:, :, q * P:(q + 1) * P], tmp[q % 2][:, :].rearrange("p (k s) -> p k s", s=P))\
                        .then_inc(x2_hi_done, 1)
                if t < ST:
                    take_root(ST + 2 * t + 1, t)

            def mlp_group(g, last):
                for t in range(GROUP):
                    act.wait_ge(f1_done, g * GROUP + (t + 1))
                    if t >= 2:
                        act.wait_ge(h_lo_done, g * GROUP + (t - 1))
                    nc.scalar.activation(tmp[t % 2][:, :], banks(2 * (t % 2)), ACT.Relu,
                                         bias=cols[:, bass.ds(g * GROUP + (R_FF1 + t), 1)]).then_inc(relu_done, 1)
                    act.wait_ge(relu_done, g * GROUP + (t + 1))
                    nc.scalar.activation(tmp[t % 2][:, :], tmp[t % 2][:, :], ACT.Square).then_inc(sq_done, 1)
                    act.wait_ge(sq_done, g * GROUP + (t + 1))
                    copy(h_hi[:, t, :], tmp[t % 2][:, :]).then_inc(h_hi_done, 1)
                    if not (last and t >= 2):
                        act.wait_ge(w_arrived[t % 2], ff_arrived(g, t + 2))
                        copy(w_hi[t % 2][:, :, :], w_raw[t % 2][:, :, :]).then_inc(w_hi_done, 1)
                    act.wait_ge(row_scaled, g * GROUP + (t + 1))
                    copy(w2_hi[:, t, :], row_raw[t % 2][:, :]).then_inc(row_hi_done, 1)

            with act.Fori(0, GROUPS - 1) as g:
                mlp_group(g, False)
            mlp_group(GROUPS - 1, True)
            for t in range(ST):
                if t >= 2:
                    act.wait_ge(stored[t % 2], 16 * (t // 2))
                take_root(3 * ST + t, t)
                norm(3 * ST + t, t, tmp[t % 2][:, :])

        @block.vector
        def _(dve):
            steps = [0]

            def link(ins, offset=0):
                steps[0] += 1
                ins.then_inc(dve_step, 1)
                dve.wait_ge(dve_step, offset + steps[0])

            def cut_lo(n):
                dve.wait_ge(w_hi_done, n + 1)
                nc.vector.tensor_tensor(w_lo[n % 2][:, :, :], w_raw[n % 2][:, :, :], f(w_hi[n % 2][:, :, :]),
                                        ALU.subtract).then_inc(w_lo_done, 1)

            def stats(src, t):
                for half in range(2):
                    ins = nc.vector.bn_stats(bn[:, 6 * half:6 * half + 6], src[:, half * HALF:(half + 1) * HALF])
                link(ins)
                link(nc.vector.bn_aggr(mean_var[:, t, :], bn[:, :]))
                nc.vector.tensor_scalar_add(rstd[:, t:t + 1], mean_var[:, t, 1:2], EPS).then_inc(var_done, 1)

            def scale_bias(count, t):
                dve.wait_ge(std_done, count + 1)
                link(nc.vector.reciprocal(rstd[:, t:t + 1], rstd[:, t:t + 1]))
                nc.vector.scalar_tensor_tensor(out=neg_mean[:, t:t + 1], in0=mean_var[:, t, 0:1], scalar=-1.0,
                                               in1=rstd[:, t:t + 1], op0=ALU.mult, op1=ALU.mult)\
                    .then_inc(norm_ready, 1)

            dve.wait_ge(c_sig_done, 1)
            nc.vector.tensor_tensor(c_act[:, :], c_raw[:, :], c_sig[:, :], ALU.mult).then_inc(c_act_done, 1)
            dve.wait_ge(c_act_done, 1)
            for i in range(ST):
                dve.wait_ge(x_in[i], 16)
                stats(mid[:, i, :], i)
                if i >= 1:
                    scale_bias(i - 1, i - 1)
            scale_bias(ST - 1, ST - 1)

            def ada_chunk(i):
                dve.wait_ge(ada_in[i % 3], 16 * (i // 3 + 1))
                if i >= 2 + N_DIRECT:
                    dve.wait_ge(reduced, i - 1)
                dst, src = partial[i % 2][:, :], ada[i % 3]
                link(nc.vector.tensor_scalar(dst, src[:, 0, :], c_act[:, 0:1], None, ALU.mult))
                for k in range(1, 8):
                    if i == 3 and k == 4:
                        dve.wait_ge(ada3_end_in, 16)
                    ins = nc.vector.scalar_tensor_tensor(out=dst, in0=src[:, k, :], scalar=c_act[:, k:k + 1], in1=dst,
                                                         op0=ALU.mult, op1=ALU.add)
                    if k < 7:
                        link(ins)
                ins.then_inc(partial_done, 1)

            def gate_chunk(i):
                dve.wait_ge(reduced, i + 1)
                dve.wait_ge(ada_bias_in, 32)
                half = slice(i % 2 * HALF, i % 2 * HALF + HALF)
                dst = (gate_mix if i < 6 else gate_ff)[:, half]
                nc.vector.tensor_tensor(dst, ps[:, 4 + i % 2, :], dst, ALU.add).then_inc(gates_done, 1)

            def mod_columns(c0, bank):
                link(nc.vector.tensor_tensor(mod[:, c0:c0 + 16], ps[:, bank, 0:16], cols[:, c0:c0 + 16], ALU.add))
                nc.vector.tensor_scalar_add(mod[:, c0 + 8:c0 + 16], mod[:, c0 + 8:c0 + 16], 1.0).then_inc(mod_done, 1)

            dve.wait_ge(cols_t, 2)
            nc.vector.tensor_copy(cols[:, 0:ROWS_A], ps[:, 4, 0:ROWS_A])
            nc.vector.tensor_copy(cols[:, ROWS_A:ROWS_A + ROWS_C], ps[:, 5, 0:ROWS_C]).then_inc(cols_done, 1)
            for i in range(N_DIRECT, 4):
                ada_chunk(i)
            dve.wait_ge(rel_in, 16)
            nc.vector.tensor_copy(rel_ext[:, 2 * REL_CLIP:768],
                                  rel_ext[:, 2 * REL_CLIP - 1:2 * REL_CLIP].to_broadcast([HEADS, 768 - 2 * REL_CLIP]))\
                .then_inc(rel_done, 1)
            dve.wait_ge(cols_done, 1)
            cut_lo(0)
            cut_lo(1)
            dve.wait_ge(reduced, 4)
            mod_columns(0, 6)
            for k in range(KT):
                dve.wait_ge(u_tmp_done, k + 1)
                link(nc.vector.tensor_copy(act_hi[:, k, :], u_tmp[k % 2][:, :]))
                nc.vector.tensor_tensor(act_lo[:, k, :], u_tmp[k % 2][:, :], f(act_hi[:, k, :]), ALU.subtract)\
                    .then_inc(u_lo_done, 1)
            chunks_at = {0: (4,), 1: (5, 6), 2: (7,), 3: (8, 9), 4: (10,), 5: (11,)}
            for n in range(N_P1):
                for i in chunks_at[n]:
                    ada_chunk(i)
                if n in (1, 3):
                    t = n // 2
                    dve.wait_ge(z_done, KT + n + 1)
                    dve.wait_ge(glu_sig_done, t + 1)
                    dve.wait_ge(consts_done, 3)
                    nc.vector.tensor_tensor(h_pad[:, t, PAD:PAD + SEQ], banks(2), glu_gate[:, :], ALU.mult)\
                        .then_inc(glu_done, 1)
                cut_lo(n + 2)
                for i in chunks_at[n]:
                    if i in (4, 5, 10, 11):
                        gate_chunk(i)
            dve.wait_ge(reduced, 10)
            mod_columns(24, 7)

            def take_half_lo(pair, r):
                part, half = divmod(r, 2)
                cs = slice(half * HALF, (half + 1) * HALF)
                src, s = ps[:, r % 2, :], pair % 2
                if part != 2 and pair < PAIRS:
                    dve.wait_ge(half_hi, 6 * pair + (r if r < 4 else r - 2) + 1)
                if pair == PAIRS:
                    pass
                elif part == 0:
                    nc.vector.scalar_tensor_tensor(out=q_lo[s][:, cs], in0=src, scalar=HEAD_DIM ** -0.5,
                                                   in1=f(q_hi[s][:, cs]), op0=ALU.mult, op1=ALU.subtract)\
                        .then_inc(h_free[r % 2], 1)
                elif part == 1:
                    nc.vector.tensor_tensor(k_lo[s][:, cs], src, f(k_hi[s][:, cs]), ALU.subtract)\
                        .then_inc(h_free[r % 2], 1)
                elif part == 3:
                    ts = slice(4 * half, 4 * half + 4)
                    nc.vector.tensor_tensor(v_lo[s][:, ts, :], src.rearrange("p (t d) -> p t d", d=P),
                                            f(v_hi[s][:, ts, :]), ALU.subtract).then_inc(h_free[r % 2], 1)
                if r in (1, 3, 5):
                    cut_lo(N_P1 + 3 * pair + part + 2)

            def conv_tap(n):
                t, tap = divmod(n, TAPS)
                w = cols[:, ROWS_A + 2 * tap + t:ROWS_A + 2 * tap + t + 1]
                src, acc = h_pad[:, t, tap:tap + SEQ], mid[:, 6 + t, :]
                if tap == 0:
                    nc.vector.tensor_scalar(acc, src, w, cols[:, R_CONVB + t:R_CONVB + t + 1], ALU.mult, ALU.add)\
                        .then_inc(tap_done, 1)
                else:
                    dve.wait_ge(tap_done, n)
                    nc.vector.scalar_tensor_tensor(out=acc, in0=src, scalar=w, in1=acc, op0=ALU.mult, op1=ALU.add)\
                        .then_inc(tap_done, 1)

            dve.wait_ge(glu_done, 2)
            for r in range(6):
                take_half_lo(0, r)
            N_STEPS = PAIRS * STEPS
            for a in range(N_STEPS + 1):
                pair, i = divmod(a, STEPS)
                if a < N_STEPS:
                    col, width = a % (2 * STEPS), P * blocks_of(i // 2)
                    dve.wait_ge(scores_done, a + 1)
                    if i == 0:
                        dve.wait_ge(bias_ready, pair + 1)
                    if a >= 2:
                        dve.wait_ge(pt_done, a - 1)
                    nb = blocks_of(i // 2)
                    bias = bias_rev[pair % 2][:, i % 2, 0:width][:, ::-1]
                    nc.vector.tensor_tensor_reduce(out=like_scores(probs[a % 2][:, 0:width], nb), in0=score_cols(nb),
                                                   in1=like_scores(bias, nb),
                                                   scale=-1.0, scalar=3e38, op0=ALU.add, op1=ALU.min,
                                                   accum_out=neg_max[:, col:col + 1]).then_inc(biased, 1)
                if a < N_STEPS and i == 0:
                    take_half_lo(pair, 6)
                    take_half_lo(pair, 7)
                if a < 2 * TAPS:
                    conv_tap(a)
                if a < N_STEPS:
                    dve.wait_ge(exp_done, a + 1)
                    link(nc.vector.reciprocal(inv_sum[:, col:col + 1], row_sum[:, col:col + 1]))
                    nc.vector.tensor_scalar(probs[a % 2][:, 0:width], probs[a % 2][:, 0:width],
                                            inv_sum[:, col:col + 1], None, ALU.mult).then_inc(probs_done, 1)
                if a >= 1:
                    b = a - 1
                    nb = blocks_of(b % STEPS // 2)
                    dve.wait_ge(pt_hi_done, b + 1)
                    nc.vector.tensor_tensor(pt_lo[:, 0:nb, b % 2, :],
                                            banks(6)[:, 0:nb * P].rearrange("p (b q) -> p b q", q=P),
                                            f(pt_hi[:, 0:nb, b % 2, :]), ALU.subtract).then_inc(pt_lo_done, 1)
                if half_of(pair, i):
                    take_half_lo(*half_of(pair, i))

            def cut_branch_lo(k):
                dve.wait_ge(br_hi_done, k + 1)
                nc.vector.tensor_tensor(br_lo[:, k, :], mid[:, k, :], f(br_hi[:, k, :]), ALU.subtract)\
                    .then_inc(br_lo_done, 1)

            dve.wait_ge(cmean_done, 1)
            for t in range(2):
                acc = mid[:, 6 + t, :]
                nc.vector.scalar_tensor_tensor(out=acc, in0=banks(4), scalar=-1.0 / D_CONV, in1=acc,
                                               op0=ALU.mult, op1=ALU.add).then_inc(centred, 1)
            cut_branch_lo(0)
            cut_branch_lo(1)
            dve.wait_ge(cvar_done, 1)
            nc.vector.tensor_scalar(conv_rstd[:, :], banks(2), 1.0 / D_CONV, EPS, ALU.mult, ALU.add)\
                .then_inc(cvar_read, 1)
            dve.wait_ge(cstd_done, 1)
            link(nc.vector.reciprocal(conv_rstd[:, :], conv_rstd[:, :]))
            dve.wait_ge(centred, 2)
            dve.wait_ge(squared, 2)
            for t in range(2):
                acc = mid[:, 6 + t, :]
                nc.vector.tensor_tensor(acc, acc, conv_rstd[:, :], ALU.mult).then_inc(cnormed, 1)
            for k in range(2, 6):
                cut_branch_lo(k)
            for t in range(2):
                acc = mid[:, 6 + t, :]
                dve.wait_ge(conv_sig_done, t + 1)
                link(nc.vector.tensor_scalar(acc, acc, cols[:, R_CLNG + t:R_CLNG + t + 1],
                                             cols[:, R_CLNB + t:R_CLNB + t + 1], ALU.mult, ALU.add))
                nc.vector.tensor_tensor(acc, acc, conv_sig[:, :], ALU.mult).then_inc(conv_done, 1)
            cut_branch_lo(6)
            cut_branch_lo(7)

            def cut_gate_lo(j, b):
                dve.wait_ge(w_hi_done, j * 4 + (N_GATE0 + b + 3))
                nc.vector.tensor_tensor(w_lo[b % 2][:, :, :], w_raw[b % 2][:, :, :], f(w_hi[b % 2][:, :, :]),
                                        ALU.subtract).then_inc(w_lo_done, 1)

            def merge(j):
                out_tile = mid[:, bass.ds(j, 1), :].rearrange("p o s -> p (o s)")
                for y in range(3):
                    dve.wait_ge(y_done, j * 3 + (y + 1))
                    dve.wait_ge(sig_done, j * 3 + (y + 1))
                    dst = out_tile if y == 0 else tmp[y - 1][:, :]
                    nc.vector.tensor_tensor(dst, banks((4, 6, 2)[y]), gate[y][:, :], ALU.mult).then_inc(y_used, 1)
                    dve.wait_ge(y_used, j * 3 + (y + 1))
                    if y > 0:
                        if y == 2:
                            dve.wait_ge(merged_step, j * 3 + 1)
                        nc.vector.tensor_tensor(out_tile, out_tile, tmp[y - 1][:, :], ALU.add)\
                            .then_inc(merged_step, y)

            cut_gate_lo(0, 2)
            merge(0)
            cut_gate_lo(0, 3)
            with dve.Fori(1, KT) as j:
                for b in range(4):
                    if b == 3:
                        merge(j)
                    cut_gate_lo(j, b)

            for k in range(KT):
                dve.wait_ge(mg_hi_done, k + 1)
                nc.vector.tensor_tensor(act_lo[:, k, :], mid[:, k, :], f(act_hi[:, k, :]), ALU.subtract)\
                    .then_inc(mg_lo_done, 1)
                dve.wait_ge(row_hi_done, k + 1)
                nc.vector.tensor_tensor(br_lo[:, k, :], row_raw[k % 2][:, :], f(br_hi[:, k, :]), ALU.subtract)\
                    .then_inc(row_lo_done, 1)

            def cut_x2(t):
                dve.wait_ge(x2_hi_done, t + 1)
                nc.vector.tensor_tensor(act_lo[:, :, t * P:(t + 1) * P],
                                        tmp[t % 2][:, :].rearrange("p (k s) -> p k s", s=P),
                                        f(act_hi[:, :, t * P:(t + 1) * P]), ALU.subtract).then_inc(x2_lo_done, 1)

            dve.wait_ge(ln_in, 32)
            dve.wait_ge(ff2b_scaled, 1)
            for t in range(ST + 2):
                if t < ST:
                    row = mid[:, t, :]
                    dve.wait_ge(mix_done, t + 1)
                    nc.vector.tensor_tensor(mix_tmp[:, :], banks(2 * (t % 2)), gate_mix[:, :], ALU.mult)\
                        .then_inc(mix_free, 1)
                    dve.wait_ge(mix_free, t + 1)
                    dve.wait_ge(res_in[t], 16)
                    link(nc.vector.scalar_tensor_tensor(out=row, in0=row, scalar=ALPHA, in1=mix_tmp[:, :],
                                                        op0=ALU.mult, op1=ALU.add))
                    stats(row, t)
                if t >= 3:
                    cut_x2(t - 3)
                if 1 <= t <= ST:
                    scale_bias(ST + 2 * (t - 1) + 1, t - 1)
                if t < ST:
                    scale_bias(ST + 2 * t, t)
                if t < ST:
                    dve.wait_ge(normed, ST + 2 * t + 1)
                    link(nc.vector.tensor_tensor(mix_tmp[:, :], mix_tmp[:, :], ln_g[:, :], ALU.mult))
                    nc.vector.tensor_tensor(row, mix_tmp[:, :], ln_b[:, :], ALU.add).then_inc(x1_done, 1)
                    dve.wait_ge(x1_done, t + 1)
                    stats(row, t)
            cut_x2(ST - 1)
            dve.wait_ge(res_done, ST)

            def mlp_group(g, last):
                for t in range(GROUP):
                    row = row_raw[t % 2]
                    dve.wait_ge(row_in[t % 2], g * (16 * GROUP // 2) + (16 * KT // 2 + 16 * (t // 2 + 1)))
                    nc.vector.tensor_tensor(row[:, :], row[:, :], gate_ff[:, :], ALU.mult).then_inc(row_scaled, 1)
                    dve.wait_ge(row_scaled, g * GROUP + (t + 1))
                    dve.wait_ge(h_hi_done, g * GROUP + (t + 1))
                    nc.vector.tensor_tensor(h_lo[:, t, :], tmp[t % 2][:, :], f(h_hi[:, t, :]), ALU.subtract)\
                        .then_inc(h_lo_done, 1)
                    if not (last and t >= 2):
                        dve.wait_ge(w_hi_done, g * GROUP + (N_FF0 + t + 3))
                        nc.vector.tensor_tensor(w_lo[t % 2][:, :, :], w_raw[t % 2][:, :, :],
                                                f(w_hi[t % 2][:, :, :]), ALU.subtract).then_inc(w_lo_done, 1)
                    dve.wait_ge(row_hi_done, g * GROUP + (KT + t + 1))
                    nc.vector.tensor_tensor(w2_lo[:, t, :], row[:, :], f(w2_hi[:, t, :]), ALU.subtract)\
                        .then_inc(row_lo_done, 1)
                for t in range(ST):
                    dve.wait_ge(f2_done, g * ST + (t + 1))
                    nc.vector.tensor_tensor(mid[:, t, :], mid[:, t, :], banks(4 + 2 * (t % 2)), ALU.add)\
                        .then_inc(acc_done, 1)
                    if last:
                        dve.wait_ge(acc_done, g * ST + (t + 1))
                        stats(mid[:, t, :], t)
                        if t >= 1:
                            finish_tile(t - 1)
                        scale_bias(3 * ST + t, t)
                if last:
                    finish_tile(ST - 1)

            def finish_tile(t):
                dve.wait_ge(normed, 3 * ST + t + 1)
                if t == 0:
                    dve.wait_ge(ln2_in, 32)
                tile = tmp[t % 2][:, :]
                link(nc.vector.tensor_tensor(tile, tile, ln_g[:, :], ALU.mult))
                nc.vector.tensor_tensor(tile, tile, ln_b[:, :], ALU.add).then_inc(y_ready, 1)

            with dve.Fori(0, GROUPS - 1) as g:
                mlp_group(g, False)
            mlp_group(GROUPS - 1, True)

        @block.tensor
        def _(pe):
            def product(out, parts, first, last):
                (sh, sl), (mh, ml) = parts
                nc.tensor.matmul(out, sh, mh, start=first, stop=False)
                nc.tensor.matmul(out, sh, ml, start=False, stop=False)
                return nc.tensor.matmul(out, sl, mh, start=False, stop=last)

            def act_part(k, cs):
                return act_hi[:, k, cs], act_lo[:, k, cs]

            def w_part(n, k):
                return w_hi[n % 2][:, k, :], w_lo[n % 2][:, k, :]

            def half_cols(h):
                return slice(h * HALF, (h + 1) * HALF)

            pe.wait_ge(consts_done, 2)

            def direct_chunk(i):
                pe.wait_ge(ada_in[i], 16)
                for m in range(4):
                    for k in range(8):
                        ins = nc.tensor.matmul(ps[:, 6, 4 * i + m:4 * i + m + 1], ada[i][:, k, m * P:(m + 1) * P],
                                               c_act[:, k:k + 1], start=k == 0, stop=k == 7)
                ins.then_inc(reduced, 1)

            def reduce_chunk(i):
                pe.wait_ge(partial_done, i + 1 - N_DIRECT)
                if i in (4, 5, 10, 11):
                    if i < 6:
                        pe.wait_ge(cols_done, 1)
                    else:
                        pe.wait_ge(gates_done, i - 9)
                    ins = nc.tensor.matmul(ps[:, 4 + i % 2, :], ones_row[:, :], partial[i % 2][:, :],
                                           start=True, stop=True)
                else:
                    bank, first = (6, 0) if i < 4 else (7, 6)
                    for m in range(4):
                        col = (i - first) * 4 + m
                        ins = nc.tensor.matmul(ps[:, bank, col:col + 1], partial[i % 2][:, m * P:(m + 1) * P],
                                               ones_row[:, 0:1], start=True, stop=True)
                ins.then_inc(reduced, 1)

            pe.wait_ge(c_act_done, 1)
            direct_chunk(0)
            direct_chunk(1)
            pe.wait_ge(small_in, 16 * 8)
            nc.tensor.transpose(ps[:, 4, 0:ROWS_A], rows_a[:, :], ident[0:ROWS_A, 0:ROWS_A]).then_inc(cols_t, 1)
            nc.tensor.transpose(ps[:, 5, 0:ROWS_C], rows_c[:, :], ident[0:ROWS_C, 0:ROWS_C]).then_inc(cols_t, 1)
            reduce_chunk(2)
            pe.wait_ge(normed, ST)
            for k in range(KT):
                if k == 2:
                    reduce_chunk(3)
                if k >= 2:
                    pe.wait_ge(u_tmp_done, k - 1)
                for i in range(ST):
                    ins = nc.tensor.transpose(ps[:, 2 * (k % 2) + i // 4, (i % 4) * P:(i % 4 + 1) * P],
                                              mid[:, i, k * P:(k + 1) * P], ident[:, :])
                ins.then_inc(z_done, 1)
            chunks_at = {0: (4,), 1: (5, 6), 2: (7,), 3: (8, 9), 4: (10,), 5: (11,)}
            for n in range(N_P1):
                pe.wait_ge(w_lo_done, n + 1)
                if n < 2:
                    pe.wait_ge(u_tmp_done, KT + n - 1)
                elif n in (2, 4):
                    pe.wait_ge(glu_sig_done, n // 2)
                else:
                    pe.wait_ge(glu_done, n // 2)
                for h in range(2):
                    for k in range(KT):
                        if n == 0 and h == 0:
                            pe.wait_ge(u_lo_done, k + 1)
                        ins = product(ps[:, 2 * (n % 2) + h, :], (w_part(n, k), act_part(k, half_cols(h))),
                                      k == 0, k == KT - 1)
                ins.then_inc(z_done, 1)
                for i in chunks_at[n]:
                    reduce_chunk(i)

            def project(pair, m):
                part, r = divmod(m, 48)
                half, kk = divmod(r, 24)
                k, term = divmod(kk, 3)
                n, hz = N_P1 + 3 * pair + part, 2 * part + half
                if r == 0:
                    pe.wait_ge(w_lo_done, n + 1)
                if kk == 0:
                    wait_bank(pair, hz)
                (sh, sl), (mh, ml) = w_part(n, k), act_part(k, half_cols(half))
                s, v = ((sh, mh), (sh, ml), (sl, mh))[term]
                ins = nc.tensor.matmul(ps[:, hz % 2, :], s, v, start=kk == 0, stop=kk == 23)
                if kk == 23:
                    ins.then_inc(h_done, 1)

            def wait_bank(pair, r):
                if pair == 0 and r < 2:
                    pe.wait_ge(zp_done, 1)
                else:
                    pe.wait_ge(h_free[r % 2], 4 * pair + r // 2)

            def transpose_v(pair, half):
                if half == 0:
                    for b in range(2):
                        pe.wait_ge(h_free[b], 4 * pair + 3)
                wait_bank(pair, 6 + half)
                for t in range(4 * half, 4 * half + 4):
                    ins = nc.tensor.transpose(ps[:, half, (t % 4) * P:(t % 4 + 1) * P], mid[:, 5, t * P:(t + 1) * P],
                                              ident[:, :])
                ins.then_inc(h_done, 1)

            def scores(a):
                pair, i = divmod(a, STEPS)
                t, h = divmod(i, 2)
                nb = blocks_of(t)
                s, rows, qs = pair % 2, slice(h * HEAD_DIM, (h + 1) * HEAD_DIM), slice(t * P, (t + 1) * P)
                if i == 0:
                    for b in range(2):
                        pe.wait_ge(h_free[b], 4 * pair + 2)
                if a == 0:
                    pe.wait_ge(gates_done, 4)
                    pe.wait_ge(mod_done, 2)
                else:
                    pe.wait_ge(biased, a)
                first_key = (t + 1 - nb) * P
                parts = 2 if nb == BAND_BLOCKS else 1
                n = nb * P // parts
                for part in range(parts):
                    ks = slice(first_key + part * n, first_key + (part + 1) * n)
                    ins = product(ps[:, 4 + part, 0:n],
                                  ((q_hi[s][rows, qs], q_lo[s][rows, qs]), (k_hi[s][rows, ks], k_lo[s][rows, ks])),
                                  True, True)
                ins.then_inc(scores_done, 1)

            def transpose_probs(a):
                pe.wait_ge(probs_done, a + 1)
                if a >= 1:
                    pe.wait_ge(pt_lo_done, a)
                for b in range(blocks_of(a % STEPS // 2)):
                    ins = nc.tensor.transpose(banks(6)[:, b * P:(b + 1) * P], probs[a % 2][:, b * P:(b + 1) * P],
                                              ident[:, :])
                ins.then_inc(pt_done, 1)

            def weigh(tile):
                pair, t = divmod(tile, ST)
                nb = blocks_of(t)
                s = pair % 2
                pe.wait_ge(pt_lo_done, 2 * tile + 2)
                if t == 0:
                    for b in range(2):
                        pe.wait_ge(h_free[b], 4 * pair + 4)
                if tile >= 1:
                    pe.wait_ge(o_copied, 2 * tile)
                else:
                    pe.wait_ge(zp_done, 2)
                for b in range(nb):
                    kt = t + 1 - nb + b
                    ins = product(ps[:, 2, 0:2 * P],
                                  ((v_hi[s][:, kt, :], v_lo[s][:, kt, :]), (pt_hi[:, b, :, :], pt_lo[:, b, :, :])),
                                  b == 0, b == nb - 1)
                ins.then_inc(pv_done, 1)

            for m in range(PROJ):
                project(0, m)
            N_STEPS = PAIRS * STEPS
            def mix_pool(u):
                if u == 0:
                    pe.wait_ge(pooled_done, 2)
                    pe.wait_ge(pool_w_in, 64)
                else:
                    pe.wait_ge(pm_scaled, u)
                nc.tensor.matmul(ps[:, 3, :], w_pool_bd[:, u // 2, :], z_pool[:, u // 2, half_cols(u % 2)],
                                 start=True, stop=True).then_inc(pm_done, 1)

            def conv_sums(bank, src):
                for h in range(2):
                    for t in range(2):
                        ins = nc.tensor.matmul(ps[:, bank + h, :], ones_row[:, :], src[:, t, half_cols(h)],
                                               start=t == 0, stop=t == 1)
                return ins

            def gate_half(b, h):
                for k in range(KT):
                    ins = product(ps[:, 2 * (b % 2) + h, :], (w_part(b, k), act_part(k, half_cols(h))),
                                  k == 0, k == KT - 1)
                return ins

            def between(a, part):
                pair, i = divmod(a, STEPS)
                per = PER_STEP if pair < PAIRS - 1 else early_per_step
                if pair < PAIRS:
                    for m in range(per * i + part * (per // 2), per * i + (per if part else per // 2)):
                        project(pair + 1, m)

            for a in range(N_STEPS + 2):
                pair, i = divmod(a, STEPS)
                if a < N_STEPS:
                    scores(a)
                    if i == 0:
                        transpose_v(pair, 0)
                        transpose_v(pair, 1)
                if a == N_STEPS:
                    pe.wait_ge(biased, N_STEPS)
                    pe.wait_ge(tap_done, 2 * TAPS)
                    conv_sums(4, mid[:, 6:8, :]).then_inc(cmean_done, 1)
                between(a, 0)
                if a >= 3 and a % 2 == 1:
                    weigh((a - 3) // 2)
                if 1 <= a <= N_STEPS:
                    transpose_probs(a - 1)
                if pool_mix_unit(a) is not None:
                    mix_pool(pool_mix_unit(a))
                between(a, 1)
                if a == N_STEPS:
                    for b in range(2):
                        pe.wait_ge(h_free[b], 4 * PAIRS + EARLY)
                    pe.wait_ge(w_lo_done, N_GATE0 + 3)
                    gate_half(2, 0)
            pe.wait_ge(squared, 2)
            pe.wait_ge(o_copied, N_STEPS)
            conv_sums(2, sq).then_inc(cvar_done, 1)
            gate_half(2, 1).then_inc(g_done, 1)

            def branches(j, first):
                pe.wait_ge(w_lo_done, j * 4 + (N_GATE0 + 4))
                for y, (k0, k1, bank) in enumerate(((0, 2, 4), (2, 6, 6), (6, 8, 2))):
                    if first:
                        pe.wait_ge(br_lo_done, k1)
                        pe.wait_ge(*((centred, 2), (pt_lo_done, N_STEPS), (cvar_read, 1))[y])
                    elif y == 2:
                        pe.wait_ge(sig_done, j * 3 + 2)
                    for h in range(2):
                        cs = half_cols(h)
                        for k in range(k0, k1):
                            ins = product(ps[:, bank + h, :], (w_part(3, k), (br_hi[:, k, cs], br_lo[:, k, cs])),
                                          k == k0, k == k1 - 1)
                    ins.then_inc(y_done, 1)

            branches(0, True)
            with pe.Fori(1, KT) as j:
                for b in range(3):
                    pe.wait_ge(w_lo_done, j * 4 + (N_GATE0 + b + 1))
                    if b == 2:
                        pe.wait_ge(sig_done, j * 3 + 1)
                    gate_half(b, 0)
                    gate_half(b, 1).then_inc(g_done, 1)
                branches(j, False)

            def transpose_x2(t):
                pe.wait_ge(normed, ST + 2 * t + 2)
                if t >= 2:
                    pe.wait_ge(x2_tmp_done, t - 1)
                for k in range(KT):
                    ins = nc.tensor.transpose(banks(4 + 2 * (t % 2))[:, k * P:(k + 1) * P],
                                              tmp[t % 2][:, k * P:(k + 1) * P], ident[:, :])
                ins.then_inc(x2t_done, 1)

            pe.wait_ge(sig_done, 3 * KT)
            pe.wait_ge(y_used, 3 * KT)
            for t in range(ST):
                if t >= 2:
                    pe.wait_ge(mix_free, t - 1)
                ts = slice(t * P, (t + 1) * P)
                for k in range(KT):
                    if t >= 2 and k == KT // 2:
                        transpose_x2(t - 2)
                    if t == 0:
                        pe.wait_ge(mg_lo_done, k + 1)
                        pe.wait_ge(row_lo_done, k + 1)
                    for h in range(2):
                        cs = half_cols(h)
                        ins = product(ps[:, 2 * (t % 2) + h, :], (act_part(k, ts), (br_hi[:, k, cs], br_lo[:, k, cs])),
                                      k == 0, k == KT - 1)
                ins.then_inc(mix_done, 1)
            transpose_x2(ST - 2)

            def ff1_half(g, t, h):
                for k in range(KT):
                    ins = product(ps[:, 2 * (t % 2) + h, :], (w_part(t, k), act_part(k, half_cols(h))),
                                  k == 0, k == KT - 1)
                if h == 1:
                    ins.then_inc(f1_done, 1)

            def mlp_group(g, first):
                if first:
                    for h in range(2):
                        pe.wait_ge(x2_lo_done, ST // 2 * (h + 1))
                        for t in range(2):
                            if h == 0:
                                pe.wait_ge(w_lo_done, N_FF0 + t + 1)
                                pe.wait_ge(mix_free, ST - 1 + t)
                            ff1_half(g, t, h)
                        if h == 0:
                            transpose_x2(ST - 1)
                for t in range(2 if first else 0, GROUP):
                    pe.wait_ge(w_lo_done, g * GROUP + (N_FF0 + t + 1))
                    pe.wait_ge(relu_done, g * GROUP + (t - 1))
                    for h in range(2):
                        ff1_half(g, t, h)
                for pair in range(ST // 2):
                    for k in range(GROUP):
                        if pair == 0:
                            pe.wait_ge(h_lo_done, g * GROUP + (k + 1))
                            pe.wait_ge(row_lo_done, g * GROUP + (KT + k + 1))
                        for t in (2 * pair, 2 * pair + 1):
                            ts = slice(t * P, (t + 1) * P)
                            if k == 0 and not (first and pair == 0):
                                pe.wait_ge(acc_done, g * ST + (t - 1))
                            for h in range(2):
                                cs = half_cols(h)
                                ins = product(ps[:, 4 + 2 * (t % 2) + h, :],
                                              ((h_hi[:, k, ts], h_lo[:, k, ts]), (w2_hi[:, k, cs], w2_lo[:, k, cs])),
                                              k == 0, k == GROUP - 1)
                            if k == GROUP - 1:
                                ins.then_inc(f2_done, 1)

            mlp_group(0, True)
            with pe.Fori(1, GROUPS) as g:
                mlp_group(g, False)


_INS = ['x', 'c', 'w_ada', 'b_ada', 'w_in', 'b_gate', 'w_pool', 'pool_scale', 'rel_bias', 'conv_w', 'conv_b',
        'conv_ln_g', 'conv_ln_b', 'w_br_pool', 'w_br_attn', 'w_br_conv', 'w_o', 'ln_mix_g', 'ln_mix_b',
        'w_ff1', 'b_ff1', 'w_ff2', 'b_ff2', 'ln_ff_g', 'ln_ff_b']
_OUTS = [((1, SEQ, D), 'float32')]


def kernel(**inputs):
    import numpy as _np
    import concourse.bacc as _bacc
    from concourse import mybir as _mybir
    from concourse.bass_utils import run_bass_kernel_spmd as _run

    nc = _bacc.Bacc("TRN2", target_bir_lowering=False, num_devices=1, dynamic_dma_scratch_size=1024)
    arrays, args = {}, []
    for name in _INS:
        a = _np.ascontiguousarray(inputs[name])
        arrays[f"in_{name}_dram"] = a
        args.append(nc.dram_tensor(f"in_{name}_dram", a.shape, _mybir.dt.from_np(a.dtype), kind="ExternalInput").ap())
    for i, (shape, dtype) in enumerate(_OUTS):
        dt = _mybir.dt.from_np(_np.dtype(dtype))
        args.append(nc.dram_tensor(f"out_{i}_dram", shape, dt, kind="ExternalOutput").ap())
    trunk_layer(nc, *args)
    r = _run(nc, [arrays], core_ids=[0])
    got = tuple(r.results[0][f"out_{i}_dram"] for i in range(len(_OUTS)))
    return got[0]
```

```python
import concourse.bass as bass
from concourse import mybir
from contextlib import ExitStack

SEQ = 1024
D = 1024
P = 128
KT = D // P
ST = SEQ // P
HALF = 512
D_POOL, D_ATTN, D_CONV = 256, 512, 256
CHUNK, N_PREV = 64, 8
HEADS, HEAD_DIM = 8, 64
PAIRS = HEADS // 2
TAPS = 31
REL_CLIP = 128
N_REL = 2 * REL_CLIP + 1
D_FF = 4 * D
BAND_BLOCKS = N_PREV * CHUNK // P + 1
BAND = BAND_BLOCKS * P
ALPHA = 2.0 ** 0.25
EPS = 1e-5
MASKED = -1e30
C_POOL, C_Q = 0, D_POOL
C_K, C_V = C_Q + D_ATTN, C_Q + 2 * D_ATTN
C_CONV = C_Q + 3 * D_ATTN
C_GATE = C_CONV + 2 * D_CONV
R_ADA, R_GATE, R_FF1 = 0, 48, 72
R_CONVB, R_CLNG, R_CLNB, R_PSC = 104, 106, 108, 110
ROWS_A, ROWS_C = 112, 2 * TAPS
N_P1 = 6
N_GATE0 = N_P1 + 3 * PAIRS
N_FF0 = N_GATE0 + 4 * KT
GROUP = 4
GROUPS = D_FF // (P * GROUP)
STEPS = 2 * ST
PROJ = 3 * 2 * KT * 3
PER_STEP = PROJ // STEPS
EARLY = 2
N_DIRECT = 2
MIX_STEP = 24


def trunk_layer(nc, x, c, w_ada, b_ada, w_in, b_gate, w_pool, pool_scale, rel_bias, conv_w, conv_b,
                conv_ln_g, conv_ln_b, w_br_pool, w_br_attn, w_br_conv, w_o, ln_mix_g, ln_mix_b,
                w_ff1, b_ff1, w_ff2, b_ff2, ln_ff_g, ln_ff_b, out):
    f32, f32r = mybir.dt.float32, mybir.dt.float32r
    ALU, ACT = mybir.AluOpType, mybir.ActivationFunctionType

    KB = 1024
    base = (nc.sbuf_base + 63) // 64 * 64
    top = nc.sbuf_usable_end

    def at(name, shape, dt, offset):
        size = 4
        for n in shape[1:]:
            size *= n
        assert base + offset + size <= top, (name, base + offset + size - top)
        return nc.alloc_sbuf_tensor_at(name, shape, dt, offset=base + offset)

    act_hi = at("act_hi", [P, KT, SEQ], f32r, 0)
    act_lo = at("act_lo", [P, KT, SEQ], f32r, 32 * KB)
    mid = at("mid", [P, KT, SEQ], f32, 64 * KB)
    w_raw = [at(f"w_raw{i}", [P, KT, P], f32, (96 + 4 * i) * KB) for i in range(2)]
    w_hi = [at(f"w_hi{i}", [P, KT, P], f32r, (104 + 4 * i) * KB) for i in range(2)]
    w_lo = [at(f"w_lo{i}", [P, KT, P], f32r, (112 + 4 * i) * KB) for i in range(2)]
    X = 120 * KB
    ada = [at(f"ada{i}", [P, 8, HALF], f32, X + 16 * i * KB) for i in range(3)]
    partial = [at(f"partial{i}", [P, HALF], f32, X + (48 + 2 * i) * KB) for i in range(2)]
    glu_gate = at("glu_gate", [P, SEQ], f32, X + 52 * KB)
    u_tmp = [at(f"u_tmp{i}", [P, SEQ], f32, X + (56 - 4 * i) * KB) for i in range(2)]
    rel_ext = at("rel_ext", [HEADS, 768], f32, X + 60 * KB)
    rows_a = at("rows_a", [ROWS_A, P], f32, X + 63 * KB)
    rows_c = at("rows_c", [ROWS_C, P], f32, X + 63 * KB + 512)
    q_hi = [at(f"q_hi{i}", [P, SEQ], f32r, X + 16 * i * KB) for i in range(2)]
    q_lo = [at(f"q_lo{i}", [P, SEQ], f32r, X + (16 * i + 4) * KB) for i in range(2)]
    k_hi = [at(f"k_hi{i}", [P, SEQ], f32r, X + (16 * i + 8) * KB) for i in range(2)]
    k_lo = [at(f"k_lo{i}", [P, SEQ], f32r, X + (16 * i + 12) * KB) for i in range(2)]
    v_hi = [at(f"v_hi{i}", [P, ST, P], f32r, X + (32 + 8 * i) * KB) for i in range(2)]
    v_lo = [at(f"v_lo{i}", [P, ST, P], f32r, X + (36 + 8 * i) * KB) for i in range(2)]
    bias_rev = [at(f"bias_rev{i}", [P, 2, BAND], f32, X + (48 + 5 * i) * KB) for i in range(2)]
    probs = [at(f"probs{i}", [P, BAND], f32, X + 58 * KB + 2560 * i) for i in range(2)]
    pt_hi = at("pt_hi", [P, BAND_BLOCKS, 2, P], f32r, X + 63 * KB)
    pt_lo = at("pt_lo", [P, BAND_BLOCKS, 2, P], f32r, X + 68 * KB)
    PAD = TAPS - 1
    h_pad = at("h_pad", [P, 2, PAD + SEQ], f32, X + 74 * KB)
    z_pool = at("z_pool", [P, 2, SEQ], f32, X + 82 * KB + 512)
    w_pool_bd = at("w_pool_bd", [P, 2, P], f32, X + 90 * KB + 512)
    sq = at("sq", [P, 2, SEQ], f32, X + 64 * KB)
    conv_sig = [at(f"conv_sig{i}", [P, SEQ], f32, X + (72 + 4 * i) * KB) for i in range(2)]
    conv_std = conv_sig[1]
    br_hi = at("br_hi", [P, KT, SEQ], f32r, X)
    br_lo = at("br_lo", [P, KT, SEQ], f32r, X + 32 * KB)
    gate_z = [at(f"gate_z{i}", [P, SEQ], f32, X + (82 + 4 * i) * KB + 512) for i in range(2)]
    gate = [at(f"gate{i}", [P, SEQ], f32, X + (72 + 4 * i) * KB) for i in range(3)]
    row_raw = [at(f"row_raw{i}", [P, D], f32, X + (64 + 4 * i) * KB) for i in range(2)]
    ln_g = at("ln_g", [P, D], f32, X + 72 * KB)
    ln_b = at("ln_b", [P, D], f32, X + 76 * KB)
    ff2_bias = at("ff2_bias", [P, D], f32, X + 80 * KB)
    tmp = [at(f"tmp{i}", [P, D], f32, X + (84 + 4 * i) * KB) for i in range(2)]
    mix_tmp = [at(f"mix_tmp{i}", [P, D], f32, (96 + 4 * i) * KB) for i in range(2)]
    gate_mix = at("gate_mix", [P, D], f32, X + 92 * KB)
    gate_ff = at("gate_ff", [P, D], f32, X + 96 * KB)
    h_hi = at("h_hi", [P, GROUP, SEQ], f32r, X)
    h_lo = at("h_lo", [P, GROUP, SEQ], f32r, X + 16 * KB)
    w2_hi = at("w2_hi", [P, GROUP, D], f32r, X + 32 * KB)
    w2_lo = at("w2_lo", [P, GROUP, D], f32r, X + 48 * KB)
    small = X + 100 * KB

    def little(name, shape):
        nonlocal small
        t = at(name, shape, f32, small)
        n = 4
        for m in shape[1:]:
            n *= m
        small += (n + 31) // 32 * 32
        return t

    ident = little("ident", [P, P])
    cols = little("cols", [P, ROWS_A + ROWS_C])
    mod = little("mod", [P, 48])
    ones_row = at("ones_row", [P, P], f32, X + 91 * KB + 512)
    inv_count = little("inv_count", [P, 2, 16])
    c_raw = little("c_raw", [P, 8])
    c_sig = little("c_sig", [P, 8])
    c_act = little("c_act", [P, 8])
    neg_max = little("neg_max", [P, 2 * STEPS])
    row_sum = little("row_sum", [P, 2 * STEPS])
    inv_sum = little("inv_sum", [P, 2 * STEPS])
    bn = little("bn", [P, 12])
    mean_var = little("mean_var", [P, ST, 2])
    rstd = little("rstd", [P, ST])
    neg_mean = little("neg_mean", [P, ST])

    rel_dram = nc.dram_tensor("rel_scratch", (HEADS, 768), f32, kind="Internal").ap()

    x_rows = x[0].rearrange("(t p) d -> t p d", p=P)
    out_rows = out[0].rearrange("(t p) d -> t p d", p=P)
    ada_view = w_ada[0].rearrange("(p k) n -> p k n", k=8)
    win_view = w_in[0].rearrange("(k p) n -> p k n", p=P)
    wff1_view = w_ff1[0].rearrange("(k p) n -> p k n", p=P)
    brp_view = w_br_pool[0].rearrange("(k p) n -> p k n", p=P)
    bra_view = w_br_attn[0].rearrange("(k p) n -> p k n", p=P)
    brc_view = w_br_conv[0].rearrange("(k p) n -> p k n", p=P)

    def win_col(n):
        if n < 4:
            return C_CONV + ((n + 1) % 2) * D_CONV + (n // 2) * P
        if n < N_P1:
            return C_POOL + (n - 4) * P
        pair, part = divmod(n - N_P1, 3)
        if pair == PAIRS:
            return C_GATE + part * D
        return (C_Q, C_K, C_V)[part] + pair * P

    with ExitStack() as ctx:
        ps = ctx.enter_context(nc.psum_tensor("ps", [P, 8, HALF], f32))

        def sem(name):
            return ctx.enter_context(nc.semaphore(name))

        def banks(b, n=2):
            return ps[:, b:b + n, :].rearrange("p b n -> p (b n)")

        def f(ap):
            return ap.bitcast(f32)

        c_in, small_in = sem("c_in"), sem("small_in")
        x_in = [sem(f"x_in{i}") for i in range(ST)]
        ada_in, ada3_end_in = [sem(f"ada_in{i}") for i in range(3)], sem("ada3_end_in")
        w_arrived = [sem(f"w_arrived{i}") for i in range(2)]
        pool_w_in, rel_in, rel_stored = sem("pool_w_in"), sem("rel_in"), sem("rel_stored")
        bias_in = [sem(f"bias_in{i}") for i in range(2)]
        row_in = [sem(f"row_in{i}") for i in range(2)]
        res_in = [sem(f"res_in{i}") for i in range(ST)]
        ada_bias_in, ln_in, ln2_in, ff2b_in = sem("ada_bias_in"), sem("ln_in"), sem("ln2_in"), sem("ff2b_in")
        stored = [sem(f"stored{i}") for i in range(2)]
        consts_done, bd_zeroed = sem("consts_done"), sem("bd_zeroed")
        pool_step, dve_step = sem("pool_step"), sem("dve_step")
        c_sig_done, c_act_done, cols_t, cols_done, rel_done = (
            sem("c_sig_done"), sem("c_act_done"), sem("cols_t"), sem("cols_done"), sem("rel_done"))
        partial_done, reduced, mod_done, gates_done = (
            sem("partial_done"), sem("reduced"), sem("mod_done"), sem("gates_done"))
        var_done, std_done, norm_ready, normed = sem("var_done"), sem("std_done"), sem("norm_ready"), sem("normed")
        w_hi_done, w_lo_done = sem("w_hi_done"), sem("w_lo_done")
        row_hi_done, row_lo_done, row_scaled = sem("row_hi_done"), sem("row_lo_done"), sem("row_scaled")
        z_done, u_tmp_done, u_lo_done = sem("z_done"), sem("u_tmp_done"), sem("u_lo_done")
        glu_sig_done, glu_done, zp_done, pooled_done = (
            sem("glu_sig_done"), sem("glu_done"), sem("zp_done"), sem("pooled_done"))
        h_done, half_hi, h_free = sem("h_done"), sem("half_hi"), [sem(f"h_free{i}") for i in range(2)]
        vt_done, vt_hi, vt_free = sem("vt_done"), sem("vt_hi"), sem("vt_free")
        scores_done, biased, exp_done, probs_done = (
            sem("scores_done"), sem("biased"), sem("exp_done"), sem("probs_done"))
        pt_done, pt_hi_done, pt_lo_done = sem("pt_done"), sem("pt_hi_done"), sem("pt_lo_done")
        pv_done, o_copied, bias_ready = sem("pv_done"), sem("o_copied"), sem("bias_ready")
        pm_done, pm_scaled, tap_done = sem("pm_done"), sem("pm_scaled"), sem("tap_done")
        cmean_done, centred, squared, cvar_done, cvar_read = (
            sem("cmean_done"), sem("centred"), sem("squared"), sem("cvar_done"), sem("cvar_read"))
        cstd_done, cnormed, conv_sig_done, conv_done = (
            sem("cstd_done"), sem("cnormed"), sem("conv_sig_done"), sem("conv_done"))
        br_hi_done, br_lo_done = sem("br_hi_done"), sem("br_lo_done")
        g_done, sig_done, y_done, y_used, merged_step = (
            sem("g_done"), sem("sig_done"), sem("y_done"), sem("y_used"), sem("merged_step"))
        mg_hi_done, mg_lo_done = sem("mg_hi_done"), sem("mg_lo_done")
        mix_done, mix_free, res_done, x1_done = sem("mix_done"), sem("mix_free"), sem("res_done"), sem("x1_done")
        x2t_done, x2_tmp_done, x2_hi_done, x2_lo_done = (
            sem("x2t_done"), sem("x2_tmp_done"), sem("x2_hi_done"), sem("x2_lo_done"))
        ff2b_scaled, x1_scaled, mix_scaled, y_scaled = (
            sem("ff2b_scaled"), sem("x1_scaled"), sem("mix_scaled"), sem("y_scaled"))
        f1_done, relu_done, sq_done, h_hi_done, h_lo_done = (
            sem("f1_done"), sem("relu_done"), sem("sq_done"), sem("h_hi_done"), sem("h_lo_done"))
        f2_done, acc_done, y_ready = sem("f2_done"), sem("acc_done"), sem("y_ready")

        block = ctx.enter_context(nc.Block())

        def block_used(n):
            if n < N_P1:
                return z_done, 8 + n + 1
            pair, part = divmod(n - N_P1, 3)
            return h_done, 6 * pair + 2 * part + 2

        W0_GATES = 16 * N_GATE0 // 2
        W0_FF = [W0_GATES + 32 * KT, W0_GATES + 64 * KT]

        def blocks_of(t):
            return min(t + 1, BAND_BLOCKS)

        def score_cols(nb):
            if nb < BAND_BLOCKS:
                return banks(4)[:, 0:nb * P]
            return ps[:, 4:6, 0:BAND // 2]

        def like_scores(ap, nb):
            return ap if nb < BAND_BLOCKS else ap.rearrange("p (b n) -> p b n", b=2)

        def first_norm(t):
            return ST + max(2 * t - 1, 0)

        def second_norm(t):
            return ST + min(2 * t + 2, 2 * ST - 1)

        @block.sync
        def _(sp):
            def load_block(n):
                if n >= 2:
                    sp.wait_ge(w_lo_done, n - 1)
                c0 = win_col(n)
                sp.dma_start(w_raw[n % 2][:, :, :], win_view[:, :, c0:c0 + P]).then_inc(w_arrived[n % 2], 16)

            def load_ada(i):
                if 3 <= i < 3 + N_DIRECT:
                    sp.wait_ge(reduced, i - 2)
                elif i >= 3:
                    sp.wait_ge(partial_done, i - 2 - N_DIRECT)
                cs = slice(i * HALF, (i + 1) * HALF)
                if i == 3:
                    sp.dma_start(ada[0][:, 0:4, :], ada_view[:, 0:4, cs]).then_inc(ada_in[0], 16)
                    sp.dma_start(ada[0][:, 4:8, :], ada_view[:, 4:8, cs]).then_inc(ada3_end_in, 16)
                else:
                    sp.dma_start(ada[i % 3][:, :, :], ada_view[:, :, cs]).then_inc(ada_in[i % 3], 16)

            sp.dma_start(c_raw[:, :], c[0].rearrange("(p k) -> p k", k=8)).then_inc(c_in, 16)
            load_ada(0)
            for i in range(ST // 2):
                sp.dma_start(mid[:, i, :], x_rows[i]).then_inc(x_in[i], 16)
            for row, n, src in ((R_ADA, 48, b_ada), (R_GATE, 24, b_gate), (R_FF1, 32, b_ff1), (R_CONVB, 2, conv_b),
                                (R_CLNG, 2, conv_ln_g), (R_CLNB, 2, conv_ln_b), (R_PSC, 2, pool_scale)):
                sp.dma_start(rows_a[row:row + n, :], src[0].rearrange("(r p) -> r p", p=P)).then_inc(small_in, 16)
            sp.dma_start(rows_c[:, :], conv_w[0].rearrange("t (c p) -> (t c) p", p=P)).then_inc(small_in, 16)
            load_ada(1)
            for i in range(ST // 2, ST):
                sp.dma_start(mid[:, i, :], x_rows[i]).then_inc(x_in[i], 16)
            load_ada(2)
            load_ada(3)
            load_block(0)
            load_block(1)
            sp.dma_start(rel_ext[:, 0:2 * REL_CLIP], rel_bias[0][:, 1:N_REL]).then_inc(rel_in, 16)
            sp.wait_ge(bd_zeroed, 1)
            for g in range(4):
                lo = 64 * (g % 2)
                sp.dma_start(w_pool_bd[lo:lo + 64, g // 2, lo:lo + 64], w_pool[0, g]).then_inc(pool_w_in, 16)
            for t, col in ((gate_mix, 2 * D), (gate_ff, 5 * D)):
                sp.dma_start(t[:, :], b_ada[0:1, col:col + D].partition_broadcast(P)).then_inc(ada_bias_in, 16)
            sp.wait_ge(rel_done, 1)
            sp.dma_start(rel_dram, rel_ext[:, :]).then_inc(rel_stored, 16)
            load_ada(4)
            for n in range(2, 9):
                load_ada(n + 3)
                load_block(n)

            def load_bias(pair):
                if pair >= 2:
                    sp.wait_ge(biased, STEPS * (pair - 1))
                for h in range(2):
                    head = 2 * pair + h
                    src = bass.AP(rel_dram.tensor, head * 768, [[1, P], [1, BAND]])
                    sp.dma_start(bias_rev[pair % 2][:, h, :], src).then_inc(bias_in[pair % 2], 16)

            load_block(9)
            sp.wait_ge(reduced, 12)
            sp.wait_ge(glu_done, 2)
            sp.wait_ge(u_lo_done, KT)
            sp.wait_ge(rel_stored, 16)
            load_bias(0)
            load_bias(1)
            for n in range(10, N_GATE0 + 3):
                if n == N_P1 + 10:
                    load_bias(2)
                if n == N_GATE0 + 1:
                    load_bias(3)
                load_block(n)

            def load_branches(slot, col):
                for k0, k1, view in ((0, 2, brp_view), (2, 6, bra_view), (6, 8, brc_view)):
                    sp.dma_start(w_raw[slot][:, k0:k1, :], view[:, :, bass.ds(col, P)]).then_inc(w_arrived[slot], 16)

            sp.wait_ge(w_lo_done, N_GATE0 + 2)
            load_branches((N_GATE0 + 3) % 2, 0)

            with sp.Fori(2, KT + 1) as j_next:
                j = j_next - 1
                first = [sp.snap(j * P + (C_GATE + b * D)) for b in range(3)]
                cut = [sp.snap(j * 4 + (N_GATE0 + b - 1)) for b in range(4)]
                for b in range(4):
                    sp.wait_ge(w_lo_done, cut[b])
                    slot = (N_GATE0 + b) % 2
                    if b < 3:
                        sp.dma_start(w_raw[slot][:, :, :], win_view[:, :, bass.ds(first[b], P)])\
                            .then_inc(w_arrived[slot], 16)
                    else:
                        load_branches(slot, j_next * P - P)

            def load_row(q, src):
                sp.dma_start(row_raw[q % 2][:, :], src).then_inc(row_in[q % 2], 16)

            sp.wait_ge(conv_done, 2)
            for q in range(2):
                load_row(q, w_o[0, q * P:(q + 1) * P, :])
            for n in range(2):
                sp.wait_ge(w_lo_done, N_FF0 + n - 1)
                sp.dma_start(w_raw[n][:, :, :], wff1_view[:, :, n * P:(n + 1) * P]).then_inc(w_arrived[n], 16)
            sp.wait_ge(y_used, 3 * KT)
            for q in range(2, KT):
                sp.wait_ge(row_lo_done, q - 1)
                load_row(q, w_o[0, q * P:(q + 1) * P, :])
                if q == 2:
                    sp.dma_start(ln_g[:, :], ln_mix_g[0:1, :].partition_broadcast(P)).then_inc(ln_in, 16)
                    sp.dma_start(ln_b[:, :], ln_mix_b[0:1, :].partition_broadcast(P)).then_inc(ln_in, 16)
                    sp.dma_start(ff2_bias[:, :], b_ff2[0:1, :].partition_broadcast(P)).then_inc(ff2b_in, 16)
                if q >= 4:
                    sp.wait_ge(mg_lo_done, q - 3)
                    sp.dma_start(mid[:, q - 4, :], x_rows[q - 4]).then_inc(res_in[q - 4], 16)
            for i in range(4, ST):
                sp.wait_ge(mg_lo_done, i + 1)
                sp.dma_start(mid[:, i, :], x_rows[i]).then_inc(res_in[i], 16)

            def ff_loads(g, last):
                first = [g * (GROUP * P) + t * P for t in range(GROUP + 2)]
                rows_cut = [g * GROUP + (KT + t - 1) for t in range(GROUP)]
                block_cut = [g * GROUP + (N_FF0 + t + 1) for t in range(GROUP)]
                if not last:
                    first, rows_cut, block_cut = ([sp.snap(v) for v in vs] for vs in (first, rows_cut, block_cut))
                for t in range(GROUP):
                    sp.wait_ge(row_lo_done, rows_cut[t])
                    sp.dma_start(row_raw[t % 2][:, :], w_ff2[0, bass.ds(first[t], P), :]).then_inc(row_in[t % 2], 16)
                    if not (last and t >= 2):
                        sp.wait_ge(w_lo_done, block_cut[t])
                        sp.dma_start(w_raw[t % 2][:, :, :], wff1_view[:, :, bass.ds(first[t + 2], P)])\
                            .then_inc(w_arrived[t % 2], 16)

            sp.wait_ge(x1_done, ST)
            with sp.Fori(0, GROUPS - 1) as g:
                ff_loads(g, False)
            ff_loads(GROUPS - 1, True)
            sp.dma_start(ln_g[:, :], ln_ff_g[0:1, :].partition_broadcast(P)).then_inc(ln2_in, 16)
            sp.dma_start(ln_b[:, :], ln_ff_b[0:1, :].partition_broadcast(P)).then_inc(ln2_in, 16)
            for t in range(ST):
                sp.wait_ge(y_ready, t + 1)
                sp.dma_start(out_rows[t], tmp[t % 2][:, :]).then_inc(stored[t % 2], 16)
            for b in range(2):
                sp.wait_ge(stored[b], 16 * ST // 2)

        def arrived(n):
            if n < N_GATE0:
                return 16 * (n // 2 + 1)
            j, b = divmod(n - N_GATE0, 4)
            return gate_arrived(j, b)

        def gate_arrived(j, b):
            return (j * 32 + (W0_GATES + (16, 16, 32, 64)[b])) if b % 2 == 0 else (j * 64 + (W0_GATES + (16, 16, 32, 64)[b]))

        def ff_arrived(g, t):
            return g * (16 * GROUP // 2) + (W0_FF[t % 2] + 16 * (t // 2 + 1))

        @block.gpsimd
        def _(pool):
            steps = [0]

            def link(ins):
                steps[0] += 1
                ins.then_inc(pool_step, 1)
                pool.wait_ge(pool_step, steps[0])

            link(nc.gpsimd.memset(ident[:, :], 0.0))
            nc.gpsimd.affine_select(out=ident[:, :], in_=ident[:, :], compare_op=ALU.not_equal, fill=1.0, base=0,
                                    pattern=[[-1, P]], channel_multiplier=1).then_inc(consts_done, 1)
            pool.wait_ge(consts_done, 1)
            nc.gpsimd.memset(ones_row[:, :], 1.0).then_inc(consts_done, 1)
            pool.wait_ge(consts_done, 2)
            nc.gpsimd.memset(w_pool_bd[:, :, :], 0.0).then_inc(bd_zeroed, 1)
            pool.wait_ge(bd_zeroed, 1)
            nc.gpsimd.memset(h_pad[:, :, 0:PAD], 0.0).then_inc(consts_done, 1)
            pool.wait_ge(consts_done, 3)
            for g, window in enumerate((2, 4, 8, 16)):
                rows = slice(64 * (g % 2), 64 * (g % 2) + 64)
                for t in range(window - 1):
                    link(nc.gpsimd.memset(inv_count[rows, g // 2, t:t + 1], 1.0 / (t + 1)))
                link(nc.gpsimd.memset(inv_count[rows, g // 2, window - 1:16], 1.0 / window))

            def shifted_sum(dst, src, shift, rows=slice(0, P)):
                link(nc.gpsimd.tensor_copy(dst[rows, 0:shift], src[rows, 0:shift]))
                link(nc.gpsimd.tensor_tensor(dst[rows, shift:SEQ], src[rows, shift:SEQ], src[rows, 0:SEQ - shift],
                                             ALU.add))

            def window_mean(c, half, total):
                rows = slice(64 * half, 64 * half + 64)
                first = total[rows, 0:16]
                link(nc.gpsimd.tensor_tensor(first, first, inv_count[rows, c, :], ALU.mult))
                link(nc.gpsimd.tensor_scalar(total[rows, 16:SEQ], total[rows, 16:SEQ], inv_count[rows, c, 15:16], None,
                                             ALU.mult))
                z = z_pool[rows, c, :]
                ins = nc.gpsimd.tensor_tensor(z, total[rows, :], z, ALU.subtract)
                if half == 1:
                    ins.then_inc(pooled_done, 1)
                    pool.wait_ge(pooled_done, c + 1)
                else:
                    link(ins)

            def mask_bias(pair):
                pool.wait_ge(bias_in[pair % 2], 32 * (pair // 2 + 1))
                link(nc.gpsimd.memset(bias_rev[pair % 2][0:64, :, 0:CHUNK], MASKED))
                nc.gpsimd.memset(bias_rev[pair % 2][64:P, :, BAND - CHUNK:BAND], MASKED).then_inc(bias_ready, 1)
                pool.wait_ge(bias_ready, pair + 1)

            pool.wait_ge(z_done, KT)
            a, b = mid[:, 3, :], mid[:, 4, :]
            pool.wait_ge(zp_done, 1)
            z = z_pool[:, 0, :]
            shifted_sum(a, z, 1)
            shifted_sum(b, a, 2, slice(64, P))
            window_mean(0, 0, a)
            window_mean(0, 1, b)
            mask_bias(0)
            pool.wait_ge(zp_done, 2)
            z = z_pool[:, 1, :]
            shifted_sum(a, z, 1)
            shifted_sum(b, a, 2)
            shifted_sum(a, b, 4)
            shifted_sum(b, a, 8, slice(64, P))
            window_mean(1, 0, a)
            window_mean(1, 1, b)
            for pair in range(1, PAIRS):
                mask_bias(pair)
            pool.wait_ge(gates_done, 4)
            pool.wait_ge(ff2b_in, 16)
            nc.gpsimd.tensor_tensor(ff2_bias[:, :], ff2_bias[:, :], gate_ff[:, :], ALU.mult).then_inc(ff2b_scaled, 1)
            pool.wait_ge(ff2b_scaled, 1)
            pool.wait_ge(ln_in, 32)
            for t in range(ST + 1):
                if t < ST:
                    pool.wait_ge(mix_scaled, t + 1)
                    nc.gpsimd.tensor_tensor(mid[:, t, :], mix_tmp[t % 2][:, :], ln_b[:, :], ALU.add).then_inc(x1_done, 1)
                    pool.wait_ge(x1_done, t + 1)
                if t >= 1:
                    pool.wait_ge(x1_scaled, t)
                    row = mid[:, t - 1, :]
                    nc.gpsimd.tensor_tensor(row, row, ff2_bias[:, :], ALU.add).then_inc(res_done, 1)
                    pool.wait_ge(res_done, t)
            for t in range(ST - 1):
                pool.wait_ge(y_scaled, t + 1)
                tile = tmp[t % 2][:, :]
                nc.gpsimd.tensor_tensor(tile, tile, ln_b[:, :], ALU.add).then_inc(y_ready, 1)
                pool.wait_ge(y_ready, t + 1)

        half_after = {}
        for r in range(6):
            half_after[-(-24 * (r + 1) // PER_STEP) - 1] = r
        early_per_step = EARLY * 48 // STEPS
        early_after = {24 * (r + 1) // early_per_step - 1: r for r in range(2 * EARLY)}

        def half_of(pair, i):
            if pair < PAIRS - 1 and i in half_after:
                return pair + 1, half_after[i]
            if pair == PAIRS - 1 and i in early_after:
                return PAIRS, early_after[i]
            return None

        def pool_mix_unit(a):
            u = (a - MIX_STEP) // 2
            return u if a >= MIX_STEP and a % 2 == 0 and u < 4 else None

        @block.scalar
        def _(act):
            def copy(out, in_, **kw):
                return nc.scalar.activation(out, in_, ACT.Copy, **kw)

            def cut_hi(n):
                act.wait_ge(w_arrived[n % 2], arrived(n))
                if n >= 2:
                    act.wait_ge(*block_used(n - 2))
                copy(w_hi[n % 2][:, :, :], w_raw[n % 2][:, :, :]).then_inc(w_hi_done, 1)

            def take_root(count, t):
                act.wait_ge(var_done, count + 1)
                nc.scalar.activation(rstd[:, t:t + 1], rstd[:, t:t + 1], ACT.Sqrt).then_inc(std_done, 1)

            def norm(count, t, tile):
                act.wait_ge(norm_ready, count + 1)
                nc.scalar.activation(tile, mid[:, t, :], ACT.Identity, bias=neg_mean[:, t:t + 1],
                                     scale=rstd[:, t:t + 1]).then_inc(normed, 1)

            act.wait_ge(c_in, 16)
            nc.scalar.activation(c_sig[:, :], c_raw[:, :], ACT.Sigmoid).then_inc(c_sig_done, 1)
            for i in range(ST + 1):
                if i < ST:
                    take_root(i, i)
                if i >= 1:
                    norm(i - 1, i - 1, mid[:, i - 1, :])
            cut_hi(0)
            cut_hi(1)
            for k in range(KT):
                if k == 0:
                    act.wait_ge(mod_done, 1)
                if k >= 2:
                    act.wait_ge(u_lo_done, k - 1)
                act.wait_ge(z_done, k + 1)
                nc.scalar.activation(u_tmp[k % 2][:, :], banks(2 * (k % 2)), ACT.Identity, bias=mod[:, k:k + 1],
                                     scale=mod[:, KT + k:KT + k + 1]).then_inc(u_tmp_done, 1)
            for n in range(N_P1):
                act.wait_ge(z_done, KT + n + 1)
                src = banks(4 if n == 0 else 2 * (n % 2))
                if n in (0, 2):
                    if n == 0:
                        act.wait_ge(u_lo_done, KT)
                    else:
                        act.wait_ge(glu_done, 1)
                    nc.scalar.activation(glu_gate[:, :], src, ACT.Sigmoid).then_inc(glu_sig_done, 1)
                if n >= 4:
                    copy(z_pool[:, n - 4, :], src).then_inc(zp_done, 1)
                cut_hi(n + 2)

            def take_half(pair, r):
                hz = 6 * pair + r
                part, half = divmod(r, 2)
                cs = slice(half * HALF, (half + 1) * HALF)
                src = ps[:, r % 2, :]
                act.wait_ge(h_done, hz + 1)
                if pair == PAIRS:
                    act.wait_ge(pm_scaled, 4)
                    copy(gate_z[part][:, cs], src).then_inc(h_free[r % 2], 1)
                elif part == 0:
                    if pair >= 2:
                        act.wait_ge(scores_done, STEPS * (pair - 1))
                    elif pair == 0:
                        act.wait_ge(partial_done, 10 - N_DIRECT)
                    else:
                        act.wait_ge(partial_done, 12 - N_DIRECT)
                    copy(q_hi[pair % 2][:, cs], src, scale=HEAD_DIM ** -0.5).then_inc(half_hi, 1)
                elif part == 1:
                    copy(k_hi[pair % 2][:, cs], src).then_inc(half_hi, 1)
                else:
                    copy(mid[:, 5, cs], src).then_inc(h_free[r % 2], 1)
                if r in (1, 3, 5):
                    cut_hi(N_P1 + 3 * pair + part + 2)

            def take_v(pair, half):
                act.wait_ge(vt_done, 2 * pair + half + 1)
                act.wait_ge(partial_done, 12 - N_DIRECT)
                if pair >= 2:
                    act.wait_ge(pv_done, ST * (pair - 1))
                copy(v_hi[pair % 2][:, 4 * half:4 * half + 4, :], ps[:, 3, :].rearrange("p (t d) -> p t d", d=P))\
                    .then_inc(vt_hi, 1)

            for r in range(6):
                take_half(0, r)
            N_STEPS = PAIRS * STEPS
            for a in range(N_STEPS + 2):
                pair, i = divmod(a, STEPS)
                if a < N_STEPS:
                    col, width = a % (2 * STEPS), P * blocks_of(i // 2)
                    act.wait_ge(biased, a + 1)
                    nc.scalar.activation(probs[a % 2][:, 0:width], probs[a % 2][:, 0:width], ACT.Exp,
                                         bias=neg_max[:, col:col + 1], scale=-1.0,
                                         accum_out=row_sum[:, col:col + 1]).then_inc(exp_done, 1)
                if a < N_STEPS and i < 2:
                    take_v(pair, i)
                if a >= 3 and a % 2 == 1:
                    tile = (a - 3) // 2
                    act.wait_ge(pv_done, tile + 1)
                    if tile == ST:
                        act.wait_ge(pooled_done, 2)
                    ts = slice(tile % ST * P, (tile % ST + 1) * P)
                    for h in range(2):
                        rows = slice(h * HEAD_DIM, (h + 1) * HEAD_DIM)
                        copy(mid[rows, 2 + tile // ST, ts], ps[rows, 2, h * P:(h + 1) * P]).then_inc(o_copied, 1)
                if 1 <= a <= N_STEPS:
                    b = a - 1
                    nb = blocks_of(b % STEPS // 2)
                    act.wait_ge(pt_done, b + 1)
                    if b >= 2:
                        act.wait_ge(pv_done, b // 2)
                    copy(pt_hi[:, 0:nb, b % 2, :], banks(6)[:, 0:nb * P].rearrange("p (b q) -> p b q", q=P))\
                        .then_inc(pt_hi_done, 1)
                if pool_mix_unit(a) is not None:
                    t, half = divmod(pool_mix_unit(a), 2)
                    act.wait_ge(pm_done, 2 * t + half + 1)
                    copy(mid[:, t, half * HALF:(half + 1) * HALF], ps[:, 3, :],
                         scale=cols[:, R_PSC + t:R_PSC + t + 1]).then_inc(pm_scaled, 1)
                if half_of(pair, i):
                    take_half(*half_of(pair, i))

            def cut_branch_hi(k):
                copy(br_hi[:, k, :], mid[:, k, :]).then_inc(br_hi_done, 1)

            act.wait_ge(o_copied, N_STEPS)
            act.wait_ge(pt_lo_done, N_STEPS)
            for t in range(2):
                act.wait_ge(centred, t + 1)
                nc.scalar.activation(sq[:, t, :], mid[:, 6 + t, :], ACT.Square).then_inc(squared, 1)
            for k in range(4):
                cut_branch_hi(k)
            act.wait_ge(cvar_read, 1)
            nc.scalar.activation(conv_std[:, :], conv_std[:, :], ACT.Sqrt).then_inc(cstd_done, 1)
            cut_branch_hi(4)
            cut_branch_hi(5)
            for t in range(2):
                act.wait_ge(cnormed, 2 if t == 1 else 1)
                nc.scalar.activation(conv_sig[t][:, :], mid[:, 6 + t, :], ACT.Sigmoid,
                                     bias=cols[:, R_CLNB + t:R_CLNB + t + 1],
                                     scale=cols[:, R_CLNG + t:R_CLNG + t + 1]).then_inc(conv_sig_done, 1)
            for t in range(2):
                act.wait_ge(conv_done, t + 1)
                cut_branch_hi(6 + t)

            def gate_sigmoid(j, b, src):
                nc.scalar.activation(gate[b][:, :], src, ACT.Sigmoid,
                                     bias=cols[:, bass.ds(j + (R_GATE + 8 * b), 1)]).then_inc(sig_done, 1)

            def cut_gate_hi(j, b):
                act.wait_ge(w_arrived[b % 2], gate_arrived(j, b + 2) if b < 2 else gate_arrived(j + 1, b - 2))
                copy(w_hi[b % 2][:, :, :], w_raw[b % 2][:, :, :]).then_inc(w_hi_done, 1)

            for b in range(EARLY):
                gate_sigmoid(0, b, gate_z[b][:, :])
            act.wait_ge(g_done, 1)
            act.wait_ge(sig_done, EARLY)
            gate_sigmoid(0, 2, banks(0))
            cut_gate_hi(0, 2)
            act.wait_ge(y_done, 3)
            cut_gate_hi(0, 3)

            def gate_step(j):
                for b in range(3):
                    act.wait_ge(g_done, j * 3 + (b + 1 - EARLY))
                    if b == 0:
                        act.wait_ge(w_lo_done, j * 4 + (N_GATE0 + 2))
                    gate_sigmoid(j, b, banks(2 * (b % 2)))
                    cut_gate_hi(j, b)

            with act.Fori(1, KT - 1) as j:
                gate_step(j)
                act.wait_ge(y_done, j * 3 + 3)
                cut_gate_hi(j, 3)
            gate_step(KT - 1)

            def cut_merged_hi(k):
                act.wait_ge(merged_step, 3 * (k + 1))
                copy(act_hi[:, k, :], mid[:, k, :]).then_inc(mg_hi_done, 1)

            act.wait_ge(g_done, 3 * KT - EARLY)
            for k in range(KT - 1):
                cut_merged_hi(k)
            act.wait_ge(y_done, 3 * KT)
            for k in range(KT):
                act.wait_ge(row_in[k % 2], 16 * (k // 2 + 1))
                copy(br_hi[:, k, :], row_raw[k % 2][:, :]).then_inc(row_hi_done, 1)
                if k == 1:
                    cut_merged_hi(KT - 1)
                if k == 2:
                    cut_gate_hi(KT - 1, 3)

            for t in range(ST + 2):
                if t < ST:
                    take_root(first_norm(t), t)
                if 1 <= t <= ST:
                    take_root(second_norm(t - 1), t - 1)
                if t < ST:
                    norm(first_norm(t), t, mix_tmp[t % 2][:, :])
                if 1 <= t <= ST:
                    q = t - 1
                    if q >= 2:
                        act.wait_ge(x2_lo_done, q - 1)
                    norm(second_norm(q), q, tmp[q % 2][:, :])
                    copy(mid[:, q, :], mid[:, q, :], scale=ALPHA).then_inc(x1_scaled, 1)
                if t >= 2:
                    q = t - 2
                    act.wait_ge(x2t_done, q + 1)
                    for k in range(KT):
                        ins = nc.scalar.activation(tmp[q % 2][:, k * P:(k + 1) * P],
                                                   banks(4 + 2 * (q % 2))[:, k * P:(k + 1) * P], ACT.Identity,
                                                   bias=mod[:, 24 + k:25 + k], scale=mod[:, 32 + k:33 + k])
                    ins.then_inc(x2_tmp_done, 1)
                    act.wait_ge(x2_tmp_done, q + 1)
                    copy(act_hi[:, :, q * P:(q + 1) * P], tmp[q % 2][:, :].rearrange("p (k s) -> p k s", s=P))\
                        .then_inc(x2_hi_done, 1)

            def mlp_group(g, last):
                for t in range(GROUP):
                    act.wait_ge(f1_done, g * GROUP + (t + 1))
                    if t >= 2:
                        act.wait_ge(h_lo_done, g * GROUP + (t - 1))
                    nc.scalar.activation(tmp[t % 2][:, :], banks(2 * (t % 2)), ACT.Relu,
                                         bias=cols[:, bass.ds(g * GROUP + (R_FF1 + t), 1)]).then_inc(relu_done, 1)
                    act.wait_ge(relu_done, g * GROUP + (t + 1))
                    nc.scalar.activation(tmp[t % 2][:, :], tmp[t % 2][:, :], ACT.Square).then_inc(sq_done, 1)
                    act.wait_ge(sq_done, g * GROUP + (t + 1))
                    copy(h_hi[:, t, :], tmp[t % 2][:, :]).then_inc(h_hi_done, 1)
                    if not (last and t >= 2):
                        act.wait_ge(w_arrived[t % 2], ff_arrived(g, t + 2))
                        copy(w_hi[t % 2][:, :, :], w_raw[t % 2][:, :, :]).then_inc(w_hi_done, 1)
                    act.wait_ge(row_scaled, g * GROUP + (t + 1))
                    copy(w2_hi[:, t, :], row_raw[t % 2][:, :]).then_inc(row_hi_done, 1)

            with act.Fori(0, GROUPS - 1) as g:
                mlp_group(g, False)
            mlp_group(GROUPS - 1, True)
            for t in range(ST):
                if t >= 2:
                    act.wait_ge(stored[t % 2], 16 * (t // 2))
                take_root(3 * ST + t, t)
                norm(3 * ST + t, t, tmp[t % 2][:, :])

        @block.vector
        def _(dve):
            steps = [0]

            def link(ins, offset=0):
                steps[0] += 1
                ins.then_inc(dve_step, 1)
                dve.wait_ge(dve_step, offset + steps[0])

            def cut_lo(n):
                dve.wait_ge(w_hi_done, n + 1)
                nc.vector.tensor_tensor(w_lo[n % 2][:, :, :], w_raw[n % 2][:, :, :], f(w_hi[n % 2][:, :, :]),
                                        ALU.subtract).then_inc(w_lo_done, 1)

            def stats(src, t):
                for half in range(2):
                    ins = nc.vector.bn_stats(bn[:, 6 * half:6 * half + 6], src[:, half * HALF:(half + 1) * HALF])
                link(ins)
                link(nc.vector.bn_aggr(mean_var[:, t, :], bn[:, :]))
                nc.vector.tensor_scalar_add(rstd[:, t:t + 1], mean_var[:, t, 1:2], EPS).then_inc(var_done, 1)

            def scale_bias(count, t):
                dve.wait_ge(std_done, count + 1)
                link(nc.vector.reciprocal(rstd[:, t:t + 1], rstd[:, t:t + 1]))
                nc.vector.scalar_tensor_tensor(out=neg_mean[:, t:t + 1], in0=mean_var[:, t, 0:1], scalar=-1.0,
                                               in1=rstd[:, t:t + 1], op0=ALU.mult, op1=ALU.mult)\
                    .then_inc(norm_ready, 1)

            dve.wait_ge(c_sig_done, 1)
            nc.vector.tensor_tensor(c_act[:, :], c_raw[:, :], c_sig[:, :], ALU.mult).then_inc(c_act_done, 1)
            dve.wait_ge(c_act_done, 1)
            for i in range(ST):
                dve.wait_ge(x_in[i], 16)
                stats(mid[:, i, :], i)
                if i >= 1:
                    scale_bias(i - 1, i - 1)
            scale_bias(ST - 1, ST - 1)

            def ada_chunk(i):
                dve.wait_ge(ada_in[i % 3], 16 * (i // 3 + 1))
                if i >= 2 + N_DIRECT:
                    dve.wait_ge(reduced, i - 1)
                dst, src = partial[i % 2][:, :], ada[i % 3]
                link(nc.vector.tensor_scalar(dst, src[:, 0, :], c_act[:, 0:1], None, ALU.mult))
                for k in range(1, 8):
                    if i == 3 and k == 4:
                        dve.wait_ge(ada3_end_in, 16)
                    ins = nc.vector.scalar_tensor_tensor(out=dst, in0=src[:, k, :], scalar=c_act[:, k:k + 1], in1=dst,
                                                         op0=ALU.mult, op1=ALU.add)
                    if k < 7:
                        link(ins)
                ins.then_inc(partial_done, 1)

            def gate_chunk(i):
                dve.wait_ge(reduced, i + 1)
                dve.wait_ge(ada_bias_in, 32)
                half = slice(i % 2 * HALF, i % 2 * HALF + HALF)
                dst = (gate_mix if i < 6 else gate_ff)[:, half]
                nc.vector.tensor_tensor(dst, ps[:, 4 + i % 2, :], dst, ALU.add).then_inc(gates_done, 1)

            def mod_columns(c0, bank):
                link(nc.vector.tensor_tensor(mod[:, c0:c0 + 16], ps[:, bank, 0:16], cols[:, c0:c0 + 16], ALU.add))
                nc.vector.tensor_scalar_add(mod[:, c0 + 8:c0 + 16], mod[:, c0 + 8:c0 + 16], 1.0).then_inc(mod_done, 1)

            dve.wait_ge(cols_t, 2)
            nc.vector.tensor_copy(cols[:, 0:ROWS_A], ps[:, 4, 0:ROWS_A])
            nc.vector.tensor_copy(cols[:, ROWS_A:ROWS_A + ROWS_C], ps[:, 5, 0:ROWS_C]).then_inc(cols_done, 1)
            for i in range(N_DIRECT, 4):
                ada_chunk(i)
            dve.wait_ge(rel_in, 16)
            nc.vector.tensor_copy(rel_ext[:, 2 * REL_CLIP:768],
                                  rel_ext[:, 2 * REL_CLIP - 1:2 * REL_CLIP].to_broadcast([HEADS, 768 - 2 * REL_CLIP]))\
                .then_inc(rel_done, 1)
            dve.wait_ge(cols_done, 1)
            cut_lo(0)
            cut_lo(1)
            dve.wait_ge(reduced, 4)
            mod_columns(0, 6)
            for k in range(KT):
                dve.wait_ge(u_tmp_done, k + 1)
                link(nc.vector.tensor_copy(act_hi[:, k, :], u_tmp[k % 2][:, :]))
                nc.vector.tensor_tensor(act_lo[:, k, :], u_tmp[k % 2][:, :], f(act_hi[:, k, :]), ALU.subtract)\
                    .then_inc(u_lo_done, 1)
            for n in range(N_P1):
                ada_chunk(4 + n)
                if n in (1, 3):
                    t = n // 2
                    dve.wait_ge(z_done, KT + n + 1)
                    dve.wait_ge(glu_sig_done, t + 1)
                    dve.wait_ge(consts_done, 3)
                    nc.vector.tensor_tensor(h_pad[:, t, PAD:PAD + SEQ], banks(2), glu_gate[:, :], ALU.mult)\
                        .then_inc(glu_done, 1)
                cut_lo(n + 2)
                if n in (2, 3):
                    gate_chunk(n + 2)

            def take_half_lo(pair, r):
                part, half = divmod(r, 2)
                cs = slice(half * HALF, (half + 1) * HALF)
                src, s = ps[:, r % 2, :], pair % 2
                if part < 2 and pair < PAIRS:
                    dve.wait_ge(half_hi, 4 * pair + r + 1)
                    if part == 0:
                        ins = nc.vector.scalar_tensor_tensor(out=q_lo[s][:, cs], in0=src, scalar=HEAD_DIM ** -0.5,
                                                             in1=f(q_hi[s][:, cs]), op0=ALU.mult, op1=ALU.subtract)
                    else:
                        ins = nc.vector.tensor_tensor(k_lo[s][:, cs], src, f(k_hi[s][:, cs]), ALU.subtract)
                    ins.then_inc(h_free[r % 2], 1)
                if r in (1, 3, 5):
                    cut_lo(N_P1 + 3 * pair + part + 2)

            def take_v_lo(pair, half):
                dve.wait_ge(vt_hi, 2 * pair + half + 1)
                s, ts = pair % 2, slice(4 * half, 4 * half + 4)
                nc.vector.tensor_tensor(v_lo[s][:, ts, :], ps[:, 3, :].rearrange("p (t d) -> p t d", d=P),
                                        f(v_hi[s][:, ts, :]), ALU.subtract).then_inc(vt_free, 1)

            def conv_tap(n):
                t, tap = divmod(n, TAPS)
                w = cols[:, ROWS_A + 2 * tap + t:ROWS_A + 2 * tap + t + 1]
                src, acc = h_pad[:, t, tap:tap + SEQ], mid[:, 6 + t, :]
                if tap == 0:
                    nc.vector.tensor_scalar(acc, src, w, cols[:, R_CONVB + t:R_CONVB + t + 1], ALU.mult, ALU.add)\
                        .then_inc(tap_done, 1)
                else:
                    dve.wait_ge(tap_done, n)
                    nc.vector.scalar_tensor_tensor(out=acc, in0=src, scalar=w, in1=acc, op0=ALU.mult, op1=ALU.add)\
                        .then_inc(tap_done, 1)

            dve.wait_ge(glu_done, 2)
            for r in range(6):
                if r in (0, 2):
                    ada_chunk(10 + r // 2)
                if r in (3, 5):
                    gate_chunk(10 + r // 4)
                take_half_lo(0, r)
                if r == 2:
                    dve.wait_ge(reduced, 10)
                    mod_columns(24, 7)
            N_STEPS = PAIRS * STEPS
            for a in range(N_STEPS + 1):
                pair, i = divmod(a, STEPS)
                if a < N_STEPS:
                    col, width = a % (2 * STEPS), P * blocks_of(i // 2)
                    dve.wait_ge(scores_done, a + 1)
                    if i == 0:
                        dve.wait_ge(bias_ready, pair + 1)
                    if a >= 2:
                        dve.wait_ge(pt_done, a - 1)
                    nb = blocks_of(i // 2)
                    bias = bias_rev[pair % 2][:, i % 2, 0:width][:, ::-1]
                    nc.vector.tensor_tensor_reduce(out=like_scores(probs[a % 2][:, 0:width], nb), in0=score_cols(nb),
                                                   in1=like_scores(bias, nb),
                                                   scale=-1.0, scalar=3e38, op0=ALU.add, op1=ALU.min,
                                                   accum_out=neg_max[:, col:col + 1]).then_inc(biased, 1)
                if a < N_STEPS and i < 2:
                    take_v_lo(pair, i)
                if a < 2 * TAPS:
                    conv_tap(a)
                if a < N_STEPS:
                    dve.wait_ge(exp_done, a + 1)
                    link(nc.vector.reciprocal(inv_sum[:, col:col + 1], row_sum[:, col:col + 1]))
                    nc.vector.tensor_scalar(probs[a % 2][:, 0:width], probs[a % 2][:, 0:width],
                                            inv_sum[:, col:col + 1], None, ALU.mult).then_inc(probs_done, 1)
                if a >= 1:
                    b = a - 1
                    nb = blocks_of(b % STEPS // 2)
                    dve.wait_ge(pt_hi_done, b + 1)
                    nc.vector.tensor_tensor(pt_lo[:, 0:nb, b % 2, :],
                                            banks(6)[:, 0:nb * P].rearrange("p (b q) -> p b q", q=P),
                                            f(pt_hi[:, 0:nb, b % 2, :]), ALU.subtract).then_inc(pt_lo_done, 1)
                if half_of(pair, i):
                    take_half_lo(*half_of(pair, i))

            def cut_branch_lo(k):
                dve.wait_ge(br_hi_done, k + 1)
                nc.vector.tensor_tensor(br_lo[:, k, :], mid[:, k, :], f(br_hi[:, k, :]), ALU.subtract)\
                    .then_inc(br_lo_done, 1)

            dve.wait_ge(cmean_done, 1)
            for t in range(2):
                acc = mid[:, 6 + t, :]
                nc.vector.scalar_tensor_tensor(out=acc, in0=banks(4), scalar=-1.0 / D_CONV, in1=acc,
                                               op0=ALU.mult, op1=ALU.add).then_inc(centred, 1)
            cut_branch_lo(0)
            cut_branch_lo(1)
            dve.wait_ge(cvar_done, 1)
            nc.vector.tensor_scalar(conv_std[:, :], banks(2), 1.0 / D_CONV, EPS, ALU.mult, ALU.add)\
                .then_inc(cvar_read, 1)
            for k in range(2, 6):
                cut_branch_lo(k)
            dve.wait_ge(cstd_done, 1)
            link(nc.vector.reciprocal(conv_std[:, :], conv_std[:, :]))
            dve.wait_ge(centred, 2)
            dve.wait_ge(squared, 2)
            for t in range(2):
                acc = mid[:, 6 + t, :]
                nc.vector.tensor_tensor(acc, acc, conv_std[:, :], ALU.mult).then_inc(cnormed, 1)
            for t in range(2):
                acc = mid[:, 6 + t, :]
                dve.wait_ge(conv_sig_done, t + 1)
                link(nc.vector.tensor_scalar(acc, acc, cols[:, R_CLNG + t:R_CLNG + t + 1],
                                             cols[:, R_CLNB + t:R_CLNB + t + 1], ALU.mult, ALU.add))
                nc.vector.tensor_tensor(acc, acc, conv_sig[t][:, :], ALU.mult).then_inc(conv_done, 1)
                cut_branch_lo(6 + t)

            def cut_gate_lo(j, b):
                dve.wait_ge(w_hi_done, j * 4 + (N_GATE0 + b + 3))
                nc.vector.tensor_tensor(w_lo[b % 2][:, :, :], w_raw[b % 2][:, :, :], f(w_hi[b % 2][:, :, :]),
                                        ALU.subtract).then_inc(w_lo_done, 1)

            def gate_product(j, y):
                dve.wait_ge(y_done, j * 3 + (y + 1))
                dve.wait_ge(sig_done, j * 3 + (y + 1))
                dst = mid[:, bass.ds(j, 1), :].rearrange("p o s -> p (o s)") if y == 0 else tmp[y - 1][:, :]
                nc.vector.tensor_tensor(dst, banks((4, 6, 2)[y]), gate[y][:, :], ALU.mult).then_inc(y_used, 1)

            def add_product(j, y):
                out_tile = mid[:, bass.ds(j, 1), :].rearrange("p o s -> p (o s)")
                dve.wait_ge(y_used, j * 3 + (y + 1))
                if y == 2:
                    dve.wait_ge(merged_step, j * 3 + 1)
                nc.vector.tensor_tensor(out_tile, out_tile, tmp[y - 1][:, :], ALU.add).then_inc(merged_step, y)

            def merge(j):
                for y in range(3):
                    gate_product(j, y)
                    if y > 0:
                        add_product(j, y)

            cut_gate_lo(0, 2)
            merge(0)
            cut_gate_lo(0, 3)
            with dve.Fori(1, KT - 1) as j:
                for b in range(4):
                    if b == 3:
                        merge(j)
                    cut_gate_lo(j, b)

            def cut_merged_lo(k):
                dve.wait_ge(mg_hi_done, k + 1)
                nc.vector.tensor_tensor(act_lo[:, k, :], mid[:, k, :], f(act_hi[:, k, :]), ALU.subtract)\
                    .then_inc(mg_lo_done, 1)

            def cut_row_lo(k):
                dve.wait_ge(row_hi_done, k + 1)
                nc.vector.tensor_tensor(br_lo[:, k, :], row_raw[k % 2][:, :], f(br_hi[:, k, :]), ALU.subtract)\
                    .then_inc(row_lo_done, 1)

            last = KT - 1
            for b in range(3):
                cut_gate_lo(last, b)
            for k in range(3):
                cut_merged_lo(k)
            gate_product(last, 0)
            for k in range(3, 6):
                cut_merged_lo(k)
            gate_product(last, 1)
            add_product(last, 1)
            cut_merged_lo(6)
            gate_product(last, 2)
            cut_row_lo(0)
            add_product(last, 2)
            cut_row_lo(1)
            cut_merged_lo(last)
            cut_row_lo(2)
            cut_gate_lo(last, 3)
            for k in range(3, KT):
                cut_row_lo(k)

            def cut_x2(t):
                dve.wait_ge(x2_hi_done, t + 1)
                nc.vector.tensor_tensor(act_lo[:, :, t * P:(t + 1) * P],
                                        tmp[t % 2][:, :].rearrange("p (k s) -> p k s", s=P),
                                        f(act_hi[:, :, t * P:(t + 1) * P]), ALU.subtract).then_inc(x2_lo_done, 1)

            dve.wait_ge(ln_in, 32)
            dve.wait_ge(ff2b_scaled, 1)
            for t in range(ST + 2):
                scratch = mix_tmp[t % 2][:, :]
                if t < ST:
                    row = mid[:, t, :]
                    dve.wait_ge(mix_done, t + 1)
                    if t >= 2:
                        dve.wait_ge(x1_done, t - 1)
                    nc.vector.tensor_tensor(scratch, banks(2 * (t % 2)), gate_mix[:, :], ALU.mult)\
                        .then_inc(mix_free, 1)
                    dve.wait_ge(mix_free, t + 1)
                    dve.wait_ge(res_in[t], 16)
                    link(nc.vector.scalar_tensor_tensor(out=row, in0=row, scalar=ALPHA, in1=scratch,
                                                        op0=ALU.mult, op1=ALU.add))
                    stats(row, t)
                if 1 <= t <= ST:
                    dve.wait_ge(x1_done, t)
                    stats(mid[:, t - 1, :], t - 1)
                if t >= 3:
                    cut_x2(t - 3)
                if t < ST:
                    scale_bias(first_norm(t), t)
                if 1 <= t <= ST:
                    scale_bias(second_norm(t - 1), t - 1)
                if t < ST:
                    dve.wait_ge(normed, first_norm(t) + 1)
                    nc.vector.tensor_tensor(scratch, scratch, ln_g[:, :], ALU.mult).then_inc(mix_scaled, 1)
            cut_x2(ST - 1)
            dve.wait_ge(res_done, ST)

            def mlp_group(g, last):
                for t in range(GROUP):
                    row = row_raw[t % 2]
                    dve.wait_ge(row_in[t % 2], g * (16 * GROUP // 2) + (16 * KT // 2 + 16 * (t // 2 + 1)))
                    nc.vector.tensor_tensor(row[:, :], row[:, :], gate_ff[:, :], ALU.mult).then_inc(row_scaled, 1)
                    dve.wait_ge(row_scaled, g * GROUP + (t + 1))
                    dve.wait_ge(h_hi_done, g * GROUP + (t + 1))
                    nc.vector.tensor_tensor(h_lo[:, t, :], tmp[t % 2][:, :], f(h_hi[:, t, :]), ALU.subtract)\
                        .then_inc(h_lo_done, 1)
                    if not (last and t >= 2):
                        dve.wait_ge(w_hi_done, g * GROUP + (N_FF0 + t + 3))
                        nc.vector.tensor_tensor(w_lo[t % 2][:, :, :], w_raw[t % 2][:, :, :],
                                                f(w_hi[t % 2][:, :, :]), ALU.subtract).then_inc(w_lo_done, 1)
                    dve.wait_ge(row_hi_done, g * GROUP + (KT + t + 1))
                    nc.vector.tensor_tensor(w2_lo[:, t, :], row[:, :], f(w2_hi[:, t, :]), ALU.subtract)\
                        .then_inc(row_lo_done, 1)
                for t in range(ST):
                    dve.wait_ge(f2_done, g * ST + (t + 1))
                    nc.vector.tensor_tensor(mid[:, t, :], mid[:, t, :], banks(4 + 2 * (t % 2)), ALU.add)\
                        .then_inc(acc_done, 1)
                    if last:
                        dve.wait_ge(acc_done, g * ST + (t + 1))
                        stats(mid[:, t, :], t)
                        if t >= 1:
                            finish_tile(t - 1)
                        scale_bias(3 * ST + t, t)
                if last:
                    finish_tile(ST - 1)

            def finish_tile(t):
                dve.wait_ge(normed, 3 * ST + t + 1)
                if t == 0:
                    dve.wait_ge(ln2_in, 32)
                tile = tmp[t % 2][:, :]
                nc.vector.tensor_tensor(tile, tile, ln_g[:, :], ALU.mult).then_inc(y_scaled, 1)
                if t == ST - 1:
                    dve.wait_ge(y_scaled, ST)
                    dve.wait_ge(y_ready, ST - 1)
                    nc.vector.tensor_tensor(tile, tile, ln_b[:, :], ALU.add).then_inc(y_ready, 1)

            with dve.Fori(0, GROUPS - 1) as g:
                mlp_group(g, False)
            mlp_group(GROUPS - 1, True)

        @block.tensor
        def _(pe):
            def product(out, parts, first, last):
                (sh, sl), (mh, ml) = parts
                nc.tensor.matmul(out, sh, mh, start=first, stop=False)
                nc.tensor.matmul(out, sh, ml, start=False, stop=False)
                return nc.tensor.matmul(out, sl, mh, start=False, stop=last)

            def act_part(k, cs):
                return act_hi[:, k, cs], act_lo[:, k, cs]

            def w_part(n, k):
                return w_hi[n % 2][:, k, :], w_lo[n % 2][:, k, :]

            def half_cols(h):
                return slice(h * HALF, (h + 1) * HALF)

            pe.wait_ge(consts_done, 2)

            def direct_chunk(i):
                pe.wait_ge(ada_in[i], 16)
                for m in range(4):
                    for k in range(8):
                        ins = nc.tensor.matmul(ps[:, 6, 4 * i + m:4 * i + m + 1], ada[i][:, k, m * P:(m + 1) * P],
                                               c_act[:, k:k + 1], start=k == 0, stop=k == 7)
                ins.then_inc(reduced, 1)

            def reduce_chunk(i):
                pe.wait_ge(partial_done, i + 1 - N_DIRECT)
                if i in (4, 5, 10, 11):
                    if i < 6:
                        pe.wait_ge(cols_done, 1)
                    else:
                        pe.wait_ge(gates_done, i - 9)
                    ins = nc.tensor.matmul(ps[:, 4 + i % 2, :], ones_row[:, :], partial[i % 2][:, :],
                                           start=True, stop=True)
                else:
                    bank, first = (6, 0) if i < 4 else (7, 6)
                    for m in range(4):
                        col = (i - first) * 4 + m
                        ins = nc.tensor.matmul(ps[:, bank, col:col + 1], partial[i % 2][:, m * P:(m + 1) * P],
                                               ones_row[:, 0:1], start=True, stop=True)
                ins.then_inc(reduced, 1)

            pe.wait_ge(c_act_done, 1)
            direct_chunk(0)
            direct_chunk(1)
            pe.wait_ge(small_in, 16 * 8)
            nc.tensor.transpose(ps[:, 4, 0:ROWS_A], rows_a[:, :], ident[0:ROWS_A, 0:ROWS_A]).then_inc(cols_t, 1)
            nc.tensor.transpose(ps[:, 5, 0:ROWS_C], rows_c[:, :], ident[0:ROWS_C, 0:ROWS_C]).then_inc(cols_t, 1)
            reduce_chunk(2)
            pe.wait_ge(normed, ST)
            def transpose_x(k):
                if k >= 2:
                    pe.wait_ge(u_tmp_done, k - 1)
                for i in range(ST):
                    ins = nc.tensor.transpose(ps[:, 2 * (k % 2) + i // 4, (i % 4) * P:(i % 4 + 1) * P],
                                              mid[:, i, k * P:(k + 1) * P], ident[:, :])
                ins.then_inc(z_done, 1)

            transpose_x(0)
            transpose_x(1)
            reduce_chunk(3)
            pe.wait_ge(w_lo_done, 1)
            pe.wait_ge(cols_done, 1)
            for k in range(KT):
                if k + 2 < KT:
                    transpose_x(k + 2)
                pe.wait_ge(u_lo_done, k + 1)
                for h in range(2):
                    ins = product(ps[:, 4 + h, :], (w_part(0, k), act_part(k, half_cols(h))), k == 0, k == KT - 1)
            ins.then_inc(z_done, 1)
            for n in range(1, N_P1):
                pe.wait_ge(w_lo_done, n + 1)
                if n in (1, 2):
                    pe.wait_ge(u_tmp_done, KT)
                elif n == 4:
                    pe.wait_ge(glu_sig_done, 2)
                else:
                    pe.wait_ge(glu_done, n // 2)
                for h in range(2):
                    for k in range(KT):
                        ins = product(ps[:, 2 * (n % 2) + h, :], (w_part(n, k), act_part(k, half_cols(h))),
                                      k == 0, k == KT - 1)
                ins.then_inc(z_done, 1)
                if n == 1:
                    pe.wait_ge(glu_sig_done, 1)
                reduce_chunk(3 + n)

            def project(pair, m):
                part, r = divmod(m, 48)
                half, kk = divmod(r, 24)
                k, term = divmod(kk, 3)
                n, hz = N_P1 + 3 * pair + part, 2 * part + half
                if r == 0:
                    pe.wait_ge(w_lo_done, n + 1)
                if kk == 0:
                    wait_bank(pair, hz)
                (sh, sl), (mh, ml) = w_part(n, k), act_part(k, half_cols(half))
                s, v = ((sh, mh), (sh, ml), (sl, mh))[term]
                ins = nc.tensor.matmul(ps[:, hz % 2, :], s, v, start=kk == 0, stop=kk == 23)
                if kk == 23:
                    ins.then_inc(h_done, 1)

            def wait_bank(pair, r):
                if pair == 0 and r < 2:
                    pe.wait_ge(zp_done, 1)
                else:
                    pe.wait_ge(h_free[r % 2], 3 * pair + r // 2)

            def transpose_v(pair, half):
                if half == 0:
                    for b in range(2):
                        pe.wait_ge(h_free[b], 3 * pair + 3)
                    if pair == 0:
                        pe.wait_ge(zp_done, 2)
                    elif pair * STEPS > MIX_STEP:
                        pe.wait_ge(pm_scaled, 4)
                if 2 * pair + half > 0:
                    pe.wait_ge(vt_free, 2 * pair + half)
                for t in range(4):
                    ts = slice((4 * half + t) * P, (4 * half + t + 1) * P)
                    ins = nc.tensor.transpose(ps[:, 3, t * P:(t + 1) * P], mid[:, 5, ts], ident[:, :])
                ins.then_inc(vt_done, 1)

            def scores(a):
                pair, i = divmod(a, STEPS)
                t, h = divmod(i, 2)
                nb = blocks_of(t)
                s, rows, qs = pair % 2, slice(h * HEAD_DIM, (h + 1) * HEAD_DIM), slice(t * P, (t + 1) * P)
                if i == 0:
                    for b in range(2):
                        pe.wait_ge(h_free[b], 3 * pair + 2)
                if a == 0:
                    pe.wait_ge(gates_done, 4)
                    pe.wait_ge(mod_done, 2)
                else:
                    pe.wait_ge(biased, a)
                first_key = (t + 1 - nb) * P
                parts = 2 if nb == BAND_BLOCKS else 1
                n = nb * P // parts
                for part in range(parts):
                    ks = slice(first_key + part * n, first_key + (part + 1) * n)
                    ins = product(ps[:, 4 + part, 0:n],
                                  ((q_hi[s][rows, qs], q_lo[s][rows, qs]), (k_hi[s][rows, ks], k_lo[s][rows, ks])),
                                  True, True)
                ins.then_inc(scores_done, 1)

            def transpose_probs(a):
                pe.wait_ge(probs_done, a + 1)
                if a >= 1:
                    pe.wait_ge(pt_lo_done, a)
                for b in range(blocks_of(a % STEPS // 2)):
                    ins = nc.tensor.transpose(banks(6)[:, b * P:(b + 1) * P], probs[a % 2][:, b * P:(b + 1) * P],
                                              ident[:, :])
                ins.then_inc(pt_done, 1)

            def weigh(tile):
                pair, t = divmod(tile, ST)
                nb = blocks_of(t)
                s = pair % 2
                pe.wait_ge(pt_lo_done, 2 * tile + 2)
                if t == 0:
                    pe.wait_ge(vt_free, 2 * pair + 2)
                if tile >= 1:
                    pe.wait_ge(o_copied, 2 * tile)
                else:
                    pe.wait_ge(zp_done, 2)
                for b in range(nb):
                    kt = t + 1 - nb + b
                    ins = product(ps[:, 2, 0:2 * P],
                                  ((v_hi[s][:, kt, :], v_lo[s][:, kt, :]), (pt_hi[:, b, :, :], pt_lo[:, b, :, :])),
                                  b == 0, b == nb - 1)
                ins.then_inc(pv_done, 1)

            for m in range(PROJ):
                project(0, m)
                if m in (23, 71, 119):
                    reduce_chunk(9 + m // 48)
            N_STEPS = PAIRS * STEPS
            def mix_pool(u):
                if u == 0:
                    pe.wait_ge(vt_free, 2 * (MIX_STEP // STEPS + 1))
                    pe.wait_ge(pooled_done, 2)
                    pe.wait_ge(pool_w_in, 64)
                else:
                    pe.wait_ge(pm_scaled, u)
                nc.tensor.matmul(ps[:, 3, :], w_pool_bd[:, u // 2, :], z_pool[:, u // 2, half_cols(u % 2)],
                                 start=True, stop=True).then_inc(pm_done, 1)

            def conv_sums(bank, src):
                for h in range(2):
                    for t in range(2):
                        ins = nc.tensor.matmul(ps[:, bank + h, :], ones_row[:, :], src[:, t, half_cols(h)],
                                               start=t == 0, stop=t == 1)
                return ins

            def gate_half(b, h):
                for k in range(KT):
                    ins = product(ps[:, 2 * (b % 2) + h, :], (w_part(b, k), act_part(k, half_cols(h))),
                                  k == 0, k == KT - 1)
                return ins

            def between(a, part):
                pair, i = divmod(a, STEPS)
                per = PER_STEP if pair < PAIRS - 1 else early_per_step
                if pair < PAIRS:
                    for m in range(per * i + part * (per // 2), per * i + (per if part else per // 2)):
                        project(pair + 1, m)

            for a in range(N_STEPS + 2):
                pair, i = divmod(a, STEPS)
                if a < N_STEPS:
                    scores(a)
                    if i < 2:
                        transpose_v(pair, i)
                if a == N_STEPS:
                    pe.wait_ge(biased, N_STEPS)
                    pe.wait_ge(tap_done, 2 * TAPS)
                    conv_sums(4, mid[:, 6:8, :]).then_inc(cmean_done, 1)
                between(a, 0)
                if a >= 3 and a % 2 == 1:
                    weigh((a - 3) // 2)
                if 1 <= a <= N_STEPS:
                    transpose_probs(a - 1)
                if pool_mix_unit(a) is not None:
                    mix_pool(pool_mix_unit(a))
                between(a, 1)
                if a == N_STEPS:
                    for b in range(2):
                        pe.wait_ge(h_free[b], 3 * PAIRS + EARLY)
                    pe.wait_ge(w_lo_done, N_GATE0 + 3)
                    gate_half(2, 0)
            pe.wait_ge(squared, 2)
            pe.wait_ge(o_copied, N_STEPS)
            conv_sums(2, sq).then_inc(cvar_done, 1)
            gate_half(2, 1).then_inc(g_done, 1)

            def branches(j, first):
                pe.wait_ge(w_lo_done, j * 4 + (N_GATE0 + 4))
                for y, (k0, k1, bank) in enumerate(((0, 2, 4), (2, 6, 6), (6, 8, 2))):
                    if first:
                        pe.wait_ge(br_lo_done, k1)
                        pe.wait_ge(*((centred, 2), (pt_lo_done, N_STEPS), (cvar_read, 1))[y])
                    elif y == 2:
                        pe.wait_ge(sig_done, j * 3 + 2)
                    for h in range(2):
                        cs = half_cols(h)
                        for k in range(k0, k1):
                            ins = product(ps[:, bank + h, :], (w_part(3, k), (br_hi[:, k, cs], br_lo[:, k, cs])),
                                          k == k0, k == k1 - 1)
                    ins.then_inc(y_done, 1)

            branches(0, True)
            with pe.Fori(1, KT) as j:
                for b in range(3):
                    pe.wait_ge(w_lo_done, j * 4 + (N_GATE0 + b + 1))
                    if b == 2:
                        pe.wait_ge(sig_done, j * 3 + 1)
                    gate_half(b, 0)
                    gate_half(b, 1).then_inc(g_done, 1)
                branches(j, False)

            def transpose_x2(t):
                pe.wait_ge(normed, second_norm(t) + 1)
                if t >= 2:
                    pe.wait_ge(x2_tmp_done, t - 1)
                for k in range(KT):
                    ins = nc.tensor.transpose(banks(4 + 2 * (t % 2))[:, k * P:(k + 1) * P],
                                              tmp[t % 2][:, k * P:(k + 1) * P], ident[:, :])
                ins.then_inc(x2t_done, 1)

            pe.wait_ge(sig_done, 3 * KT)
            pe.wait_ge(y_used, 3 * KT)
            for tiles in ((0, 1),) + tuple((t,) for t in range(2, ST)):
                if tiles[0] >= 2:
                    pe.wait_ge(mix_free, tiles[0] - 1)
                for k in range(KT):
                    if tiles[0] == 0:
                        pe.wait_ge(mg_lo_done, k + 1)
                        pe.wait_ge(row_lo_done, k + 1)
                    for t in tiles:
                        for h in range(2):
                            cs = half_cols(h)
                            ins = product(ps[:, 2 * (t % 2) + h, :],
                                          (act_part(k, slice(t * P, (t + 1) * P)), (br_hi[:, k, cs], br_lo[:, k, cs])),
                                          k == 0, k == KT - 1)
                        if k == KT - 1:
                            ins.then_inc(mix_done, 1)
                if tiles[0] >= 2:
                    transpose_x2(tiles[0] - 2)

            def ff1_half(g, t, h):
                for k in range(KT):
                    ins = product(ps[:, 2 * (t % 2) + h, :], (w_part(t, k), act_part(k, half_cols(h))),
                                  k == 0, k == KT - 1)
                if h == 1:
                    ins.then_inc(f1_done, 1)

            def mlp_group(g, first):
                if first:
                    for h in range(2):
                        pe.wait_ge(x2_lo_done, ST // 2 * (h + 1))
                        for t in range(2):
                            if h == 0:
                                pe.wait_ge(w_lo_done, N_FF0 + t + 1)
                                pe.wait_ge(mix_free, ST - 1 + t)
                            ff1_half(g, t, h)
                        if h == 0:
                            transpose_x2(ST - 2)
                            transpose_x2(ST - 1)
                for t in range(2 if first else 0, GROUP):
                    pe.wait_ge(w_lo_done, g * GROUP + (N_FF0 + t + 1))
                    pe.wait_ge(relu_done, g * GROUP + (t - 1))
                    for h in range(2):
                        ff1_half(g, t, h)
                for pair in range(ST // 2):
                    for k in range(GROUP):
                        if pair == 0:
                            pe.wait_ge(h_lo_done, g * GROUP + (k + 1))
                            pe.wait_ge(row_lo_done, g * GROUP + (KT + k + 1))
                        for t in (2 * pair, 2 * pair + 1):
                            ts = slice(t * P, (t + 1) * P)
                            if k == 0 and not (first and pair == 0):
                                pe.wait_ge(acc_done, g * ST + (t - 1))
                            for h in range(2):
                                cs = half_cols(h)
                                ins = product(ps[:, 4 + 2 * (t % 2) + h, :],
                                              ((h_hi[:, k, ts], h_lo[:, k, ts]), (w2_hi[:, k, cs], w2_lo[:, k, cs])),
                                              k == 0, k == GROUP - 1)
                            if k == GROUP - 1:
                                ins.then_inc(f2_done, 1)

            mlp_group(0, True)
            with pe.Fori(1, GROUPS) as g:
                mlp_group(g, False)


_INS = ['x', 'c', 'w_ada', 'b_ada', 'w_in', 'b_gate', 'w_pool', 'pool_scale', 'rel_bias', 'conv_w', 'conv_b',
        'conv_ln_g', 'conv_ln_b', 'w_br_pool', 'w_br_attn', 'w_br_conv', 'w_o', 'ln_mix_g', 'ln_mix_b',
        'w_ff1', 'b_ff1', 'w_ff2', 'b_ff2', 'ln_ff_g', 'ln_ff_b']
_OUTS = [((1, SEQ, D), 'float32')]


def kernel(**inputs):
    import numpy as _np
    import concourse.bacc as _bacc
    from concourse import mybir as _mybir
    from concourse.bass_utils import run_bass_kernel_spmd as _run

    nc = _bacc.Bacc("TRN2", target_bir_lowering=False, num_devices=1, dynamic_dma_scratch_size=1024)
    arrays, args = {}, []
    for name in _INS:
        a = _np.ascontiguousarray(inputs[name])
        arrays[f"in_{name}_dram"] = a
        args.append(nc.dram_tensor(f"in_{name}_dram", a.shape, _mybir.dt.from_np(a.dtype), kind="ExternalInput").ap())
    for i, (shape, dtype) in enumerate(_OUTS):
        dt = _mybir.dt.from_np(_np.dtype(dtype))
        args.append(nc.dram_tensor(f"out_{i}_dram", shape, dt, kind="ExternalOutput").ap())
    trunk_layer(nc, *args)
    r = _run(nc, [arrays], core_ids=[0])
    got = tuple(r.results[0][f"out_{i}_dram"] for i in range(len(_OUTS)))
    return got[0]
```
